# Optimizing a Trainium2 kernel written in Bass

```python
import math
import jax, jax.numpy as jnp
from jax import lax
import numpy as np

D_MODEL = 1024
BATCH = 1
SEQ = 512
DEPTH = 2

CTX_LEN = 256
GRID_W = 64
HEAD_DIM = 64
ROPE_PAIRS = HEAD_DIM // 4
ROPE_BASE = 10000.0
EPS = 1e-6
N_MOD = 6

NA_HEADS = 4
NA_WIN_ROWS = 8
NA_WIN_COLS = 16
NA_QBLK_W = 16
NA_KBAND_W = 32

DIFF_HEADS = 4
DIFF_QK_DIM = HEAD_DIM
DIFF_V_DIM = 2 * HEAD_DIM
DENSE_QBLOCK = 128

SWA_HEADS = 4
SWA_KV_HEADS = 2
SWA_GROUP = SWA_HEADS // SWA_KV_HEADS
SWA_WINDOW = 128
SWA_BLOCK = 128

N_BRANCH = 3
Q_NA = NA_HEADS * HEAD_DIM
Q_DIFF = DIFF_HEADS * 2 * DIFF_QK_DIM
Q_SWA = SWA_HEADS * HEAD_DIM
K_NA = NA_HEADS * HEAD_DIM
K_DIFF = DIFF_HEADS * 2 * DIFF_QK_DIM
K_SWA = SWA_KV_HEADS * HEAD_DIM
V_NA = NA_HEADS * HEAD_DIM
V_DIFF = DIFF_HEADS * DIFF_V_DIM
V_SWA = SWA_KV_HEADS * HEAD_DIM
O_NA = V_NA
O_DIFF = V_DIFF
O_SWA = SWA_HEADS * HEAD_DIM
Q_W = Q_NA + Q_DIFF + Q_SWA
K_W = K_NA + K_DIFF + K_SWA
KV_W = K_W + V_NA + V_DIFF + V_SWA
GATE_W = N_BRANCH * D_MODEL
IN_W = Q_W + KV_W + GATE_W
Q_SPLITS = (Q_NA, Q_NA + Q_DIFF)
KV_SPLITS = (K_NA, K_NA + K_DIFF, K_W, K_W + V_NA, K_W + V_NA + V_DIFF)

N_EXPERTS = 16
EXPERT_FF = D_MODEL
EC_CAPACITY = 2

kernel_name = "hybrid_na_diff_swa_ec_dit"

def rmsnorm(x, g):
    xf = x.astype(jnp.float32)
    y = xf * lax.rsqrt(jnp.mean(xf * xf, axis=-1, keepdims=True) + EPS)
    return (y * g.astype(jnp.float32)).astype(x.dtype)

def modulate(h, shift, scale):
    return h * (1.0 + scale) + shift

def rope_tables(n):
    t = jnp.arange(n)
    row = (t // GRID_W).astype(jnp.float32)[:, None]
    col = (t % GRID_W).astype(jnp.float32)[:, None]
    inv = ROPE_BASE ** (-jnp.arange(ROPE_PAIRS, dtype=jnp.float32) / ROPE_PAIRS)
    ang = jnp.concatenate([row * inv, row * inv, col * inv, col * inv], axis=-1)
    return jnp.cos(ang), jnp.sin(ang)

def rope2d(x, cos, sin):
    shp = (cos.shape[0],) + (1,) * (x.ndim - 3) + (HEAD_DIM,)
    cs, sn = cos.reshape(shp), sin.reshape(shp)
    xr = x.reshape(*x.shape[:-1], 2, 2, ROPE_PAIRS)
    rot = jnp.stack([-xr[..., 1, :], xr[..., 0, :]], axis=-2).reshape(x.shape)
    return (x * cs + rot * sn).astype(x.dtype)

def split_q(qblk):
    lead = qblk.shape[:-1]
    q_na, q_diff, q_swa = jnp.split(qblk, Q_SPLITS, axis=-1)
    return (q_na.reshape(*lead, NA_HEADS, HEAD_DIM),
            q_diff.reshape(*lead, DIFF_HEADS, 2, DIFF_QK_DIM),
            q_swa.reshape(*lead, SWA_HEADS, HEAD_DIM))

def split_kv(kvblk):
    lead = kvblk.shape[:-1]
    k_na, k_diff, k_swa, v_na, v_diff, v_swa = jnp.split(kvblk, KV_SPLITS, axis=-1)
    return (k_na.reshape(*lead, NA_HEADS, HEAD_DIM),
            k_diff.reshape(*lead, DIFF_HEADS, 2, DIFF_QK_DIM),
            k_swa.reshape(*lead, SWA_KV_HEADS, HEAD_DIM),
            v_na.reshape(*lead, NA_HEADS, HEAD_DIM),
            v_diff.reshape(*lead, DIFF_HEADS, DIFF_V_DIM),
            v_swa.reshape(*lead, SWA_KV_HEADS, HEAD_DIM))

def ctx_attend(q, k, v):
    B, L = q.shape[:2]
    s = jnp.einsum('bqhd,bkhd->bhqk', q, k).astype(jnp.float32) * (q.shape[-1] ** -0.5)
    p = jax.nn.softmax(s, axis=-1).astype(v.dtype)
    return jnp.einsum('bhqk,bkhd->bqhd', p, v).reshape(B, L, -1)

def na_latent(q, k, v, kc, vc, rpb):
    B, N, H, Dh = q.shape
    R = N // GRID_W
    kh = min(NA_WIN_ROWS, R)
    nj = GRID_W // NA_QBLK_W
    r = jnp.arange(R)
    row_idx = jnp.clip(r - kh // 2, 0, R - kh)[:, None] + jnp.arange(kh)[None, :]
    j = jnp.arange(nj)
    band0 = jnp.clip(j * NA_QBLK_W - NA_WIN_COLS // 2, 0, GRID_W - NA_KBAND_W)
    col_idx = band0[:, None] + jnp.arange(NA_KBAND_W)[None, :]
    qcol = j[:, None] * NA_QBLK_W + jnp.arange(NA_QBLK_W)[None, :]
    cstart = jnp.clip(qcol - NA_WIN_COLS // 2, 0, GRID_W - NA_WIN_COLS)[..., None]
    kcol = col_idx[:, None, :]
    col_ok = (kcol >= cstart) & (kcol < cstart + NA_WIN_COLS)
    dr = row_idx - r[:, None]
    dc = jnp.clip(kcol - qcol[..., None], -(NA_WIN_COLS - 1), NA_WIN_COLS - 1)
    bias = rpb[:, (dr + NA_WIN_ROWS - 1)[:, None, None, :, None],
               (dc + NA_WIN_COLS - 1)[None, :, :, None, :]]
    qg = q.reshape(B, R, nj, NA_QBLK_W, H, Dh)
    ri, ci = row_idx[:, None, :, None], col_idx[None, :, None, :]
    kw = k.reshape(B, R, GRID_W, H, Dh)[:, ri, ci]
    vw = v.reshape(B, R, GRID_W, H, Dh)[:, ri, ci]
    scale = Dh ** -0.5
    s_loc = jnp.einsum('brjqhd,brjkwhd->bhrjqkw', qg, kw).astype(jnp.float32) * scale + bias[None].astype(jnp.float32)
    s_loc = jnp.where(col_ok[:, :, None, :], s_loc, -jnp.inf)
    nloc = kh * NA_KBAND_W
    s_loc = s_loc.reshape(B, H, R, nj, NA_QBLK_W, nloc)
    s_ctx = jnp.einsum('brjqhd,bchd->bhrjqc', qg, kc).astype(jnp.float32) * scale
    p = jax.nn.softmax(jnp.concatenate([s_loc, s_ctx], axis=-1), axis=-1).astype(v.dtype)
    p_loc = p[..., :nloc].reshape(B, H, R, nj, NA_QBLK_W, kh, NA_KBAND_W)
    o = (jnp.einsum('bhrjqkw,brjkwhd->brjqhd', p_loc, vw)
         + jnp.einsum('bhrjqc,bchd->brjqhd', p[..., nloc:], vc))
    return o.reshape(B, N, H * Dh)

def diff_core(q, k, v, lam):
    s = jnp.einsum('bqhmd,bkhmd->bhmqk', q, k).astype(jnp.float32) * (q.shape[-1] ** -0.5)
    p = jax.nn.softmax(s, axis=-1)
    a = (p[:, :, 0] - lam * p[:, :, 1]).astype(v.dtype)
    return jnp.einsum('bhqk,bkhd->bqhd', a, v)

def diff_latent(q, k, v, kc, vc, lam):
    B, N = q.shape[:2]
    k_all = jnp.concatenate([kc, k], axis=1)
    v_all = jnp.concatenate([vc, v], axis=1)
    nb = N // DENSE_QBLOCK
    qb = jnp.moveaxis(q.reshape(B, nb, DENSE_QBLOCK, DIFF_HEADS, 2, DIFF_QK_DIM), 1, 0)
    o = lax.map(lambda qi: diff_core(qi, k_all, v_all, lam), qb)
    return jnp.moveaxis(o, 0, 1).reshape(B, N, DIFF_HEADS, DIFF_V_DIM)

def diff_finish(o, g, lam_init):
    y = rmsnorm(o, g) * (1.0 - lam_init)
    return y.reshape(*o.shape[:-2], DIFF_HEADS * DIFF_V_DIM)

def swa_latent(q, k, v, kc, vc, sink):
    B, N = q.shape[:2]
    nb = N // SWA_BLOCK
    qb = q.reshape(B, nb, SWA_BLOCK, SWA_KV_HEADS, SWA_GROUP, HEAD_DIM)

    def band(t):
        tb = t.reshape(B, nb, SWA_BLOCK, SWA_KV_HEADS, HEAD_DIM)
        tp = jnp.pad(tb, ((0, 0), (1, 1), (0, 0), (0, 0), (0, 0)))
        return jnp.concatenate([tp[:, :-2], tp[:, 1:-1], tp[:, 2:]], axis=2)

    kw, vw = band(k), band(v)
    blk = jnp.arange(nb)[:, None, None]
    qpos = blk * SWA_BLOCK + jnp.arange(SWA_BLOCK)[None, :, None]
    kpos = (blk - 1) * SWA_BLOCK + jnp.arange(3 * SWA_BLOCK)[None, None, :]
    ok = (kpos >= 0) & (kpos < N) & (jnp.abs(qpos - kpos) <= SWA_WINDOW)
    scale = HEAD_DIM ** -0.5
    s_loc = jnp.einsum('bnqgmd,bnkgd->bgmnqk', qb, kw).astype(jnp.float32) * scale
    s_loc = jnp.where(ok, s_loc, -jnp.inf)
    s_ctx = jnp.einsum('bnqgmd,bcgd->bgmnqc', qb, kc).astype(jnp.float32) * scale
    sk = jnp.broadcast_to(sink.astype(jnp.float32).reshape(1, SWA_KV_HEADS, SWA_GROUP, 1, 1, 1),
                          s_loc.shape[:-1] + (1,))
    p = jax.nn.softmax(jnp.concatenate([s_loc, s_ctx, sk], axis=-1), axis=-1).astype(v.dtype)
    nloc = 3 * SWA_BLOCK
    o = (jnp.einsum('bgmnqk,bnkgd->bnqgmd', p[..., :nloc], vw)
         + jnp.einsum('bgmnqc,bcgd->bnqgmd', p[..., nloc:-1], vc))
    return o.reshape(B, N, SWA_HEADS * HEAD_DIM)

def swa_ctx(q, k, v, sink):
    B, L = q.shape[:2]
    qg = q.reshape(B, L, SWA_KV_HEADS, SWA_GROUP, HEAD_DIM)
    s = jnp.einsum('bqgmd,bkgd->bgmqk', qg, k).astype(jnp.float32) * (HEAD_DIM ** -0.5)
    sk = jnp.broadcast_to(sink.astype(jnp.float32).reshape(1, SWA_KV_HEADS, SWA_GROUP, 1, 1),
                          s.shape[:-1] + (1,))
    p = jax.nn.softmax(jnp.concatenate([s, sk], axis=-1), axis=-1)[..., :-1].astype(v.dtype)
    return jnp.einsum('bgmqk,bkgd->bqgmd', p, v).reshape(B, L, SWA_HEADS * HEAD_DIM)

def merge(o_na, o_diff, o_swa, gates, w_na, w_diff, w_swa, w_o):
    g = jax.nn.sigmoid(gates.astype(jnp.float32)).astype(o_na.dtype)
    g = g.reshape(*gates.shape[:-1], N_BRANCH, D_MODEL)
    y = g[..., 0, :] * (o_na @ w_na) + g[..., 1, :] * (o_diff @ w_diff) + g[..., 2, :] * (o_swa @ w_swa)
    return y @ w_o

def ec_ffn(h, w_router, w_gate, w_up, w_down):
    B, n, _ = h.shape
    cap = max(1, EC_CAPACITY * n // N_EXPERTS)
    aff = jax.nn.softmax(jnp.einsum('bnd,de->bne', h, w_router).astype(jnp.float32), axis=-1)
    top_w, top_i = lax.top_k(jnp.swapaxes(aff, 1, 2), cap)
    bidx = jnp.arange(B)[:, None, None]
    xs = h[bidx, top_i]
    hid = jax.nn.silu(jnp.einsum('becd,edf->becf', xs, w_gate)) * jnp.einsum('becd,edf->becf', xs, w_up)
    ye = jnp.einsum('becf,efd->becd', hid, w_down) * top_w[..., None].astype(h.dtype)
    return jnp.zeros_like(h).at[bidx, top_i].add(ye)

def diff_lambda_init(layer):
    return 0.8 - 0.6 * math.exp(-0.3 * layer)

def setup_inputs(seed: int = 0) -> dict:
    key = jax.random.key(seed)
    ks = jax.random.split(key, 22)
    D = D_MODEL

    def nrm(k, shape, s):
        return jax.random.normal(k, shape, jnp.float32) * s

    return {
        "x": nrm(ks[0], (BATCH, SEQ, D), 1.0),
        "c": nrm(ks[1], (BATCH, D), 1.0),
        "ctx": nrm(ks[2], (BATCH, CTX_LEN, D), 1.0),
        "c_ctx": nrm(ks[3], (D,), 1.0),
        "w_mod": nrm(ks[4], (DEPTH, D, N_MOD * D), 0.5 * D ** -0.5),
        "b_mod": nrm(ks[5], (DEPTH, N_MOD * D), 0.01),
        "norm1_g": 1.0 + nrm(ks[6], (DEPTH, D), 0.01),
        "w_in": nrm(ks[7], (DEPTH, D, IN_W), D ** -0.5),
        "na_rpb": nrm(ks[8], (DEPTH, NA_HEADS, 2 * NA_WIN_ROWS - 1, 2 * NA_WIN_COLS - 1), 0.1),
        "diff_lambda": nrm(ks[9], (DEPTH, 4, DIFF_QK_DIM), 0.1),
        "diff_subln_g": 1.0 + nrm(ks[10], (DEPTH, DIFF_V_DIM), 0.01),
        "swa_sink": nrm(ks[11], (DEPTH, SWA_HEADS), 0.5),
        "w_branch_na": nrm(ks[12], (DEPTH, O_NA, D), O_NA ** -0.5),
        "w_branch_diff": nrm(ks[13], (DEPTH, O_DIFF, D), O_DIFF ** -0.5),
        "w_branch_swa": nrm(ks[14], (DEPTH, O_SWA, D), O_SWA ** -0.5),
        "w_out": nrm(ks[15], (DEPTH, D, D), D ** -0.5),
        "norm2_g": 1.0 + nrm(ks[16], (DEPTH, D), 0.01),
        "w_router": nrm(ks[17], (DEPTH, D, N_EXPERTS), D ** -0.5),
        "w_expert_gate": nrm(ks[18], (DEPTH, N_EXPERTS, D, EXPERT_FF), D ** -0.5),
        "w_expert_up": nrm(ks[19], (DEPTH, N_EXPERTS, D, EXPERT_FF), D ** -0.5),
        "w_expert_down": nrm(ks[20], (DEPTH, N_EXPERTS, EXPERT_FF, D), EXPERT_FF ** -0.5),
        "final_g": 1.0 + nrm(ks[21], (D,), 0.01),
    }

def reference(x, c, ctx, c_ctx, w_mod, b_mod, norm1_g, w_in, na_rpb, diff_lambda, diff_subln_g,
              swa_sink, w_branch_na, w_branch_diff, w_branch_swa, w_out, norm2_g, w_router,
              w_expert_gate, w_expert_up, w_expert_down, final_g):
    N = x.shape[1]
    cos, sin = rope_tables(N)
    xc = ctx
    for l in range(DEPTH):
        last = l == DEPTH - 1
        lam_init = diff_lambda_init(l)
        mod = jax.nn.silu(c) @ w_mod[l] + b_mod[l]
        mod_c = jax.nn.silu(c_ctx) @ w_mod[l] + b_mod[l]
        sh1, sc1, gt1, sh2, sc2, gt2 = jnp.split(mod[:, None, :], N_MOD, axis=-1)
        sh1c, sc1c, gt1c, sh2c, sc2c, gt2c = jnp.split(mod_c, N_MOD, axis=-1)

        lam_p = diff_lambda[l].astype(jnp.float32)
        lam = (jnp.exp(jnp.sum(lam_p[0] * lam_p[1])) - jnp.exp(jnp.sum(lam_p[2] * lam_p[3]))
               + lam_init)

        h = modulate(rmsnorm(x, norm1_g[l]), sh1, sc1)
        hc = modulate(rmsnorm(xc, norm1_g[l]), sh1c, sc1c)
        proj = h @ w_in[l]
        q_na, q_diff, q_swa = split_q(proj[..., :Q_W])
        k_na, k_diff, k_swa, v_na, v_diff, v_swa = split_kv(proj[..., Q_W:Q_W + KV_W])
        gates = proj[..., Q_W + KV_W:]
        q_diff, k_diff = rope2d(q_diff, cos, sin), rope2d(k_diff, cos, sin)
        q_swa, k_swa = rope2d(q_swa, cos, sin), rope2d(k_swa, cos, sin)
        if last:
            kv_c = hc @ w_in[l][:, Q_W:Q_W + KV_W]
        else:
            proj_c = hc @ w_in[l]
            kv_c = proj_c[..., Q_W:Q_W + KV_W]
        kc_na, kc_diff, kc_swa, vc_na, vc_diff, vc_swa = split_kv(kv_c)

        o_na = na_latent(q_na, k_na, v_na, kc_na, vc_na, na_rpb[l])
        o_diff = diff_finish(diff_latent(q_diff, k_diff, v_diff, kc_diff, vc_diff, lam),
                             diff_subln_g[l], lam_init)
        o_swa = swa_latent(q_swa, k_swa, v_swa, kc_swa, vc_swa, swa_sink[l])
        y = merge(o_na, o_diff, o_swa, gates, w_branch_na[l], w_branch_diff[l], w_branch_swa[l], w_out[l])
        x = x + gt1 * y

        if not last:
            qc_na, qc_diff, qc_swa = split_q(proj_c[..., :Q_W])
            gates_c = proj_c[..., Q_W + KV_W:]
            oc_na = ctx_attend(qc_na, kc_na, vc_na)
            oc_diff = diff_finish(diff_core(qc_diff, kc_diff, vc_diff, lam), diff_subln_g[l], lam_init)
            oc_swa = swa_ctx(qc_swa, kc_swa, vc_swa, swa_sink[l])
            yc = merge(oc_na, oc_diff, oc_swa, gates_c, w_branch_na[l], w_branch_diff[l],
                       w_branch_swa[l], w_out[l])
            xc = xc + gt1c * yc

        h2 = modulate(rmsnorm(x, norm2_g[l]), sh2, sc2)
        x = x + gt2 * ec_ffn(h2, w_router[l], w_expert_gate[l], w_expert_up[l], w_expert_down[l])
        if not last:
            h2c = modulate(rmsnorm(xc, norm2_g[l]), sh2c, sc2c)
            xc = xc + gt2c * ec_ffn(h2c, w_router[l], w_expert_gate[l], w_expert_up[l], w_expert_down[l])

    return rmsnorm(x, final_g)


_drawn_inputs = setup_inputs


def setup_inputs(seed=0):
    import zlib

    import numpy as np

    out = dict(_drawn_inputs(seed))
    spreads = {}
    factors = {'b_mod': 4.301,
     'norm1_g': 8.0,
     'na_rpb': 8.0,
     'diff_lambda': 6.9,
     'diff_subln_g': 8.0,
     'swa_sink': 8.0,
     'norm2_g': 7.622,
     'final_g': 5.479}
    for name, (base, spread) in spreads.items():
        noise = np.random.default_rng([zlib.crc32(name.encode()), seed]).standard_normal(out[name].shape)
        drawn = base * np.exp(spread * noise) if base else spread * noise
        out[name] = __import__('jax').numpy.asarray(drawn.astype(out[name].dtype))
    for name, factor in factors.items():
        out[name] = (out[name] * factor).astype(out[name].dtype)
    return out
```

```python
import math
from contextlib import ExitStack

import numpy as np

import concourse.bass as bass
from concourse import mybir

D = 1024
KD = D // 128
NC_, NL = 256, 512
NT = NC_ + NL
DEPTH = 2
GRID_W = 64
NE = 16
CAP_L, CAP_C = 2 * NL // NE, 2 * NC_ // NE
SLOT = 2048
RING = 6
NEG = -1.0e30
SCALE = 64 ** -0.5
EPS = 1e-6
FF_HALF = 512

MOD_SLOTS, QK_SLOTS, V_SLOTS, MERGE_SLOTS, OUT_SLOTS, MOE_SLOTS = 24, 8, 4, 16, 4, 12 * NE
QK0 = MOD_SLOTS
V0 = QK0 + QK_SLOTS
MERGE0 = V0 + V_SLOTS
OUT0 = MERGE0 + MERGE_SLOTS
MOE0 = OUT0 + OUT_SLOTS
LAYER_SLOTS = MOE0 + MOE_SLOTS
TOTAL_SLOTS = DEPTH * LAYER_SLOTS

O_BMOD, O_G1, O_G2, O_SUBG, O_LAM, O_SINK, O_WR = 0, 48, 56, 64, 192, 448, 452
SMALL = O_WR + 128
O_C, O_FG, O_ID, O_IOTA = 0, 16, 24, 152
GLOBAL = O_IOTA + 64

N_Q, N_K = 8, 7
ROPE_BLOCKS = (2, 3, 4, 5, 6, 7, 10, 11, 12, 13, 14)
N_UNITS, N_MAPS = 12, 16


def unit_list():
    units = []
    for h in range(4):
        units.append(("na", h // 2, 8 + h // 2, 64 * h, 64 * h, h, None))
    for h in range(4):
        units.append(("diff", 2 + h, 10 + h, 256 + 128 * h, 256 + 128 * h, None, None))
    for j in range(2):
        for kv in range(2):
            head = 2 * kv + j
            units.append(("swa", 6 + j, 14, 768 + 64 * kv, 768 + 64 * head, 4, head))
    return units


def build(nc, stream, x_in, small_in, global_in, rope_in, mask_in, rpb_in, out):
    f32 = mybir.dt.float32
    ALU = mybir.AluOpType
    ACT = mybir.ActivationFunctionType
    AX = mybir.AxisListType.X
    UNITS = unit_list()
    MAPS = [(u, half) for u in range(N_UNITS) for half in ((0, 1) if UNITS[u][0] == "diff" else (None,))]
    FIRST_MAP = [min(n for n, (v, _) in enumerate(MAPS) if v == u) for u in range(N_UNITS)]
    LAST_MAP = [max(n for n, (v, _) in enumerate(MAPS) if v == u) for u in range(N_UNITS)]
    ctx = ExitStack()
    with ctx:
        def sb(name, shape):
            return ctx.enter_context(nc.sbuf_tensor(name, shape, f32))

        def sem(name):
            return ctx.enter_context(nc.semaphore(name))

        def sems(name):
            return [sem(f"{name}{L}") for L in range(DEPTH)]

        ring = sb("ring", [128, RING, SLOT])
        region_x = sb("region_x", [128, KD * NT])
        region_h = sb("region_h", [128, KD * NT])
        x_fm = region_x[:, :].rearrange("p (k t) -> p k t", k=KD)
        o_fm = x_fm
        h_fm = region_h[:, :].rearrange("p (k t) -> p k t", k=KD)
        h_tok = region_h[:, :].rearrange("p (n d) -> p n d", n=NT // 128)
        small = sb("small", [128, SMALL])
        glob = sb("glob", [128, GLOBAL])
        ones = sb("ones", [128, 128])
        mod = sb("mod", [128, 48, 2])
        amp = sb("amp", [128, 2, KD, 2])
        tiny = sb("tiny", [128, 96])
        junk = sb("junk", [128, 128])
        q_pad = sb("q_pad", [128, 2, 128])
        ARENA = 27030
        arena = sb("arena", [128, ARENA])
        ident = glob[:, O_ID:O_ID + 128]
        iota = glob[:, O_IOTA:O_IOTA + 64]
        eps_col, neg_lam, lam_a, lam_b = (tiny[:, c:c + 1] for c in (64, 65, 66, 67))
        sink8, ssq, rms4, rr4, zero_col = tiny[:, 68:72], tiny[:, 72:76], tiny[:, 76:80], tiny[:, 80:84], tiny[:, 84:85]

        def carve(at, *dims):
            n = int(np.prod(dims))
            assert at + n <= ARENA, (at, n)
            flat = arena[:, at:at + n]
            if len(dims) == 2:
                flat = flat.rearrange("p (a b) -> p a b", a=dims[0])
            return flat, at + n

        qk, a_v = carve(0, N_Q + N_K, NT)
        v_tok, a_b = carve(a_v, NT // 128, 896)
        bias, a_p = carve(a_b, 5, 896)
        probs, a_t = carve(a_p, 4, NT)
        probs_t, a_o = carve(a_t, 2, NT)
        o_tok, _ = carve(a_o, D)
        rope, a1 = carve(a_p, 2, NL)
        rot, a1 = carve(a1, NL)
        col_mask, _ = carve(a1, GRID_W)
        sq, a1 = carve(0, 2, NT)
        rstd, a1 = carve(a1, NT)
        xr, a1 = carve(a1, 2, NT)
        c_pad, a1 = carve(a1, KD, 32)
        mod_row, a1 = carve(a1, 512)
        rpb_pad = arena[0:60, a1:a1 + 128]
        lam_t, _ = carve(a1 + 128, 64)
        y_fm, a1 = carve(0, KD, NT)
        gate, a1 = carve(a1, 3, NT)
        term, _ = carve(a1, 3, NT)
        h2_fm, a_e = carve(KD * NT, KD, NT)
        logit_e, a1 = carve(a_e, NT)
        aff_e, a1 = carve(a1, NT)
        work_e, a1 = carve(a1, NT)
        pos_e, a1 = carve(a1, NT)
        mask_e, a1 = carve(a1, NT)
        zero_e, a1 = carve(a1, NT)
        best, a1 = carve(a1, 8)
        ex_t, a1 = carve(a1, 6, NE)
        red_t, a1 = carve(a1, 2, 6)
        aff_t, a1 = carve(a1, 6, NE)
        pos_t, a_s = carve(a1, 6, NE)
        sel, a1 = carve(a_s, 4, 128)
        selw, a1 = carve(a1, 4, 128)
        selc, a1 = carve(a1, 2, 128)
        selcw, a1 = carve(a1, 2, 128)
        selw_t, a1 = carve(a1, NL)
        selcw_t, a1 = carve(a1, NC_)
        xs, a1 = carve(a1, KD, 128)
        xsc, a1 = carve(a1, KD, 128)
        silu, a1 = carve(0, 2, NT)
        hid, a1 = carve(a1, 2, NT)
        hid_t, a1 = carve(a1, 2, NT)
        y_pair, a1 = carve(a1, D)
        y_ctx, a1 = carve(a1, D)

        PS = [ctx.enter_context(nc.psum_tensor(f"PS{i}", [128, 1024], f32)) for i in range(4)]
        rpb_scr = [nc.dram_tensor(f"rpb_scr{L}", (60, 64, 128), f32, kind="Internal").ap() for L in range(DEPTH)]
        x_scr = nc.dram_tensor("x_scr", (128, KD, NT), f32, kind="Internal").ap()

        slot_loaded, slot_done = [sem(f"slot_loaded{s}") for s in range(RING)], sem("slot_done")
        consts_in, x_in_s, x_saved, out_done = sem("consts_in"), sem("x_in_s"), sem("x_saved"), sem("out_done")
        pad_zeroed = sem("pad_zeroed")
        small_in_s, rpb_in_s, rpb_out, bias_in, rope_in_s, x_back = (
            sems("small_in"), sems("rpb_in"), sems("rpb_out"), sems("bias_in"), sems("rope_in"), sems("x_back"))
        c_zeroed, c_ready, mod_ev, mod_tr, mod_done = (
            sems("c_zeroed"), sems("c_ready"), sems("mod_ev"), sems("mod_tr"), sems("mod_done"))
        NORMS = 2 * DEPTH + 1
        sq_done, sum_done, rms_done, xr_done, h_done = (
            sem("sq_done"), sem("sum_done"), sem("rms_done"), sem("xr_done"), sem("h_done"))
        consts_set = sem("consts_set")
        lam_in, lam_exp = sems("lam_in"), sems("lam_exp")
        qk_ev, rope_done, v_mm, v_ev, bias_done = (
            sems("qk_ev"), sems("rope_done"), sems("v_mm"), sems("v_ev"), sems("bias_done"))
        BLOCKS_BEFORE, n = {}, 0
        for L in range(DEPTH):
            for name, tokens in (("c", 0 if L == DEPTH - 1 else NC_), ("l", NL)):
                BLOCKS_BEFORE[L, name] = n
                n += tokens // 128
        q_staged, s_mm, max_done, exp_done, mix_done, pt_mm, pt_ev = (
            sem("q_staged"), sem("s_mm"), sem("max_done"), sem("exp_done"),
            sem("mix_done"), sem("pt_mm"), sem("pt_ev"))
        o_mm, o_ev, sub_rms, o_norm, ot_mm, ot_ev = (
            sem("o_mm"), sem("o_ev"), sem("sub_rms"), sem("o_norm"),
            sem("ot_mm"), sem("ot_ev"))
        gate_mm, gate_ev, br_mm, br_ev, y_done, out_ev = (
            sems("gate_mm"), sems("gate_ev"), sems("br_mm"), sems("br_ev"), sems("y_done"), sems("out_ev"))
        lg_mm, lg_ev, lt_mm, ex_in, ex_out, aff_done, at_mm, pos_done, pos_tr, router_done = (
            sems("lg_mm"), sems("lg_ev"), sems("lt_mm"), sems("ex_in"), sems("ex_out"), sems("aff_done"),
            sems("at_mm"), sems("pos_done"), sems("pos_tr"), sems("router_done"))
        ht_mm, ht_ev = sems("ht_mm"), sems("ht_ev")
        sel_done, selc_done, gat_mm, gat_ev, gatc_mm, gatc_ev, st_mm, st_ev = (
            sem("sel_done"), sem("selc_done"), sem("gat_mm"), sem("gat_ev"), sem("gatc_mm"),
            sem("gatc_ev"), sem("st_mm"), sem("st_ev"))
        g_ev, hid_done, hidt_mm, hidt_ev, d_ev, dc_ev, cb_mm, cb_ev, cbc_mm, cbc_ev = (
            sem("g_ev"), sem("hid_done"), sem("hidt_mm"), sem("hidt_ev"), sem("d_ev"), sem("dc_ev"),
            sem("cb_mm"), sem("cb_ev"), sem("cbc_mm"), sem("cbc_ev"))
        dve_chain, act_chain = sem("dve_chain"), sem("act_chain")

        class Chain:

            def __init__(self, engine, s):
                self.engine, self.s, self.count, self.extra = engine, s, 0, 0

            def done(self, ins):
                self.count += 1
                ins.then_inc(self.s, 1)
                self.engine.wait_ge(self.s, self.count + self.extra)

            def enter(self, i, step):
                self.start, self.step, self.extra = self.count, step, i * step

            def leave(self, trips):
                assert self.count - self.start == self.step, (self.count - self.start, self.step)
                self.count, self.extra = self.start + self.step * trips, 0

        def finished(L, slots):
            return RING + L * LAYER_SLOTS + slots

        def pieces(last):
            return [(NC_, NT, 0)] if last else [(0, 512, 0), (512, NT, 512)]

        def segments(last):
            return [(0, NC_, NT, 0)] if last else [(1, 0, NC_, 0), (0, NC_, NT, NC_)]

        def x_final(engine, L):
            engine.wait_ge(cb_ev, 4 + (L + 1) * KD * NE // 2)
            if L < DEPTH - 1:
                engine.wait_ge(cbc_ev, 2 + (L + 1) * 4 * NE // 4)

        block = ctx.enter_context(nc.Block())

        @block.sync
        def _(sp):
            rows = stream.rearrange("s p n -> p s n")

            def load(t, s, rotation):
                sp.wait_ge(slot_done, rotation * RING + s + 1)
                sp.dma_start(ring[:, s:s + 1, :], rows[:, bass.ds(t, 1), :]).then_inc(slot_loaded[s], 16)

            with sp.Fori(0, TOTAL_SLOTS // RING) as i:
                for s in range(RING):
                    load(i * RING + s, s, i)
            for s in range(TOTAL_SLOTS % RING):
                load(TOTAL_SLOTS - TOTAL_SLOTS % RING + s, s, TOTAL_SLOTS // RING)
            sp.wait_ge(h_done, NORMS * KD)
            sp.dma_start(out, h_fm[:, :, NC_:NT]).then_inc(out_done, 16)
            sp.wait_ge(out_done, 16)

        @block.gpsimd
        def _(pool):
            pool.dma_start(x_fm, x_in).then_inc(x_in_s, 16)
            pool.dma_start(glob[:, :], global_in).then_inc(consts_in, 16)
            for L in range(DEPTH):
                last = L == DEPTH - 1
                if L:
                    x_final(pool, L - 1)
                    pool.dma_start(x_scr, x_fm).then_inc(x_saved, 16)
                pool.dma_start(small[:, :], small_in[L]).then_inc(small_in_s[L], 16)
                pool.memset(rpb_pad, 0.0).then_inc(pad_zeroed, 1)
                pool.wait_ge(pad_zeroed, L + 1)
                pool.dma_start(rpb_pad[:, 48:79], rpb_in[L]).then_inc(rpb_in_s[L], 16)
                pool.wait_ge(rpb_in_s[L], 16)
                pool.dma_start(rpb_scr[L], rpb_pad.unsqueeze(1).broadcast_to((60, 64, 128))).then_inc(rpb_out[L], 16)
                pool.dma_start(bias[:, 4, :], mask_in[:, 0:896]).then_inc(bias_in[L], 16)
                pool.dma_start(col_mask, mask_in[:, 896:896 + GRID_W]).then_inc(bias_in[L], 16)
                pool.dma_start(rope, rope_in).then_inc(rope_in_s[L], 16)
                pool.wait_ge(rpb_out[L], 16)
                for h in range(4):
                    for half in range(2):
                        first = (15 * h + 1 - half) * 64 * 128 + GRID_W - 1
                        shifted = bass.AP(rpb_scr[L].tensor, first, [[127, 64], [64 * 128, 14], [1, 64]])
                        dst = bias[64 * half:64 * half + 64, h, :].rearrange("p (r c) -> p r c", c=64)
                        pool.dma_start(dst, shifted).then_inc(bias_in[L], 16)

                def stage_queries(key, first, trips):
                    with pool.Fori(0, trips) as turn:
                        b = turn + BLOCKS_BEFORE[key]
                        for n, (u, _) in enumerate(MAPS):
                            half = 64 * (n % 2)
                            pool.wait_ge(s_mm, b * N_MAPS + n + 1)
                            pool.tensor_copy(q_pad[half:half + 64, n % 2, :],
                                             qk[half:half + 64, UNITS[u][1], bass.ds(turn * 128 + first, 128)]
                                             ).then_inc(q_staged, 1)

                pool.wait_ge(qk_ev[L], N_Q + N_K)
                pool.wait_ge(rope_done[L], len(ROPE_BLOCKS))
                if not last:
                    stage_queries((L, "c"), 0, NC_ // 128)
                stage_queries((L, "l"), NC_, NL // 128)
                pool.wait_ge(y_done[L], KD + 1)
                if L:
                    pool.wait_ge(x_saved, 16)
                pool.dma_start(x_fm, x_scr if L else x_in).then_inc(x_back[L], 16)

        @block.tensor
        def _(pe):
            def take(L, t, rotations=0):
                n = L * LAYER_SLOTS + t
                pe.wait_ge(slot_loaded[n % RING], (rotations + n // RING + 1) * 16)
                return ring[:, n % RING, :]

            def norm_sums(n, last):
                for k in range(KD):
                    pe.wait_ge(sq_done, n * KD + k + 1)
                    for lo, hi, c in pieces(last):
                        m = pe.matmul(PS[2][:, c:c + hi - lo], ones[:, :], sq[:, k % 2, lo:hi],
                                      start=(k == 0), stop=(k == KD - 1))
                    m.then_inc(sum_done, 1)

            def product(tile, weights, moving, last, kn=KD, start=True):
                for k in range(kn):
                    for lo, hi, c in pieces(last):
                        m = pe.matmul(PS[tile][:, c:c + hi - lo], weights[:, 128 * k:128 * k + 128],
                                      moving[:, k, lo:hi], start=(k == 0), stop=(k == kn - 1))
                return m

            def heads(key, trips, n_keys):
                with pe.Fori(0, trips) as turn:
                    b = turn + BLOCKS_BEFORE[key]
                    def scores(n):
                        pe.wait_ge(q_staged, b * N_MAPS + n + 1)
                        pe.wait_ge(exp_done, b * N_MAPS + n + 1)
                        for lo in range(0, n_keys, 512):
                            hi = min(lo + 512, n_keys)
                            m = pe.matmul(PS[n % 2][:, lo:hi], q_pad[:, n % 2, :], qk[:, UNITS[MAPS[n][0]][2], lo:hi],
                                          start=True, stop=True)
                        m.then_inc(s_mm, 1)

                    def transposes(u):
                        if UNITS[u][0] == "diff":
                            pe.wait_ge(mix_done, b * 4 + u - 4 + 1)
                        else:
                            pe.wait_ge(exp_done, b * N_MAPS + FIRST_MAP[u] + 3)
                        pe.wait_ge(pt_ev, b * N_UNITS + u + 1)
                        if u == 0:
                            pe.wait_ge(ot_ev, b + 1)
                        for kb in range(n_keys // 128):
                            m = pe.transpose(PS[2][:, 128 * kb:128 * kb + 128],
                                             probs[:, FIRST_MAP[u] % 4, 128 * kb:128 * kb + 128], ident)
                        m.then_inc(pt_mm, 1)

                    def values(u):
                        kind, qb, kb_, vc, oc, br, sk = UNITS[u]
                        w = 128 if kind == "diff" else 64
                        pe.wait_ge(pt_ev, b * N_UNITS + u + 2)
                        pe.wait_ge(o_ev, b * N_UNITS + u + 1)
                        for kb in range(n_keys // 128):
                            m = pe.matmul(PS[3][:, 512 * (u % 2):512 * (u % 2) + w],
                                          probs_t[:, u % 2, 128 * kb:128 * kb + 128], v_tok[:, kb, vc:vc + w],
                                          start=(kb == 0), stop=(kb == n_keys // 128 - 1))
                        m.then_inc(o_mm, 1)

                    scores(0)
                    for n in range(N_MAPS + 3):
                        if n + 1 < N_MAPS:
                            scores(n + 1)
                        if n - 2 in LAST_MAP:
                            transposes(LAST_MAP.index(n - 2))
                        if n - 3 in LAST_MAP:
                            values(LAST_MAP.index(n - 3))
                    pe.wait_ge(o_norm, b + 1)
                    for k in range(KD):
                        m = pe.transpose(PS[2][:, 128 * k:128 * k + 128], o_tok[:, 128 * k:128 * k + 128], ident)
                    m.then_inc(ot_mm, 1)
                pe.wait_ge(ot_ev, BLOCKS_BEFORE[key] + trips + 1)

            def merge_block(L, j, t, rotations):
                last = L == DEPTH - 1
                wa = take(L, t, rotations)
                pe.wait_ge(br_ev[L], 3 * j + 1)
                product(0, wa[:, 0:1024], h_fm, last).then_inc(gate_mm[L], 1)
                pe.wait_ge(br_ev[L], 3 * j + 2)
                product(1, wa[:, 1024:2048], h_fm, last).then_inc(slot_done, 1)
                wb = take(L, t + 1, rotations)
                pe.wait_ge(br_ev[L], 3 * j + 3)
                product(2, wb[:, 0:1024], h_fm, last).then_inc(gate_mm[L], 1)
                for br, (k0, kn) in enumerate(((0, 2), (2, 4), (6, 2))):
                    pe.wait_ge(gate_ev[L], 3 * j + br + 1)
                    m = product(br, wb[:, 1024 + 128 * k0:2048], o_fm[:, k0:KD, :], last, kn)
                    m.then_inc(slot_done if br == 2 else br_mm[L], 1)

            def expert_up(L, turn, t, tile, lhs, lhs_c, ctx_too):
                passes = (0, 1) if ctx_too else (0,)
                for p in passes:
                    for s in range(4):
                        w = take(L, t + s, 8 * turn) if p == 0 else ring[:, (L * LAYER_SLOTS + t + s) % RING, :]
                        for kk in range(2):
                            k = 2 * s + kk
                            row = w[:, 1024 * kk:1024 * kk + 1024]
                            n_t, width, src, at = ((2, 512, lhs, 0), (4, 256, lhs_c, 512))[p]
                            for g in range(n_t):
                                m = pe.matmul(PS[tile][128 // n_t * g:128 // n_t * (g + 1), at:at + width],
                                              src(k), row[:, width * g:width * (g + 1)],
                                              start=(k == 0), stop=(k == KD - 1))
                        if p == passes[-1]:
                            m.then_inc(slot_done, 1)

            pe.sem_inc(slot_done, RING)
            pe.sem_inc(s_mm, 2)
            pe.sem_inc(pt_mm, N_UNITS)
            pe.sem_inc(o_mm, 2)
            pe.sem_inc(ot_mm, 1)
            pe.sem_inc(st_mm, 1)
            pe.wait_ge(consts_in, 16)
            pe.wait_ge(consts_set, 1)
            for L in range(DEPTH):
                last = L == DEPTH - 1
                ctx_too = not last
                norm_sums(2 * L, False)
                pe.wait_ge(c_ready[L], 1)
                for r in range(3):
                    if r:
                        pe.wait_ge(mod_ev[L], r)
                    for k in range(KD):
                        w = take(L, KD * r + k)
                        for g in range(4):
                            m = pe.matmul(PS[0][32 * g:32 * g + 32, 0:512], c_pad[:, k, :], w[:, 512 * g:512 * g + 512],
                                          start=(k == 0), stop=(k == KD - 1))
                        m.then_inc(slot_done, 1)
                    pe.wait_ge(mod_ev[L], r + 1)
                    if r:
                        pe.wait_ge(mod_done[L], r)
                    for c in range(4):
                        m = pe.transpose(PS[1][:, 128 * c:128 * c + 128], mod_row[:, 128 * c:128 * c + 128], ident)
                    m.then_inc(mod_tr[L], 1)
                pe.wait_ge(h_done, (2 * L + 1) * KD)
                pe.wait_ge(mod_done[L], 3)
                for s in range(QK_SLOTS):
                    if s >= 2:
                        pe.wait_ge(qk_ev[L], 2 * s - 2)
                    w = take(L, QK0 + s)
                    for j in (2 * s, 2 * s + 1):
                        if j < N_Q + N_K:
                            m = product(j % 4, w[:, 1024 * (j % 2):1024 * (j % 2) + 1024], h_fm, last and j < N_Q)
                    m.then_inc(slot_done, 1)
                wv = [take(L, V0 + s) for s in range(V_SLOTS)]
                pe.wait_ge(qk_ev[L], N_Q + N_K)
                for nb in range(NT // 128):
                    if nb >= 4:
                        pe.wait_ge(v_ev[L], nb - 3)
                    for k in range(KD):
                        for c in range(2):
                            m = pe.matmul(PS[nb % 4][:, 512 * c:512 * c + 448], h_fm[:, k, 128 * nb:128 * nb + 128],
                                          wv[k // 2][:, 896 * (k % 2) + 448 * c:896 * (k % 2) + 448 * c + 448],
                                          start=(k == 0), stop=(k == KD - 1))
                    if nb < NT // 128 - 1:
                        m.then_inc(v_mm[L], 1)
                    else:
                        m.then_inc(slot_done, V_SLOTS)
                pe.wait_ge(v_ev[L], NT // 128)
                pe.wait_ge(rope_done[L], len(ROPE_BLOCKS))
                if ctx_too:
                    heads((L, "c"), NC_ // 128, NC_)
                heads((L, "l"), NL // 128, NT)
                with pe.Fori(0, 2) as i:
                    for j in range(3):
                        merge_block(L, 3 * i + j, MERGE0 + 2 * j, i)
                for j in (6, 7):
                    merge_block(L, j, MERGE0 + 2 * j, 0)
                pe.wait_ge(y_done[L], KD + 1)
                for s in range(OUT_SLOTS):
                    if s >= 2:
                        pe.wait_ge(out_ev[L], 2 * s - 2)
                    w = take(L, OUT0 + s)
                    for j in (2 * s, 2 * s + 1):
                        m = product(j % 4, w[:, 1024 * (j % 2):1024 * (j % 2) + 1024], y_fm, last)
                    m.then_inc(slot_done, 1)
                pe.wait_ge(out_ev[L], KD)
                norm_sums(2 * L + 1, last)
                nb0 = 2 if last else 0
                pe.wait_ge(h_done, (2 * L + 2) * KD)
                for k in range(KD):
                    for lo, hi, c in pieces(last):
                        m = pe.matmul(PS[0][0:NE, c:c + hi - lo], small[:, O_WR + NE * k:O_WR + NE * k + NE],
                                      h2_fm[:, k, lo:hi], start=(k == 0), stop=(k == KD - 1))
                m.then_inc(lg_mm[L], 1)
                pe.wait_ge(lg_ev[L], 1)
                for nb in range(nb0, 6):
                    m = pe.transpose(PS[1][:, NE * nb:NE * nb + NE], logit_e[0:NE, 128 * nb:128 * nb + 128],
                                     ident[0:NE, 0:NE])
                m.then_inc(lt_mm[L], 1)
                pe.wait_ge(aff_done[L], 1)
                for nb in range(nb0, 6):
                    m = pe.transpose(PS[2][0:NE, 128 * nb:128 * nb + 128], aff_t[:, nb, :], ident)
                m.then_inc(at_mm[L], 1)
                for n, nb in enumerate(range(nb0, 6)):
                    if n >= 2:
                        pe.wait_ge(ht_ev[L], n - 1)
                    for k in range(KD):
                        m = pe.transpose(PS[n % 2][:, 128 * k:128 * k + 128], h2_fm[:, k, 128 * nb:128 * nb + 128], ident)
                    m.then_inc(ht_mm[L], 1)
                pe.wait_ge(pos_done[L], 1)
                for nb in range(nb0, 6):
                    m = pe.transpose(PS[3][:, NE * nb:NE * nb + NE], pos_e[0:NE, 128 * nb:128 * nb + 128],
                                     ident[0:NE, 0:NE])
                m.then_inc(pos_tr[L], 1)
                pe.wait_ge(router_done[L], 1)
                pe.wait_ge(ht_ev[L], 6 - nb0)
                with pe.Fori(0, NE // 4) as turn:
                    i = turn + L * (NE // 4)
                    for pair in range(2):
                        pr = i * 2 + pair
                        pe.wait_ge(cb_ev, pr * KD + 4)
                        pe.wait_ge(sel_done, pr + 1)
                        for k in range(KD):
                            for nb in range(4):
                                m = pe.matmul(PS[2][:, 128 * k:128 * k + 128], h_tok[:, 2 + nb, 128 * k:128 * k + 128],
                                              sel[:, nb, :], start=(nb == 0), stop=(nb == 3))
                        m.then_inc(gat_mm, 1)
                        if ctx_too and pair == 0:
                            pe.wait_ge(cbc_ev, i * 4 + 2)
                            pe.wait_ge(selc_done, i + 1)
                            for k in range(KD):
                                for nb in range(2):
                                    m = pe.matmul(PS[3][:, 128 * k:128 * k + 128], h_tok[:, nb, 128 * k:128 * k + 128],
                                                  selc[:, nb, :], start=(nb == 0), stop=(nb == 1))
                            m.then_inc(gatc_mm, 1)
                            for nb in range(2):
                                pe.transpose(PS[1][:, 512 + 128 * nb:512 + 128 * nb + 128], selcw[:, nb, :], ident)
                        for nb in range(4):
                            m = pe.transpose(PS[1][:, 128 * nb:128 * nb + 128], selw[:, nb, :], ident)
                        m.then_inc(st_mm, 1)
                        pe.wait_ge(gat_ev, pr + 1)
                        if ctx_too and pair == 0:
                            pe.wait_ge(gatc_ev, i + 1)
                        t = MOE0 + 24 * pair
                        for par in range(2):
                            q = 2 * pair + par
                            e = i * 4 + q

                            def lhs(k):
                                return xs[:, k, 64 * par:64 * par + 64]

                            def lhs_c(k):
                                return xsc[:, k, 32 * q:32 * q + 32]

                            if par:
                                pe.wait_ge(g_ev, e)
                            expert_up(L, turn, t + 8 * par, 0, lhs, lhs_c, ctx_too)
                            if par:
                                pe.wait_ge(hid_done, e)
                            else:
                                pe.wait_ge(st_ev, pr + 1)
                            expert_up(L, turn, t + 8 * par + 4, 1, lhs, lhs_c, ctx_too)
                        for par in range(2):
                            q = 2 * pair + par
                            e = i * 4 + q
                            pe.wait_ge(hid_done, e + 1)
                            if par:
                                pe.wait_ge(hidt_ev, e)
                            for c in range(6 if ctx_too else 4):
                                m = pe.transpose(PS[3][:, 128 * c:128 * c + 128], hid[:, q % 2, 128 * c:128 * c + 128], ident)
                            m.then_inc(hidt_mm, 1)
                            pe.wait_ge(hidt_ev, e + 1)
                            if par:
                                pe.wait_ge(g_ev, e + 1)

                            def lhs(k):
                                at = 128 * (k % 4) + 64 * (k // 4)
                                return hid_t[:, q % 2, at:at + 64]

                            def lhs_c(k):
                                at = 512 + 128 * (k % 2) + 32 * (k // 2)
                                return hid_t[:, q % 2, at:at + 32]

                            expert_up(L, turn, t + 16 + 4 * par, 0 if par else 2, lhs, lhs_c, ctx_too)
                        pe.wait_ge(d_ev, pr * 2 + 2)
                        if ctx_too:
                            pe.wait_ge(dc_ev, pr * 2 + 2)
                        for k in range(KD):
                            pe.wait_ge(cb_ev, pr * KD + k + 1)
                            bank = PS[1 + (k % 4) // 2][:, 512 * (k % 2):512 * (k % 2) + 512]
                            pe.matmul(bank, y_pair[:, 128 * k:128 * k + 128], selw_t, start=True, stop=True
                                      ).then_inc(cb_mm, 1)
                        if ctx_too and pair == 1:
                            for c in range(4):
                                pe.wait_ge(cbc_ev, i * 4 + c + 1)
                                for k in (2 * c, 2 * c + 1):
                                    at = 512 * (c % 2) + 256 * (k % 2)
                                    m = pe.matmul(PS[3][:, at:at + 256], y_ctx[:, 128 * k:128 * k + 128], selcw_t,
                                                  start=True, stop=True)
                                m.then_inc(cbc_mm, 1)
                x_final(pe, L)
            norm_sums(NORMS - 1, True)

        @block.scalar
        def _(act):
            chain = Chain(act, act_chain)

            def norm(n, last, x_ready, gains, shifts, dst):
                x_ready()
                lo = NC_ if last else 0
                for k in range(KD):
                    if k >= 2:
                        act.wait_ge(sum_done, n * KD + k - 1)
                    act.activation(sq[:, k % 2, lo:NT], x_fm[:, k, lo:NT], ACT.Square).then_inc(sq_done, 1)
                act.wait_ge(sum_done, n * KD + KD)
                act.activation(rstd[:, lo:NT], PS[2][:, 0:NT - lo], ACT.Sqrt, bias=eps_col, scale=1.0 / D
                               ).then_inc(rms_done, 1)
                if n % 2 == 0 and n < NORMS - 1:
                    modulation(n // 2)
                if n < NORMS - 1:
                    act.wait_ge(mod_done[n // 2], 4)
                for k in range(KD):
                    act.wait_ge(xr_done, n * KD + k + 1)
                    for m_i, (v, a, b, c) in enumerate(segments(last)):
                        ins = act.activation(dst[:, k, a:b], xr[:, k % 2, a:b], ACT.Identity,
                                             bias=shifts(k, v), scale=gains(k, v))
                    ins.then_inc(h_done, 1)

            def modulation(L):
                for r in range(3):
                    act.wait_ge(slot_done, finished(L, KD * (r + 1)))
                    if r:
                        act.wait_ge(mod_tr[L], r)
                    act.activation(mod_row, PS[0][:, 0:512], ACT.Copy).then_inc(mod_ev[L], 1)

            def heads(key, first, trips, n_keys):
                L = key[0]
                latent = key[1] == "l"
                with act.Fori(0, trips) as turn:
                    b = turn + BLOCKS_BEFORE[key]
                    chain.enter(turn, 4)

                    def exps(n):
                        kind, qb, kb, vc, oc, br, sk = UNITS[MAPS[n][0]]
                        t8 = 8 * (n % 8)
                        nm = tiny[:, t8 + 3:t8 + 4]
                        act.wait_ge(max_done, b * N_MAPS + n + 1)
                        if kind == "diff" or not latent:
                            before = MAPS[(n - 4) % N_MAPS][0] + 1 + (N_UNITS if n >= 4 else 0)
                            act.wait_ge(pt_mm, b * N_UNITS + before)
                            if sk is not None:
                                act.activation(tiny[:, t8 + 6:t8 + 7], sink8[:, sk:sk + 1], ACT.Exp, bias=nm, scale=SCALE)
                            act.activation(probs[:, n % 4, 0:n_keys], PS[n % 2][:, 0:n_keys], ACT.Exp, bias=nm,
                                           scale=SCALE, accum_out=tiny[:, t8 + 4:t8 + 5]).then_inc(exp_done, 1)
                        else:
                            if sk is not None:
                                act.activation(tiny[:, t8 + 6:t8 + 7], sink8[:, sk:sk + 1], ACT.Exp, bias=nm, scale=SCALE)
                            act.activation(probs[:, n % 4, NC_:NT], probs[:, n % 4, NC_:NT], ACT.Exp, bias=nm,
                                           scale=SCALE, accum_out=tiny[:, t8 + 4:t8 + 5])
                            act.activation(probs[:, n % 4, 0:NC_], PS[n % 2][:, 0:NC_], ACT.Exp, bias=nm,
                                           scale=SCALE, accum_out=tiny[:, t8 + 5:t8 + 6]).then_inc(exp_done, 1)

                    def evacuate(u):
                        act.wait_ge(pt_mm, b * N_UNITS + u + 1 + N_UNITS)
                        act.wait_ge(o_mm, b * N_UNITS + u + 1)
                        act.activation(probs_t[:, u % 2, 0:n_keys], PS[2][:, 0:n_keys], ACT.Copy).then_inc(pt_ev, 1)

                    for n in range(N_MAPS + 2):
                        if n < N_MAPS:
                            exps(n)
                        if n - 2 in LAST_MAP:
                            evacuate(LAST_MAP.index(n - 2))
                    act.wait_ge(o_ev, b * N_UNITS + 8 + 2)
                    for h in range(4):
                        chain.done(act.activation(junk[:, :], o_tok[:, 256 + 128 * h:384 + 128 * h], ACT.Square,
                                                  accum_out=ssq[:, h:h + 1]))
                    act.activation(rms4, ssq, ACT.Sqrt, bias=eps_col, scale=1.0 / 128).then_inc(sub_rms, 1)
                    act.wait_ge(ot_mm, b + 2)
                    act.activation(o_fm[:, :, bass.ds(turn * 128 + first, 128)],
                                   PS[2][:, :].rearrange("p (k t) -> p k t", k=KD), ACT.Copy).then_inc(ot_ev, 1)
                chain.leave(trips)

            def merge_block(L, j, done):
                lo = NC_ if L == DEPTH - 1 else 0
                for br in range(3):
                    if br == 1:
                        act.wait_ge(slot_done, done)
                    else:
                        act.wait_ge(gate_mm[L], 2 * j + 1 + br // 2)
                    act.activation(gate[:, br, lo:NT], PS[br][:, 0:NT - lo], ACT.Sigmoid).then_inc(gate_ev[L], 1)

            act.sem_inc(exp_done, 2)
            act.sem_inc(pt_ev, 1)
            act.sem_inc(ot_ev, 1)
            act.wait_ge(consts_in, 16)
            act.wait_ge(consts_set, 1)
            for L in range(DEPTH):
                last = L == DEPTH - 1
                ctx_too = not last
                nb0 = 2 if last else 0
                act.wait_ge(c_zeroed[L], 1)
                act.activation(c_pad[:, :, 0:2], glob[:, O_C:O_C + 16].rearrange("p (k v) -> p k v", v=2),
                               ACT.Silu).then_inc(c_ready[L], 1)

                def x_ready_1():
                    if L:
                        x_final(act, L - 1)
                    else:
                        act.wait_ge(x_in_s, 16)

                norm(2 * L, False, x_ready_1, lambda k, v: amp[:, 0, k, v:v + 1], lambda k, v: mod[:, k, v:v + 1], h_fm)
                act.wait_ge(lam_in[L], 1)
                act.activation(tiny[:, 66:68], tiny[:, 66:68], ACT.Exp).then_inc(lam_exp[L], 1)
                act.wait_ge(rpb_out[L], 16)
                for j in range(N_Q + N_K):
                    act.wait_ge(slot_done, finished(L, QK0 + j // 2 + 1))
                    lo = NC_ if last and j < N_Q else 0
                    act.activation(qk[:, j, lo:NT], PS[j % 4][:, 0:NT - lo], ACT.Copy).then_inc(qk_ev[L], 1)
                if L:
                    act.wait_ge(x_saved, 16)
                if ctx_too:
                    heads((L, "c"), 0, NC_ // 128, NC_)
                heads((L, "l"), NC_, NL // 128, NT)
                with act.Fori(0, 2) as i:
                    for j in range(3):
                        merge_block(L, 3 * i + j, finished(L, MERGE0 + 2 * j + 1) + i * 6)
                for j in (6, 7):
                    merge_block(L, j, finished(L, MERGE0 + 2 * j + 1))

                def x_ready_2():
                    act.wait_ge(out_ev[L], KD)

                norm(2 * L + 1, last, x_ready_2, lambda k, v: amp[:, 1, k, v:v + 1],
                     lambda k, v: mod[:, 24 + k, v:v + 1], h2_fm)
                lo = NC_ if last else 0
                act.wait_ge(lg_mm[L], 1)
                act.activation(logit_e[0:NE, lo:NT], PS[0][0:NE, 0:NT - lo], ACT.Copy).then_inc(lg_ev[L], 1)
                act.wait_ge(ex_in[L], 1)
                act.activation(ex_t[:, nb0:6, :], ex_t[:, nb0:6, :], ACT.Exp).then_inc(ex_out[L], 1)
                for n, nb in enumerate(range(nb0, 6)):
                    act.wait_ge(ht_mm[L], n + 1)
                    act.activation(h_tok[:, nb, :], PS[n % 2][:, :], ACT.Copy).then_inc(ht_ev[L], 1)
                wide = NT if ctx_too else NL
                with act.Fori(0, NE // 4) as turn:
                    i = turn + L * (NE // 4)
                    for pair in range(2):
                        pr = i * 2 + pair
                        act.wait_ge(gat_mm, pr + 1)
                        act.activation(xs.rearrange("p k s -> p (k s)"), PS[2][:, :], ACT.Copy).then_inc(gat_ev, 1)
                        if ctx_too and pair == 0:
                            act.wait_ge(gatc_mm, i + 1)
                            act.activation(xsc.rearrange("p k s -> p (k s)"), PS[3][:, :], ACT.Copy).then_inc(gatc_ev, 1)
                        base = finished(L, MOE0 + 24 * pair)
                        for par in range(2):
                            act.wait_ge(slot_done, turn * 48 + base + 8 * par + 4)
                            act.activation(silu[:, par, 0:wide], PS[0][:, 0:wide], ACT.Silu).then_inc(g_ev, 1)
                        for par in range(2):
                            act.wait_ge(hidt_mm, pr * 2 + par + 1)
                            act.activation(hid_t[:, par, 0:wide], PS[3][:, 0:wide], ACT.Copy).then_inc(hidt_ev, 1)
                            act.wait_ge(slot_done, turn * 48 + base + 16 + 4 * par + 4)
                            for half in range(2):
                                ins = act.activation(y_pair[64 * par:64 * par + 64, 512 * half:512 * half + 512],
                                                     PS[0 if par else 2][64 * half:64 * half + 64, 0:512], ACT.Copy)
                            ins.then_inc(d_ev, 1)

            def x_ready_f():
                x_final(act, DEPTH - 1)

            norm(NORMS - 1, True, x_ready_f, lambda k, v: glob[:, O_FG + k:O_FG + k + 1], lambda k, v: zero_col, h_fm)

        @block.vector
        def _(dve):
            chain = Chain(dve, dve_chain)
            done = chain.done

            def norm(n, last, x_ready):
                lo = NC_ if last else 0
                x_ready()
                dve.wait_ge(rms_done, n + 1)
                if n % 2 == 0 and n < NORMS - 1:
                    modulation(n // 2)
                done(dve.reciprocal(rstd[:, lo:NT], rstd[:, lo:NT]))
                for k in range(KD):
                    if k >= 2:
                        dve.wait_ge(h_done, n * KD + k - 1)
                    dve.tensor_tensor(xr[:, k % 2, lo:NT], x_fm[:, k, lo:NT], rstd[:, lo:NT], ALU.mult
                                      ).then_inc(xr_done, 1)

            def modulation(L):
                dve.wait_ge(small_in_s[L], 16)
                for r in range(3):
                    dve.wait_ge(mod_tr[L], r + 1)
                    cols = PS[1][:, 0:512].rearrange("p (c g v) -> p g c v", c=4, g=4)[:, :, :, 0:2]
                    dst = mod[:, 16 * r:16 * r + 16, :].rearrange("p (g c) v -> p g c v", g=4)
                    b_mod = small[:, O_BMOD + 16 * r:O_BMOD + 16 * r + 16].rearrange("p (g c) -> p g c", g=4)
                    dve.tensor_tensor(dst, cols, b_mod.unsqueeze(3).broadcast_to((128, 4, 4, 2)), ALU.add
                                      ).then_inc(mod_done[L], 1)
                dve.wait_ge(mod_done[L], 3)
                for n, off in ((0, O_G1), (1, O_G2)):
                    g = small[:, off:off + KD].unsqueeze(2).broadcast_to((128, KD, 2))
                    ins = dve.scalar_tensor_tensor(out=amp[:, n, :, :], in0=mod[:, 8 + 24 * n:16 + 24 * n, :],
                                                   scalar=1.0, in1=g, op0=ALU.add, op1=ALU.mult)
                    if n == 0:
                        done(ins)
                ins.then_inc(mod_done[L], 1)

            def lambdas(L):
                init = 0.8 - 0.6 * math.exp(-0.3 * L)
                for n, dst in enumerate((lam_a, lam_b)):
                    a = small[:, O_LAM + 128 * n:O_LAM + 128 * n + 64]
                    b = small[:, O_LAM + 128 * n + 64:O_LAM + 128 * n + 128]
                    done(dve.tensor_tensor(lam_t, a, b, ALU.mult))
                    done(dve.tensor_reduce(dst, lam_t, AX, ALU.add))
                dve.tensor_scalar(sink8, small[:, O_SINK:O_SINK + 4], 1.0 / SCALE, None, ALU.mult)
                g = small[:, O_SUBG:O_SUBG + 128]
                dve.tensor_scalar(g, g, 1.0 - init, None, ALU.mult).then_inc(lam_in[L], 1)
                dve.wait_ge(lam_exp[L], 1)
                dve.tensor_scalar(neg_lam, lam_b, lam_a, -init, ALU.subtract, ALU.add).then_inc(bias_done[L], 1)

            def heads(key, trips, n_keys):
                L = key[0]
                latent = key[1] == "l"
                steps = 0
                for kind, *_ in UNITS:
                    steps += {"na": 4 if latent else 2, "diff": 5, "swa": 5 if latent else 4}[kind]
                with dve.Fori(0, trips) as turn:
                    b = turn + BLOCKS_BEFORE[key]
                    chain.enter(turn, steps + 1)

                    def maxima(n):
                        kind, qb, kb, vc, oc, br, sk = UNITS[MAPS[n][0]]
                        t8 = 8 * (n % 8)
                        mx0, mx1, nm = (tiny[:, t8 + c:t8 + c + 1] for c in (0, 1, 3))
                        dve.wait_ge(s_mm, b * N_MAPS + n + 3)
                        if kind == "diff" or not latent:
                            done(dve.tensor_reduce(mx0, PS[n % 2][:, 0:n_keys], AX, ALU.max))
                        else:
                            before = MAPS[(n - 4) % N_MAPS][0] + 1 + (N_UNITS if n >= 4 else 0)
                            dve.wait_ge(pt_mm, b * N_UNITS + before)
                            shifted = bias[:, br, bass.ds(384 - turn * 128, NL)]
                            done(dve.tensor_tensor(probs[:, n % 4, NC_:NT], PS[n % 2][:, NC_:NT], shifted, ALU.add))
                            dve.tensor_reduce(mx1, PS[n % 2][:, 0:NC_], AX, ALU.max)
                            done(dve.tensor_reduce(mx0, probs[:, n % 4, NC_:NT], AX, ALU.max))
                        both = mx1 if (kind != "diff" and latent) else mx0
                        if sk is not None:
                            done(dve.tensor_scalar(mx0, mx0, both, sink8[:, sk:sk + 1], ALU.max, ALU.max))
                            dve.tensor_scalar(nm, mx0, -SCALE, None, ALU.mult).then_inc(max_done, 1)
                        else:
                            dve.tensor_scalar(nm, mx0, both, -SCALE, ALU.max, ALU.mult).then_inc(max_done, 1)

                    def mix(u):
                        n = FIRST_MAP[u]
                        dve.wait_ge(exp_done, b * N_MAPS + n + 4)
                        s0 = tiny[:, 8 * (n % 8) + 4:8 * (n % 8) + 5]
                        s1 = tiny[:, 8 * ((n + 1) % 8) + 4:8 * ((n + 1) % 8) + 5]
                        r1 = tiny[:, 8 * ((n + 1) % 8) + 5:8 * ((n + 1) % 8) + 6]
                        coef = tiny[:, 8 * ((n + 1) % 8) + 6:8 * ((n + 1) % 8) + 7]
                        done(dve.reciprocal(r1, s1))
                        done(dve.tensor_scalar(coef, r1, s0, neg_lam, ALU.mult, ALU.mult))
                        dve.scalar_tensor_tensor(out=probs[:, n % 4, 0:n_keys], in0=probs[:, (n + 1) % 4, 0:n_keys],
                                                 scalar=coef, in1=probs[:, n % 4, 0:n_keys], op0=ALU.mult, op1=ALU.add
                                                 ).then_inc(mix_done, 1)

                    def outputs(u):
                        kind, qb, kb, vc, oc, br, sk = UNITS[u]
                        w = 128 if kind == "diff" else 64
                        t8 = 8 * (FIRST_MAP[u] % 8)
                        s0, s1, s2, rs = (tiny[:, t8 + c:t8 + c + 1] for c in (4, 5, 6, 7))
                        dve.wait_ge(o_mm, b * N_UNITS + u + 3)
                        if u == 0:
                            dve.wait_ge(ot_mm, b + 1)
                        if kind == "diff":
                            done(dve.reciprocal(rs, s0))
                        else:
                            if latent and sk is not None:
                                done(dve.tensor_scalar(s0, s0, s1, s2, ALU.add, ALU.add))
                            elif latent:
                                done(dve.tensor_scalar(s0, s0, s1, None, ALU.add))
                            elif sk is not None:
                                done(dve.tensor_scalar(s0, s0, s2, None, ALU.add))
                            done(dve.reciprocal(rs, s0))
                        dve.tensor_scalar(o_tok[:, oc:oc + w], PS[3][:, 512 * (u % 2):512 * (u % 2) + w], rs, None, ALU.mult
                                          ).then_inc(o_ev, 1)

                    for n in range(N_MAPS + 4):
                        if n < N_MAPS:
                            maxima(n)
                        if n - 1 in LAST_MAP and UNITS[LAST_MAP.index(n - 1)][0] == "diff":
                            mix(LAST_MAP.index(n - 1))
                        if n - 4 in LAST_MAP:
                            outputs(LAST_MAP.index(n - 4))
                    dve.wait_ge(sub_rms, b + 1)
                    done(dve.reciprocal(rr4, rms4))
                    dve.wait_ge(o_ev, b * N_UNITS + N_UNITS + 2)
                    for h in range(4):
                        o = o_tok[:, 256 + 128 * h:384 + 128 * h]
                        ins = dve.scalar_tensor_tensor(out=o, in0=o, scalar=rr4[:, h:h + 1],
                                                       in1=small[:, O_SUBG:O_SUBG + 128], op0=ALU.mult, op1=ALU.mult)
                    ins.then_inc(o_norm, 1)
                    if chain.count - chain.start != chain.step:
                        raise AssertionError((key, chain.count - chain.start, chain.step))
                chain.leave(trips)

            def merge_block(L, j, finish):
                lo = NC_ if L == DEPTH - 1 else 0
                dve.wait_ge(y_done[L], j + 1)
                for br in range(3):
                    if br == 2:
                        dve.wait_ge(slot_done, finish)
                    else:
                        dve.wait_ge(br_mm[L], 2 * j + 1 + br)
                    dve.tensor_tensor(term[:, br, lo:NT], gate[:, br, lo:NT], PS[br][:, 0:NT - lo], ALU.mult
                                      ).then_inc(br_ev[L], 1)
                dve.wait_ge(br_ev[L], 3 * j + 6)
                done(dve.tensor_tensor(term[:, 0, lo:NT], term[:, 0, lo:NT], term[:, 1, lo:NT], ALU.add))
                dst = y_fm[:, bass.ds(j, 1), lo:NT]
                dve.tensor_tensor(dst, term[:, 0:1, lo:NT], term[:, 2:3, lo:NT], ALU.add).then_inc(y_done[L], 1)

            dve.sem_inc(o_ev, 2)
            dve.sem_inc(cb_ev, 4)
            dve.sem_inc(cbc_ev, 2)
            dve.memset(ones[:, :], 1.0)
            dve.memset(q_pad[:, :, :], 0.0)
            dve.memset(zero_col, 0.0)
            dve.memset(eps_col, EPS).then_inc(consts_set, 1)
            dve.wait_ge(consts_in, 16)
            for L in range(DEPTH):
                last = L == DEPTH - 1
                ctx_too = not last
                nb0 = 2 if last else 0
                lo = NC_ if last else 0
                if L:
                    x_final(dve, L - 1)
                dve.memset(c_pad, 0.0).then_inc(c_zeroed[L], 1)

                def x_ready_1():
                    if L == 0:
                        dve.wait_ge(x_in_s, 16)

                norm(2 * L, False, x_ready_1)
                lambdas(L)
                dve.wait_ge(rope_in_s[L], 16)
                for n, j in enumerate(ROPE_BLOCKS):
                    dve.wait_ge(qk_ev[L], j + 1)
                    if n:
                        dve.wait_ge(rope_done[L], n)
                    v = qk[:, j, NC_:NT]
                    done(dve.stream_shuffle(rot, v, [(c + 16) % 32 for c in range(32)]))
                    dve.tensor_tensor(v, v, rope[:, 0, :], ALU.mult)
                    done(dve.tensor_tensor(rot, rot, rope[:, 1, :], ALU.mult))
                    dve.tensor_tensor(v, v, rot, ALU.add).then_inc(rope_done[L], 1)
                for nb in range(NT // 128):
                    if nb < NT // 128 - 1:
                        dve.wait_ge(v_mm[L], nb + 1)
                    else:
                        dve.wait_ge(slot_done, finished(L, V0 + V_SLOTS))
                    dve.tensor_copy(v_tok[:, nb, :].rearrange("p (c n) -> p c n", c=2),
                                    PS[nb % 4][:, :].rearrange("p (c n) -> p c n", c=2)[:, :, 0:448]).then_inc(v_ev[L], 1)
                dve.wait_ge(bias_in[L], 16 * 10)
                table = bias[:, 0:4, :].rearrange("p h (r c) -> p (h r) c", c=GRID_W)
                done(dve.scalar_tensor_tensor(out=table, in0=table, scalar=1.0 / SCALE,
                                              in1=col_mask.unsqueeze(1).broadcast_to((128, 56, GRID_W)),
                                              op0=ALU.mult, op1=ALU.add))
                if ctx_too:
                    heads((L, "c"), NC_ // 128, NC_)
                heads((L, "l"), NL // 128, NT)
                dve.sem_inc(br_ev[L], 3)
                dve.sem_inc(y_done[L], 1)
                with dve.Fori(0, 2) as i:
                    chain.enter(i, 3)
                    for j in range(3):
                        merge_block(L, 3 * i + j, finished(L, MERGE0 + 2 * j + 2) + i * 6)
                chain.leave(2)
                for j in (6, 7):
                    merge_block(L, j, finished(L, MERGE0 + 2 * j + 2))
                dve.wait_ge(x_back[L], 16)
                for j in range(KD):
                    dve.wait_ge(slot_done, finished(L, OUT0 + j // 2 + 1))
                    for v, a, b, c in segments(last):
                        ins = dve.scalar_tensor_tensor(out=x_fm[:, j, a:b], in0=PS[j % 4][:, c:c + b - a],
                                                       scalar=mod[:, 16 + j, v:v + 1], in1=x_fm[:, j, a:b],
                                                       op0=ALU.mult, op1=ALU.add)
                    ins.then_inc(out_ev[L], 1)
                dve.wait_ge(out_ev[L], KD)
                norm(2 * L + 1, last, lambda: None)
                dve.wait_ge(lt_mm[L], 1)
                nb_n = 6 - nb0
                logits = PS[1][:, 0:96].rearrange("p (n e) -> p n e", e=NE)[:, nb0:6, :]
                done(dve.tensor_reduce(red_t[:, 0, nb0:6], logits, AX, ALU.max))
                dve.tensor_tensor(ex_t[:, nb0:6, :], logits, red_t[:, 0, nb0:6].unsqueeze(2).broadcast_to((128, nb_n, NE)),
                                  ALU.subtract).then_inc(ex_in[L], 1)
                dve.wait_ge(ex_out[L], 1)
                done(dve.tensor_reduce(red_t[:, 1, nb0:6], ex_t[:, nb0:6, :], AX, ALU.add))
                done(dve.reciprocal(red_t[:, 0, nb0:6], red_t[:, 1, nb0:6]))
                dve.tensor_tensor(aff_t[:, nb0:6, :], ex_t[:, nb0:6, :],
                                  red_t[:, 0, nb0:6].unsqueeze(2).broadcast_to((128, nb_n, NE)), ALU.mult
                                  ).then_inc(aff_done[L], 1)
                done(dve.memset(zero_e[0:NE, :], 0.0))
                dve.wait_ge(at_mm[L], 1)
                dve.tensor_copy(aff_e[0:NE, lo:NT], PS[2][0:NE, lo:NT])
                done(dve.tensor_copy(work_e[0:NE, lo:NT], PS[2][0:NE, lo:NT]))
                for v, a, b, c in segments(last):
                    work = work_e[0:NE, a:b]
                    for _ in range((CAP_C if v else CAP_L) // 8):
                        done(dve.max(best[0:NE, :], work))
                        done(dve.match_replace(work, best[0:NE, :], work, -1.0))
                done(dve.tensor_tensor(mask_e[0:NE, lo:NT], work_e[0:NE, lo:NT], aff_e[0:NE, lo:NT], ALU.not_equal))
                for v, a, b, c in segments(last):
                    done(dve.tensor_tensor_scan(pos_e[0:NE, a:b], mask_e[0:NE, a:b], zero_e[0:NE, a:b], 0.0,
                                                ALU.add, ALU.add))
                dve.tensor_tensor(pos_e[0:NE, lo:NT], pos_e[0:NE, lo:NT], mask_e[0:NE, lo:NT], ALU.mult
                                  ).then_inc(pos_done[L], 1)
                dve.wait_ge(pos_tr[L], 1)
                dve.tensor_copy(pos_t[:, nb0:6, :], PS[3][:, 0:96].rearrange("p (n e) -> p n e", e=NE)[:, nb0:6, :]
                                ).then_inc(router_done[L], 1)
                dve.wait_ge(router_done[L], 1)
                wide = NT if ctx_too else NL
                with dve.Fori(0, NE // 4) as turn:
                    i = turn + L * (NE // 4)
                    chain.enter(turn, 3 if ctx_too else 2)
                    for pair in range(2):
                        pr = i * 2 + pair
                        dve.wait_ge(st_mm, pr + 1)
                        if ctx_too and pair == 0:
                            four = selc.rearrange("p n (e s) -> p n e s", s=CAP_C)
                            pos4 = pos_t[:, 0:2, bass.ds(turn * 4, 4)].unsqueeze(3).broadcast_to((128, 2, 4, CAP_C))
                            aff4 = aff_t[:, 0:2, bass.ds(turn * 4, 4)].unsqueeze(3).broadcast_to((128, 2, 4, CAP_C))
                            io4 = iota[:, 0:CAP_C].unsqueeze(1).unsqueeze(1).broadcast_to((128, 2, 4, CAP_C))
                            done(dve.tensor_tensor(four, pos4, io4, ALU.is_equal))
                            dve.tensor_tensor(selcw.rearrange("p n (e s) -> p n e s", s=CAP_C), four, aff4, ALU.mult
                                              ).then_inc(selc_done, 1)
                        two = sel.rearrange("p n (e s) -> p n e s", s=CAP_L)
                        pos2 = pos_t[:, 2:6, bass.ds(turn * 4 + 2 * pair, 2)].unsqueeze(3).broadcast_to((128, 4, 2, CAP_L))
                        aff2 = aff_t[:, 2:6, bass.ds(turn * 4 + 2 * pair, 2)].unsqueeze(3).broadcast_to((128, 4, 2, CAP_L))
                        io2 = iota.unsqueeze(1).unsqueeze(1).broadcast_to((128, 4, 2, CAP_L))
                        done(dve.tensor_tensor(two, pos2, io2, ALU.is_equal))
                        dve.tensor_tensor(selw.rearrange("p n (e s) -> p n e s", s=CAP_L), two, aff2, ALU.mult
                                          ).then_inc(sel_done, 1)
                        dve.wait_ge(st_mm, pr + 2)
                        if ctx_too and pair == 0:
                            dve.tensor_copy(selcw_t, PS[1][:, 512:768])
                        dve.tensor_copy(selw_t, PS[1][:, 0:512]).then_inc(st_ev, 1)
                        base = finished(L, MOE0 + 24 * pair)
                        for par in range(2):
                            dve.wait_ge(g_ev, pr * 2 + par + 1)
                            dve.wait_ge(slot_done, turn * 48 + base + 8 * par + 8)
                            dve.tensor_tensor(hid[:, par, 0:wide], silu[:, par, 0:wide], PS[1][:, 0:wide], ALU.mult
                                              ).then_inc(hid_done, 1)
                        if ctx_too:
                            for par in range(2):
                                q = 2 * pair + par
                                dve.wait_ge(slot_done, turn * 48 + base + 16 + 4 * par + 4)
                                for g in range(4):
                                    ins = dve.tensor_copy(y_ctx[32 * q:32 * q + 32, 256 * g:256 * g + 256],
                                                          PS[0 if par else 2][32 * g:32 * g + 32, 512:768])
                                ins.then_inc(dc_ev, 1)
                        for k in range(KD):
                            dve.wait_ge(cb_mm, pr * KD + k + 1)
                            bank = PS[1 + (k % 4) // 2][:, 512 * (k % 2):512 * (k % 2) + 512]
                            dve.scalar_tensor_tensor(out=x_fm[:, k, NC_:NT], in0=bank, scalar=mod[:, 40 + k, 0:1],
                                                     in1=x_fm[:, k, NC_:NT], op0=ALU.mult, op1=ALU.add
                                                     ).then_inc(cb_ev, 1)
                        if ctx_too and pair == 1:
                            for c in range(4):
                                dve.wait_ge(cbc_mm, i * 4 + c + 1)
                                for k in (2 * c, 2 * c + 1):
                                    at = 512 * (c % 2) + 256 * (k % 2)
                                    ins = dve.scalar_tensor_tensor(out=x_fm[:, k, 0:NC_], in0=PS[3][:, at:at + 256],
                                                                   scalar=mod[:, 40 + k, 1:2], in1=x_fm[:, k, 0:NC_],
                                                                   op0=ALU.mult, op1=ALU.add)
                                ins.then_inc(cbc_ev, 1)
                chain.leave(NE // 4)
            x_final(dve, DEPTH - 1)
            norm(NORMS - 1, True, lambda: None)


def shape_tables():
    f = np.float32
    t = np.arange(NL)
    row, col = (t // GRID_W).astype(f), (t % GRID_W).astype(f)
    inv = (f(10000.0) ** (-np.arange(16, dtype=f) / f(16))).astype(f)
    ang = np.concatenate([np.outer(inv, row)] * 2 + [np.outer(inv, col)] * 2).astype(f)
    sign = np.where(np.arange(64) % 32 < 16, f(-1), f(1))[:, None]
    rope = np.stack([np.tile(np.cos(ang), (2, 1)), np.tile(np.sin(ang) * sign, (2, 1))], axis=1).astype(f)
    p = np.arange(128)[:, None]
    swa = np.where(np.abs(np.arange(896)[None, :] - 384 - p) <= 128, f(0), f(NEG))
    start = np.clip(p % GRID_W - 8, 0, GRID_W - 16)
    k = np.arange(GRID_W)[None, :]
    cols = np.where((k >= start) & (k < start + 16), f(0), f(NEG))
    return rope, np.concatenate([swa, cols], axis=1).astype(f)


def feature_blocks(w):
    k = w.shape[0] // 128
    return w.reshape(k, 128, -1, 128).transpose(2, 1, 0, 3).reshape(-1, 128, k * 128)


def layer_stream(l, a):
    w_in = a["w_in"][l]
    slots = []
    mod = a["w_mod"][l].reshape(KD, 128, 3, SLOT)
    slots += [mod[k, :, r, :] for r in range(3) for k in range(KD)]
    swa_order = [768 + 64 * h + c for h in (0, 2, 1, 3) for c in range(64)]
    q = np.concatenate([w_in[:, 0:768], w_in[:, swa_order]], axis=1)
    qk = feature_blocks(np.concatenate([q, w_in[:, 1024:1920]], axis=1))
    qk = np.concatenate([qk, np.zeros((1, 128, 1024), qk.dtype)])
    slots += [np.concatenate([qk[2 * s], qk[2 * s + 1]], axis=1) for s in range(QK_SLOTS)]
    v = w_in[:, 1920:2816].reshape(4, 2, 128, 896).transpose(0, 2, 1, 3).reshape(4, 128, 1792)
    slots += list(np.concatenate([v, np.zeros((4, 128, SLOT - 1792), v.dtype)], axis=2))
    gates = feature_blocks(w_in[:, 2816:])
    branch = feature_blocks(np.concatenate([a["w_branch_na"][l], a["w_branch_diff"][l], a["w_branch_swa"][l]]))
    for j in range(KD):
        slots.append(np.concatenate([gates[j], gates[8 + j]], axis=1))
        slots.append(np.concatenate([gates[16 + j], branch[j]], axis=1))
    wo = feature_blocks(a["w_out"][l])
    slots += [np.concatenate([wo[2 * s], wo[2 * s + 1]], axis=1) for s in range(OUT_SLOTS)]
    gate, up, down = (a[n][l].reshape(NE, 4, 2, 128, D).transpose(0, 1, 3, 2, 4).reshape(NE, 4, 128, SLOT)
                      for n in ("w_expert_gate", "w_expert_up", "w_expert_down"))
    for e in range(0, NE, 2):
        for w, n in ((gate, e), (up, e), (gate, e + 1), (up, e + 1), (down, e), (down, e + 1)):
            slots += list(w[n])
    return slots


def columns(v):
    return v.reshape(-1, 128).T


def kernel(**inputs):
    import concourse.bacc as bacc
    from concourse.bass_utils import run_bass_kernel_spmd as run

    a = {k: np.asarray(v) for k, v in inputs.items()}
    f = a["x"].dtype
    stream = np.stack([s for l in range(DEPTH) for s in layer_stream(l, a)])
    assert stream.shape[0] == TOTAL_SLOTS, stream.shape
    tokens = np.concatenate([a["ctx"][0], a["x"][0]])
    x_fm = tokens.T.reshape(KD, 128, NT).transpose(1, 0, 2)

    def rep(v):
        return np.broadcast_to(v.reshape(1, -1), (128, v.size))

    small = np.stack([np.concatenate([
        columns(a["b_mod"][l]), columns(a["norm1_g"][l]), columns(a["norm2_g"][l]), rep(a["diff_subln_g"][l]),
        rep(a["diff_lambda"][l]), rep(a["swa_sink"][l]),
        a["w_router"][l].reshape(KD, 128, NE).transpose(1, 0, 2).reshape(128, KD * NE)], axis=1) for l in range(DEPTH)])
    c2 = np.stack([columns(a["c"][0]), columns(a["c_ctx"])], axis=2).reshape(128, 16)
    glob = np.concatenate([c2, columns(a["final_g"]), np.eye(128, dtype=f), rep(np.arange(1, 65, dtype=f))], axis=1)
    rope, mask = shape_tables()
    arrays = {"stream": stream, "x_in": x_fm, "small_in": small, "global_in": glob, "rope_in": rope,
              "mask_in": mask, "rpb_in": a["na_rpb"].reshape(DEPTH, 60, 31)}
    arrays = {k: np.ascontiguousarray(v) for k, v in arrays.items()}
    nc = bacc.Bacc("TRN2", target_bir_lowering=False, num_devices=1)
    args = [nc.dram_tensor(k, v.shape, mybir.dt.from_np(v.dtype), kind="ExternalInput").ap()
            for k, v in arrays.items()]
    out = nc.dram_tensor("out_fm", (128, KD, NL), mybir.dt.float32, kind="ExternalOutput").ap()
    build(nc, *args, out)
    r = run(nc, [arrays], core_ids=[0])
    y = r.results[0]["out_fm"]
    return np.ascontiguousarray(y.transpose(2, 1, 0).reshape(1, NL, D))
```

```python
import math
from contextlib import ExitStack

import numpy as np

import concourse.bass as bass
from concourse import mybir

D = 1024
KD = D // 128
NC_, NL = 256, 512
NT = NC_ + NL
DEPTH = 2
GRID_W = 64
NE = 16
CAP_L, CAP_C = 2 * NL // NE, 2 * NC_ // NE
W_BUFS = 3
SLOT = 2048
RING = 6
NEG = -1.0e30
SCALE = 64 ** -0.5
EPS = 1e-6
FF_HALF = 512

MOD_SLOTS, QK_SLOTS, V_SLOTS, MERGE_SLOTS, OUT_SLOTS, MOE_SLOTS = 24, 8, 4, 16, 4, 12 * NE
QK0 = MOD_SLOTS
V0 = QK0 + QK_SLOTS
MERGE0 = V0 + V_SLOTS
OUT0 = MERGE0 + MERGE_SLOTS
MOE0 = OUT0 + OUT_SLOTS
LAYER_SLOTS = MOE0 + MOE_SLOTS
TOTAL_SLOTS = DEPTH * LAYER_SLOTS

O_BMOD, O_G1, O_G2, O_SUBG, O_LAM, O_SINK, O_WR = 0, 48, 56, 64, 192, 448, 452
SMALL = O_WR + 128
O_C, O_FG, O_ID, O_IOTA = 0, 16, 24, 152
GLOBAL = O_IOTA + 64

ARENA = 27030
REGIONS = (("region_x", KD * NT), ("region_h", KD * NT), ("arena", ARENA))

N_Q, N_K = 8, 7
ROPE_BLOCKS = (2, 3, 4, 5, 6, 7, 10, 11, 12, 13, 14)
N_UNITS, N_MAPS = 12, 16


def unit_list():
    units = []
    for h in range(4):
        units.append(("na", h // 2, 8 + h // 2, 64 * h, 64 * h, h, None))
    for h in range(4):
        units.append(("diff", 2 + h, 10 + h, 256 + 128 * h, 256 + 128 * h, None, None))
    for j in range(2):
        for kv in range(2):
            head = 2 * kv + j
            units.append(("swa", 6 + j, 14, 768 + 64 * kv, 768 + 64 * head, 4, head))
    return units


def build(nc, stream, x_in, small_in, global_in, rope_in, mask_in, rpb_in, out):
    f32, f32r = mybir.dt.float32, mybir.dt.float32r
    ALU = mybir.AluOpType
    ACT = mybir.ActivationFunctionType
    AX = mybir.AxisListType.X
    UNITS = unit_list()
    MAPS = [(u, half) for u in range(N_UNITS) for half in ((0, 1) if UNITS[u][0] == "diff" else (None,))]
    FIRST_MAP = [min(n for n, (v, _) in enumerate(MAPS) if v == u) for u in range(N_UNITS)]
    LAST_MAP = [max(n for n, (v, _) in enumerate(MAPS) if v == u) for u in range(N_UNITS)]
    ctx = ExitStack()
    with ctx:
        def sb(name, shape, dtype=f32, stack=ctx):
            return stack.enter_context(nc.sbuf_tensor(name, shape, dtype))

        def sem(name):
            return ctx.enter_context(nc.semaphore(name))

        def sems(name):
            return [sem(f"{name}{L}") for L in range(DEPTH)]

        ring = sb("ring", [128, RING, SLOT])
        small = sb("small", [128, SMALL])
        glob = sb("glob", [128, GLOBAL])
        ones = sb("ones", [128, 128])
        mod = sb("mod", [128, 48, 2])
        amp = sb("amp", [128, 2, KD, 2])
        tiny = sb("tiny", [128, 96])
        junk = sb("junk", [128, 128])
        q_pad = sb("q_pad", [128, 2, 128])
        with ExitStack() as place:
            region_x, region_h, arena = (sb(n, [128, w], f32, place) for n, w in REGIONS)
        region_x_r, region_h_r = (sb(n + "_r", [128, w], f32r) for n, w in REGIONS[:2])
        merge_out = sb("merge_out", [128, KD + 3, NT])
        h_hi_r = sb("h_hi_r", [128, KD, NT], f32r)
        o_hi_r = sb("o_hi_r", [128, KD, NT], f32r)
        w_hi_r = sb("w_hi_r", [128, W_BUFS, 1024], f32r)
        w_lo_r = sb("w_lo_r", [128, W_BUFS, 1024], f32r)
        x_fm = region_x[:, :].rearrange("p (k t) -> p k t", k=KD)
        o_fm = x_fm
        h_fm = region_h[:, :].rearrange("p (k t) -> p k t", k=KD)
        h_tok = region_h[:, :].rearrange("p (n d) -> p n d", n=NT // 128)
        ident = glob[:, O_ID:O_ID + 128]
        iota = glob[:, O_IOTA:O_IOTA + 64]
        eps_col, neg_lam, lam_a, lam_b = (tiny[:, c:c + 1] for c in (64, 65, 66, 67))
        sink8, ssq, rms4, rr4, zero_col = tiny[:, 68:72], tiny[:, 72:76], tiny[:, 76:80], tiny[:, 80:84], tiny[:, 84:85]

        def carve(at, *dims):
            n = int(np.prod(dims))
            assert at + n <= ARENA, (at, n)
            flat = arena[:, at:at + n]
            if len(dims) == 2:
                flat = flat.rearrange("p (a b) -> p a b", a=dims[0])
            return flat, at + n

        qk, a_v = carve(0, N_Q + N_K, NT)
        v_tok, a_b = carve(a_v, NT // 128, 896)
        bias, a_p = carve(a_b, 5, 896)
        probs, a_t = carve(a_p, 4, NT)
        probs_t, a_o = carve(a_t, 2, NT)
        o_tok, _ = carve(a_o, D)
        rope, a1 = carve(a_p, 2, NL)
        rot, a1 = carve(a1, NL)
        col_mask, _ = carve(a1, GRID_W)
        sq, a1 = carve(0, 2, NT)
        rstd, a1 = carve(a1, NT)
        xr, a1 = carve(a1, 2, NT)
        c_pad, a1 = carve(a1, KD, 32)
        mod_row, a1 = carve(a1, 512)
        rpb_pad = arena[0:60, a1:a1 + 128]
        lam_t, _ = carve(a1 + 128, 64)
        y_fm = merge_out[:, 0:KD, :]
        gate = merge_out[:, KD:KD + 3, :]
        h_hi, o_hi, w_hi = (r[:, :, :].bitcast(f32) for r in (h_hi_r, o_hi_r, w_hi_r))
        h_lo_r, o_lo_r = (r[:, :].rearrange("p (k t) -> p k t", k=KD) for r in (region_h_r, region_x_r))
        h2_fm, a_e = carve(KD * NT, KD, NT)
        logit_e, a1 = carve(a_e, NT)
        aff_e, a1 = carve(a1, NT)
        work_e, a1 = carve(a1, NT)
        pos_e, a1 = carve(a1, NT)
        mask_e, a1 = carve(a1, NT)
        zero_e, a1 = carve(a1, NT)
        best, a1 = carve(a1, 8)
        ex_t, a1 = carve(a1, 6, NE)
        red_t, a1 = carve(a1, 2, 6)
        aff_t, a1 = carve(a1, 6, NE)
        pos_t, a_s = carve(a1, 6, NE + 4)
        sel, a1 = carve(a_s, 4, 128)
        selw, a1 = carve(a1, 4, 128)
        selc, a1 = carve(a1, 2, 128)
        selcw, a1 = carve(a1, 2, 128)
        selw_t, a1 = carve(a1, NL)
        selcw_t, a1 = carve(a1, NC_)
        xs, a1 = carve(a1, KD, 128)
        xsc, a1 = carve(a1, KD, 128)
        silu, a1 = carve(0, 2, NT)
        hid, a1 = carve(a1, 2, NT)
        hid_t, a1 = carve(a1, 2, NT)
        y_pair, a1 = carve(a1, D)
        y_ctx, a1 = carve(a1, D)

        PS = [ctx.enter_context(nc.psum_tensor(f"PS{i}", [128, 1024], f32)) for i in range(4)]
        rpb_scr = [nc.dram_tensor(f"rpb_scr{L}", (60, 64, 128), f32, kind="Internal").ap() for L in range(DEPTH)]
        x_scr = nc.dram_tensor("x_scr", (128, KD, NT), f32, kind="Internal").ap()

        slot_loaded, slot_done = [sem(f"slot_loaded{s}") for s in range(RING)], sem("slot_done")
        consts_in, x_in_s, x_saved, out_done = sem("consts_in"), sem("x_in_s"), sem("x_saved"), sem("out_done")
        pad_zeroed = sem("pad_zeroed")
        small_in_s, rpb_in_s, rpb_out, bias_in, rope_in_s, x_back = (
            sems("small_in"), sems("rpb_in"), sems("rpb_out"), sems("bias_in"), sems("rope_in"), sems("x_back"))
        c_zeroed, c_ready, mod_ev, mod_tr, mod_done = (
            sems("c_zeroed"), sems("c_ready"), sems("mod_ev"), sems("mod_tr"), sems("mod_done"))
        NORMS = 2 * DEPTH + 1
        sq_done, sum_done, rms_done, xr_done, h_done = (
            sem("sq_done"), sem("sum_done"), sem("rms_done"), sem("xr_done"), sem("h_done"))
        consts_set = sem("consts_set")
        lam_in, lam_exp = sems("lam_in"), sems("lam_exp")
        qk_ev, rope_done, v_mm, v_ev, bias_done = (
            sems("qk_ev"), sems("rope_done"), sems("v_mm"), sems("v_ev"), sems("bias_done"))
        BLOCKS_BEFORE, n = {}, 0
        for L in range(DEPTH):
            for name, tokens in (("c", 0 if L == DEPTH - 1 else NC_), ("l", NL)):
                BLOCKS_BEFORE[L, name] = n
                n += tokens // 128
        q_staged, s_mm, max_done, exp_done, mix_done, pt_mm, pt_ev = (
            sem("q_staged"), sem("s_mm"), sem("max_done"), sem("exp_done"),
            sem("mix_done"), sem("pt_mm"), sem("pt_ev"))
        o_mm, o_ev, sub_rms, o_norm, ot_mm, ot_ev = (
            sem("o_mm"), sem("o_ev"), sem("sub_rms"), sem("o_norm"),
            sem("ot_mm"), sem("ot_ev"))
        gate_ev, br_ev, y_done, out_ev = sems("gate_ev"), sems("br_ev"), sems("y_done"), sems("out_ev")
        prod_mm, w_hi_done, w_lo_done, hi_done, lo_done = (
            sem("prod_mm"), sem("w_hi_done"), sem("w_lo_done"), sem("hi_done"), sem("lo_done"))
        lg_mm, lg_ev, lt_mm, ex_in, ex_out, aff_done, at_mm, pos_done, pos_tr, router_done = (
            sems("lg_mm"), sems("lg_ev"), sems("lt_mm"), sems("ex_in"), sems("ex_out"), sems("aff_done"),
            sems("at_mm"), sems("pos_done"), sems("pos_tr"), sems("router_done"))
        ht_mm, ht_ev = sems("ht_mm"), sems("ht_ev")
        sel_done, selc_done, gat_mm, gat_ev, gatc_mm, gatc_ev, st_mm, st_ev = (
            sem("sel_done"), sem("selc_done"), sem("gat_mm"), sem("gat_ev"), sem("gatc_mm"),
            sem("gatc_ev"), sem("st_mm"), sem("st_ev"))
        selw_done, y_zeroed = sem("selw_done"), sems("y_zeroed")
        g_ev, hid_done, hidt_mm, hidt_ev, d_ev, dc_ev, cb_mm, cb_ev, cbc_mm, cbc_ev = (
            sem("g_ev"), sem("hid_done"), sem("hidt_mm"), sem("hidt_ev"), sem("d_ev"), sem("dc_ev"),
            sem("cb_mm"), sem("cb_ev"), sem("cbc_mm"), sem("cbc_ev"))
        dve_chain, act_chain = sem("dve_chain"), sem("act_chain")

        ROUNDS, ROUNDS_C = NE // 2 + 1, NE // 4 + 1

        def products(L, n):
            return 6 + 7 * KD * L + n

        def units(L, n):
            return products(L, 6 * (n // 4) + n % 4 if n <= 4 * KD else 2 * KD + n)

        class Chain:

            def __init__(self, engine, s):
                self.engine, self.s, self.count, self.extra = engine, s, 0, 0

            def done(self, ins):
                self.count += 1
                ins.then_inc(self.s, 1)
                self.engine.wait_ge(self.s, self.count + self.extra)

            def enter(self, i, step):
                self.start, self.step, self.extra = self.count, step, i * step

            def leave(self, trips):
                assert self.count - self.start == self.step, (self.count - self.start, self.step)
                self.count, self.extra = self.start + self.step * trips, 0

        def finished(L, slots):
            return RING + L * LAYER_SLOTS + slots

        def pieces(last):
            return [(NC_, NT, 0)] if last else [(0, 512, 0), (512, NT, 512)]

        def segments(last):
            return [(0, NC_, NT, 0)] if last else [(1, 0, NC_, 0), (0, NC_, NT, NC_)]

        def x_final(engine, L):
            engine.wait_ge(cb_ev, 4 + (L + 1) * KD * ROUNDS)
            if L < DEPTH - 1:
                engine.wait_ge(cbc_ev, 2 + (L + 1) * 4 * ROUNDS_C)

        block = ctx.enter_context(nc.Block())

        @block.sync
        def _(sp):
            rows = stream.rearrange("s p n -> p s n")

            def load(t, s, rotation):
                sp.wait_ge(slot_done, rotation * RING + s + 1)
                sp.dma_start(ring[:, s:s + 1, :], rows[:, bass.ds(t, 1), :]).then_inc(slot_loaded[s], 16)

            with sp.Fori(0, TOTAL_SLOTS // RING) as i:
                for s in range(RING):
                    load(i * RING + s, s, i)
            for s in range(TOTAL_SLOTS % RING):
                load(TOTAL_SLOTS - TOTAL_SLOTS % RING + s, s, TOTAL_SLOTS // RING)
            sp.wait_ge(h_done, NORMS * KD)
            sp.dma_start(out, h_fm[:, :, NC_:NT]).then_inc(out_done, 16)
            sp.wait_ge(out_done, 16)

        @block.gpsimd
        def _(pool):
            pool.dma_start(x_fm, x_in).then_inc(x_in_s, 16)
            pool.dma_start(glob[:, :], global_in).then_inc(consts_in, 16)
            for L in range(DEPTH):
                last = L == DEPTH - 1
                if L:
                    x_final(pool, L - 1)
                    pool.dma_start(x_scr, x_fm).then_inc(x_saved, 16)
                pool.dma_start(small[:, :], small_in[L]).then_inc(small_in_s[L], 16)
                pool.memset(rpb_pad, 0.0).then_inc(pad_zeroed, 1)
                pool.wait_ge(pad_zeroed, L + 1)
                pool.dma_start(rpb_pad[:, 48:79], rpb_in[L]).then_inc(rpb_in_s[L], 16)
                pool.wait_ge(rpb_in_s[L], 16)
                pool.dma_start(rpb_scr[L], rpb_pad.unsqueeze(1).broadcast_to((60, 64, 128))).then_inc(rpb_out[L], 16)
                pool.dma_start(bias[:, 4, :], mask_in[:, 0:896]).then_inc(bias_in[L], 16)
                pool.dma_start(col_mask, mask_in[:, 896:896 + GRID_W]).then_inc(bias_in[L], 16)
                pool.dma_start(rope, rope_in).then_inc(rope_in_s[L], 16)
                pool.wait_ge(rpb_out[L], 16)
                for h in range(4):
                    for half in range(2):
                        first = (15 * h + 1 - half) * 64 * 128 + GRID_W - 1
                        shifted = bass.AP(rpb_scr[L].tensor, first, [[127, 64], [64 * 128, 14], [1, 64]])
                        dst = bias[64 * half:64 * half + 64, h, :].rearrange("p (r c) -> p r c", c=64)
                        pool.dma_start(dst, shifted).then_inc(bias_in[L], 16)

                def stage_queries(key, first, trips):
                    with pool.Fori(0, trips) as turn:
                        b = turn + BLOCKS_BEFORE[key]
                        for n, (u, _) in enumerate(MAPS):
                            half = 64 * (n % 2)
                            pool.wait_ge(s_mm, b * N_MAPS + n + 1)
                            pool.tensor_copy(q_pad[half:half + 64, n % 2, :],
                                             qk[half:half + 64, UNITS[u][1], bass.ds(turn * 128 + first, 128)]
                                             ).then_inc(q_staged, 1)

                pool.wait_ge(qk_ev[L], N_Q + N_K)
                pool.wait_ge(rope_done[L], len(ROPE_BLOCKS))
                if not last:
                    stage_queries((L, "c"), 0, NC_ // 128)
                stage_queries((L, "l"), NC_, NL // 128)

                def lower_weights(n, i=0):
                    pool.wait_ge(w_hi_done, 5 * KD * L + n + 1 + i * 12)
                    slot = (L * LAYER_SLOTS + MERGE0 + n // 2) % RING
                    ins = pool.tensor_tensor(w_lo_r[:, n % W_BUFS, :], ring[:, slot, 1024 * (n % 2):1024 * (n % 2) + 1024],
                                             w_hi[:, n % W_BUFS, :], ALU.subtract)
                    ins.then_inc(w_lo_done, 1)
                    if n % 2:
                        pool.wait_ge(w_lo_done, 5 * KD * L + n + 1 + i * 12)
                        pool.sem_inc(slot_done, 1)

                with pool.Fori(0, 2) as i:
                    for n in range(12):
                        lower_weights(n, i)
                for n in range(24, 34):
                    lower_weights(n)
                pool.wait_ge(y_done[L], KD + 1)
                if L:
                    pool.wait_ge(x_saved, 16)
                pool.dma_start(x_fm, x_scr if L else x_in).then_inc(x_back[L], 16)
                for n in range(34, 5 * KD):
                    lower_weights(n)

        @block.tensor
        def _(pe):
            def take(L, t, rotations=0):
                n = L * LAYER_SLOTS + t
                pe.wait_ge(slot_loaded[n % RING], (rotations + n // RING + 1) * 16)
                return ring[:, n % RING, :]

            def norm_sums(n, last):
                for k in range(KD):
                    pe.wait_ge(sq_done, n * KD + k + 1)
                    for lo, hi, c in pieces(last):
                        m = pe.matmul(PS[2][:, c:c + hi - lo], ones[:, :], sq[:, k % 2, lo:hi],
                                      start=(k == 0), stop=(k == KD - 1))
                    m.then_inc(sum_done, 1)

            def product(tile, weights, moving, last):
                for k in range(KD):
                    for lo, hi, c in pieces(last):
                        m = pe.matmul(PS[tile][:, c:c + hi - lo], weights[:, 128 * k:128 * k + 128],
                                      moving[:, k, lo:hi], start=(k == 0), stop=(k == KD - 1))
                return m

            def heads(key, trips, n_keys):
                with pe.Fori(0, trips) as turn:
                    b = turn + BLOCKS_BEFORE[key]
                    def scores(n):
                        pe.wait_ge(q_staged, b * N_MAPS + n + 1)
                        pe.wait_ge(exp_done, b * N_MAPS + n + 1)
                        for lo in range(0, n_keys, 512):
                            hi = min(lo + 512, n_keys)
                            m = pe.matmul(PS[n % 2][:, lo:hi], q_pad[:, n % 2, :], qk[:, UNITS[MAPS[n][0]][2], lo:hi],
                                          start=True, stop=True)
                        m.then_inc(s_mm, 1)

                    def transposes(u):
                        if UNITS[u][0] == "diff":
                            pe.wait_ge(mix_done, b * 4 + u - 4 + 1)
                        else:
                            pe.wait_ge(exp_done, b * N_MAPS + FIRST_MAP[u] + 3)
                        pe.wait_ge(pt_ev, b * N_UNITS + u + 1)
                        if u == 0:
                            pe.wait_ge(ot_ev, b + 1)
                        for kb in range(n_keys // 128):
                            m = pe.transpose(PS[2][:, 128 * kb:128 * kb + 128],
                                             probs[:, FIRST_MAP[u] % 4, 128 * kb:128 * kb + 128], ident)
                        m.then_inc(pt_mm, 1)

                    def values(u):
                        kind, qb, kb_, vc, oc, br, sk = UNITS[u]
                        w = 128 if kind == "diff" else 64
                        pe.wait_ge(pt_ev, b * N_UNITS + u + 2)
                        pe.wait_ge(o_ev, b * N_UNITS + u + 1)
                        for kb in range(n_keys // 128):
                            m = pe.matmul(PS[3][:, 512 * (u % 2):512 * (u % 2) + w],
                                          probs_t[:, u % 2, 128 * kb:128 * kb + 128], v_tok[:, kb, vc:vc + w],
                                          start=(kb == 0), stop=(kb == n_keys // 128 - 1))
                        m.then_inc(o_mm, 1)

                    scores(0)
                    for n in range(N_MAPS + 3):
                        if n + 1 < N_MAPS:
                            scores(n + 1)
                        if n - 2 in LAST_MAP:
                            transposes(LAST_MAP.index(n - 2))
                        if n - 3 in LAST_MAP:
                            values(LAST_MAP.index(n - 3))
                    pe.wait_ge(o_norm, b + 1)
                    for k in range(KD):
                        m = pe.transpose(PS[2][:, 128 * k:128 * k + 128], o_tok[:, 128 * k:128 * k + 128], ident)
                    m.then_inc(ot_mm, 1)
                pe.wait_ge(ot_ev, BLOCKS_BEFORE[key] + trips + 1)

            def split_product(tile, n, hi, lo_, last, k0=0, kn=KD, arriving=None):
                b = n % W_BUFS
                for k in range(k0, k0 + kn):
                    if arriving is not None:
                        pe.wait_ge(lo_done, arriving + k + 1)
                    for lo, hi_t, c in pieces(last):
                        for w, v in ((w_hi_r, hi), (w_hi_r, lo_), (w_lo_r, hi)):
                            m = pe.matmul(PS[tile][:, c:c + hi_t - lo], w[:, b, 128 * k:128 * k + 128], v[:, k, lo:hi_t],
                                          start=(k == k0 and w is w_hi_r and v is hi),
                                          stop=(k == k0 + kn - 1 and w is w_lo_r))
                m.then_inc(prod_mm, 1)

            def merge_block(L, j, i=0):
                last = L == DEPTH - 1
                block = 3 * i + j
                for br in range(3):
                    pe.wait_ge(w_lo_done, 5 * KD * L + 4 * block + br + 1)
                    pe.wait_ge(br_ev[L], 3 * block + br + 1)
                    split_product(br, 4 * j + br, h_hi_r, h_lo_r, last,
                                  arriving=3 * KD * L if j == 0 and br == 0 else None)
                pe.wait_ge(w_lo_done, 5 * KD * L + 4 * block + 4)
                for br, (k0, kn) in enumerate(((0, 2), (2, 4), (6, 2))):
                    pe.wait_ge(gate_ev[L], 3 * block + br + 1)
                    split_product(br, 4 * j + 3, o_hi_r, o_lo_r, last, k0, kn,
                                  arriving=(3 * L + 1) * KD if j == 0 else None)

            def expert_up(L, turn, t, tile, lhs, lhs_c, ctx_too):
                passes = (0, 1) if ctx_too else (0,)
                for p in passes:
                    for s in range(4):
                        w = take(L, t + s, 8 * turn) if p == 0 else ring[:, (L * LAYER_SLOTS + t + s) % RING, :]
                        for kk in range(2):
                            k = 2 * s + kk
                            row = w[:, 1024 * kk:1024 * kk + 1024]
                            n_t, width, src, at = ((2, 512, lhs, 0), (4, 256, lhs_c, 512))[p]
                            for g in range(n_t):
                                m = pe.matmul(PS[tile][128 // n_t * g:128 // n_t * (g + 1), at:at + width],
                                              src(k), row[:, width * g:width * (g + 1)],
                                              start=(k == 0), stop=(k == KD - 1))
                        if p == passes[-1]:
                            m.then_inc(slot_done, 1)

            pe.sem_inc(slot_done, RING)
            pe.sem_inc(prod_mm, 6)
            pe.sem_inc(s_mm, 2)
            pe.sem_inc(pt_mm, N_UNITS)
            pe.sem_inc(o_mm, 2)
            pe.sem_inc(ot_mm, 1)
            pe.sem_inc(st_mm, 1)
            pe.wait_ge(consts_in, 16)
            pe.wait_ge(consts_set, 1)
            for L in range(DEPTH):
                last = L == DEPTH - 1
                ctx_too = not last
                norm_sums(2 * L, False)
                pe.wait_ge(c_ready[L], 1)
                for r in range(3):
                    if r:
                        pe.wait_ge(mod_ev[L], r)
                    for k in range(KD):
                        w = take(L, KD * r + k)
                        for g in range(4):
                            m = pe.matmul(PS[0][32 * g:32 * g + 32, 0:512], c_pad[:, k, :], w[:, 512 * g:512 * g + 512],
                                          start=(k == 0), stop=(k == KD - 1))
                        m.then_inc(slot_done, 1)
                    pe.wait_ge(mod_ev[L], r + 1)
                    if r:
                        pe.wait_ge(mod_done[L], r)
                    for c in range(4):
                        m = pe.transpose(PS[1][:, 128 * c:128 * c + 128], mod_row[:, 128 * c:128 * c + 128], ident)
                    m.then_inc(mod_tr[L], 1)
                pe.wait_ge(h_done, (2 * L + 1) * KD)
                pe.wait_ge(mod_done[L], 3)
                for s in range(QK_SLOTS):
                    if s >= 2:
                        pe.wait_ge(qk_ev[L], 2 * s - 2)
                    w = take(L, QK0 + s)
                    for j in (2 * s, 2 * s + 1):
                        if j < N_Q + N_K:
                            m = product(j % 4, w[:, 1024 * (j % 2):1024 * (j % 2) + 1024], h_fm, last and j < N_Q)
                    m.then_inc(slot_done, 1)
                wv = [take(L, V0 + s) for s in range(V_SLOTS)]
                pe.wait_ge(qk_ev[L], N_Q + N_K)
                for nb in range(NT // 128):
                    if nb >= 4:
                        pe.wait_ge(v_ev[L], nb - 3)
                    for k in range(KD):
                        for c in range(2):
                            m = pe.matmul(PS[nb % 4][:, 512 * c:512 * c + 448], h_fm[:, k, 128 * nb:128 * nb + 128],
                                          wv[k // 2][:, 896 * (k % 2) + 448 * c:896 * (k % 2) + 448 * c + 448],
                                          start=(k == 0), stop=(k == KD - 1))
                    if nb < NT // 128 - 1:
                        m.then_inc(v_mm[L], 1)
                    else:
                        m.then_inc(slot_done, V_SLOTS)
                pe.wait_ge(v_ev[L], NT // 128)
                pe.wait_ge(rope_done[L], len(ROPE_BLOCKS))
                if ctx_too:
                    heads((L, "c"), NC_ // 128, NC_)
                heads((L, "l"), NL // 128, NT)
                with pe.Fori(0, 2) as i:
                    for j in range(3):
                        merge_block(L, j, i)
                for j in (6, 7):
                    merge_block(L, j)
                for j in range(KD):
                    pe.wait_ge(w_lo_done, 5 * KD * L + 4 * KD + j + 1)
                    if j < 3:
                        pe.wait_ge(br_ev[L], 3 * KD + j + 1)
                    elif j >= 4:
                        pe.wait_ge(out_ev[L], j - 3)
                    split_product(j % 4, 4 * KD + j, h_hi_r, h_lo_r, last,
                                  arriving=(3 * L + 2) * KD if j == 0 else None)
                pe.wait_ge(out_ev[L], KD)
                norm_sums(2 * L + 1, last)
                nb0 = 2 if last else 0
                pe.wait_ge(h_done, (2 * L + 2) * KD)
                for k in range(KD):
                    for lo, hi, c in pieces(last):
                        m = pe.matmul(PS[0][0:NE, c:c + hi - lo], small[:, O_WR + NE * k:O_WR + NE * k + NE],
                                      h2_fm[:, k, lo:hi], start=(k == 0), stop=(k == KD - 1))
                m.then_inc(lg_mm[L], 1)
                pe.wait_ge(lg_ev[L], 1)
                for nb in range(nb0, 6):
                    m = pe.transpose(PS[1][:, NE * nb:NE * nb + NE], logit_e[0:NE, 128 * nb:128 * nb + 128],
                                     ident[0:NE, 0:NE])
                m.then_inc(lt_mm[L], 1)
                pe.wait_ge(aff_done[L], 1)
                for nb in range(nb0, 6):
                    m = pe.transpose(PS[2][0:NE, 128 * nb:128 * nb + 128], aff_t[:, nb, :], ident)
                m.then_inc(at_mm[L], 1)
                for n, nb in enumerate(range(nb0, 6)):
                    if n >= 2:
                        pe.wait_ge(ht_ev[L], n - 1)
                    for k in range(KD):
                        m = pe.transpose(PS[n % 2][:, 128 * k:128 * k + 128], h2_fm[:, k, 128 * nb:128 * nb + 128], ident)
                    m.then_inc(ht_mm[L], 1)
                pe.wait_ge(pos_done[L], 1)
                for nb in range(nb0, 6):
                    m = pe.transpose(PS[3][:, NE * nb:NE * nb + NE], pos_e[0:NE, 128 * nb:128 * nb + 128],
                                     ident[0:NE, 0:NE])
                m.then_inc(pos_tr[L], 1)
                pe.wait_ge(router_done[L], 1)
                pe.wait_ge(ht_ev[L], 6 - nb0)
                def gather(p):
                    pe.wait_ge(sel_done, L * ROUNDS + p + 1)
                    for k in range(KD):
                        for nb in range(4):
                            m = pe.matmul(PS[2][:, 128 * k:128 * k + 128], h_tok[:, 2 + nb, 128 * k:128 * k + 128],
                                          sel[:, nb, :], start=(nb == 0), stop=(nb == 3))
                    m.then_inc(gat_mm, 1)

                def gather_context(p):
                    pe.wait_ge(selc_done, p + 1)
                    for k in range(KD):
                        for nb in range(2):
                            m = pe.matmul(PS[0][:, 128 * k:128 * k + 128], h_tok[:, nb, 128 * k:128 * k + 128],
                                          selc[:, nb, :], start=(nb == 0), stop=(nb == 1))
                    m.then_inc(gatc_mm, 1)

                def combine(p):
                    n = L * ROUNDS + p
                    for k in range(KD):
                        pe.wait_ge(cb_ev, n * KD + k + 1)
                        bank = PS[2 + (k % 4) // 2][:, 512 * (k % 2):512 * (k % 2) + 512]
                        pe.matmul(bank, y_pair[:, 128 * k:128 * k + 128], selw_t, start=True, stop=True
                                  ).then_inc(cb_mm, 1)
                    pe.wait_ge(cb_ev, n * KD + KD + 4)

                def combine_context(p):
                    for c in range(4):
                        pe.wait_ge(cbc_ev, p * 4 + c + 1)
                        for k in (2 * c, 2 * c + 1):
                            at = 512 * (c % 2) + 256 * (k % 2)
                            m = pe.matmul(PS[3][:, at:at + 256], y_ctx[:, 128 * k:128 * k + 128], selcw_t,
                                          start=True, stop=True)
                        m.then_inc(cbc_mm, 1)
                    pe.wait_ge(cbc_ev, p * 4 + 4 + 2)

                take(L, MOE0 + RING - 1)
                gather(0)
                if ctx_too:
                    gather_context(0)
                    pe.wait_ge(gatc_ev, 1)
                pe.wait_ge(gat_ev, L * ROUNDS + 1)
                pe.wait_ge(y_zeroed[L], 1)
                with pe.Fori(0, NE // 4) as turn:
                    i = turn + L * (NE // 4)
                    for pair in range(2):
                        pr = i * 2 + pair
                        p = turn * 2 + pair
                        t = MOE0 + 24 * pair

                        def gate_up(par):
                            q = 2 * pair + par
                            e = i * 4 + q

                            def lhs(k):
                                return xs[:, k, 64 * par:64 * par + 64]

                            def lhs_c(k):
                                return xsc[:, k, 32 * q:32 * q + 32]

                            if par:
                                pe.wait_ge(g_ev, e)
                            expert_up(L, turn, t + 8 * par, 0, lhs, lhs_c, ctx_too)
                            if par:
                                pe.wait_ge(hid_done, e)
                            expert_up(L, turn, t + 8 * par + 4, 1, lhs, lhs_c, ctx_too)

                        def down(par):
                            q = 2 * pair + par
                            e = i * 4 + q
                            pe.wait_ge(hid_done, e + 1)
                            if par:
                                pe.wait_ge(hidt_ev, e)
                            else:
                                pe.wait_ge(st_ev, pr + 1)
                            for c in range(6 if ctx_too else 4):
                                m = pe.transpose(PS[3][:, 128 * c:128 * c + 128], hid[:, q % 2, 128 * c:128 * c + 128], ident)
                            m.then_inc(hidt_mm, 1)
                            if par:
                                pe.wait_ge(g_ev, e + 1)
                                if ctx_too and pair == 1:
                                    pe.wait_ge(gatc_ev, turn + 2)
                            else:
                                pe.wait_ge(gat_ev, L * ROUNDS + p + 2)
                            pe.wait_ge(hidt_ev, e + 1)

                            def lhs(k):
                                at = 128 * (k % 4) + 64 * (k // 4)
                                return hid_t[:, q % 2, at:at + 64]

                            def lhs_c(k):
                                at = 512 + 128 * (k % 2) + 32 * (k // 2)
                                return hid_t[:, q % 2, at:at + 32]

                            expert_up(L, turn, t + 16 + 4 * par, 0 if par else 2, lhs, lhs_c, ctx_too)

                        pe.wait_ge(d_ev, pr * 2 + 1)
                        if ctx_too:
                            pe.wait_ge(dc_ev, pr * 2 + 1)
                        gate_up(0)
                        combine(p)
                        if ctx_too and pair == 0:
                            combine_context(turn)
                        gate_up(1)
                        pe.wait_ge(selw_done, pr + 1)
                        for nb in range(4):
                            m = pe.transpose(PS[3][:, 128 * nb:128 * nb + 128], selw[:, nb, :], ident)
                        if ctx_too and pair == 0:
                            for nb in range(2):
                                m = pe.transpose(PS[3][:, 512 + 128 * nb:512 + 128 * nb + 128], selcw[:, nb, :], ident)
                        m.then_inc(st_mm, 1)
                        gather(p + 1)
                        if ctx_too and pair == 1:
                            pe.wait_ge(g_ev, i * 4 + 4)
                            gather_context(turn + 1)
                        down(0)
                        down(1)
                pe.wait_ge(d_ev, (L + 1) * NE + 1)
                if ctx_too:
                    pe.wait_ge(dc_ev, (L + 1) * NE + 1)
                combine(NE // 2)
                if ctx_too:
                    combine_context(NE // 4)
                x_final(pe, L)
            norm_sums(NORMS - 1, True)

        @block.scalar
        def _(act):
            chain = Chain(act, act_chain)

            def norm(n, last, x_ready, gains, shifts, dst):
                x_ready()
                lo = NC_ if last else 0
                for k in range(KD):
                    if k >= 2:
                        act.wait_ge(sum_done, n * KD + k - 1)
                    act.activation(sq[:, k % 2, lo:NT], x_fm[:, k, lo:NT], ACT.Square).then_inc(sq_done, 1)
                act.wait_ge(sum_done, n * KD + KD)
                act.activation(rstd[:, lo:NT], PS[2][:, 0:NT - lo], ACT.Sqrt, bias=eps_col, scale=1.0 / D
                               ).then_inc(rms_done, 1)
                if n % 2 == 0 and n < NORMS - 1:
                    modulation(n // 2)
                if n < NORMS - 1:
                    act.wait_ge(mod_done[n // 2], 4)
                for k in range(KD):
                    act.wait_ge(xr_done, n * KD + k + 1)
                    for m_i, (v, a, b, c) in enumerate(segments(last)):
                        ins = act.activation(dst[:, k, a:b], xr[:, k % 2, a:b], ACT.Identity,
                                             bias=shifts(k, v), scale=gains(k, v))
                    ins.then_inc(h_done, 1)

            def modulation(L):
                for r in range(3):
                    act.wait_ge(slot_done, finished(L, KD * (r + 1)))
                    if r:
                        act.wait_ge(mod_tr[L], r)
                    act.activation(mod_row, PS[0][:, 0:512], ACT.Copy).then_inc(mod_ev[L], 1)

            def heads(key, first, trips, n_keys):
                L = key[0]
                latent = key[1] == "l"
                with act.Fori(0, trips) as turn:
                    b = turn + BLOCKS_BEFORE[key]
                    chain.enter(turn, 4)

                    def exps(n):
                        kind, qb, kb, vc, oc, br, sk = UNITS[MAPS[n][0]]
                        t8 = 8 * (n % 8)
                        nm = tiny[:, t8 + 3:t8 + 4]
                        act.wait_ge(max_done, b * N_MAPS + n + 1)
                        if kind == "diff" or not latent:
                            before = MAPS[(n - 4) % N_MAPS][0] + 1 + (N_UNITS if n >= 4 else 0)
                            act.wait_ge(pt_mm, b * N_UNITS + before)
                            if sk is not None:
                                act.activation(tiny[:, t8 + 6:t8 + 7], sink8[:, sk:sk + 1], ACT.Exp, bias=nm, scale=SCALE)
                            act.activation(probs[:, n % 4, 0:n_keys], PS[n % 2][:, 0:n_keys], ACT.Exp, bias=nm,
                                           scale=SCALE, accum_out=tiny[:, t8 + 4:t8 + 5]).then_inc(exp_done, 1)
                        else:
                            if sk is not None:
                                act.activation(tiny[:, t8 + 6:t8 + 7], sink8[:, sk:sk + 1], ACT.Exp, bias=nm, scale=SCALE)
                            act.activation(probs[:, n % 4, NC_:NT], probs[:, n % 4, NC_:NT], ACT.Exp, bias=nm,
                                           scale=SCALE, accum_out=tiny[:, t8 + 4:t8 + 5])
                            act.activation(probs[:, n % 4, 0:NC_], PS[n % 2][:, 0:NC_], ACT.Exp, bias=nm,
                                           scale=SCALE, accum_out=tiny[:, t8 + 5:t8 + 6]).then_inc(exp_done, 1)

                    def evacuate(u):
                        act.wait_ge(pt_mm, b * N_UNITS + u + 1 + N_UNITS)
                        act.wait_ge(o_mm, b * N_UNITS + u + 1)
                        act.activation(probs_t[:, u % 2, 0:n_keys], PS[2][:, 0:n_keys], ACT.Copy).then_inc(pt_ev, 1)

                    for n in range(N_MAPS + 2):
                        if n < N_MAPS:
                            exps(n)
                        if n - 2 in LAST_MAP:
                            evacuate(LAST_MAP.index(n - 2))
                    act.wait_ge(o_ev, b * N_UNITS + 8 + 2)
                    for h in range(4):
                        chain.done(act.activation(junk[:, :], o_tok[:, 256 + 128 * h:384 + 128 * h], ACT.Square,
                                                  accum_out=ssq[:, h:h + 1]))
                    act.activation(rms4, ssq, ACT.Sqrt, bias=eps_col, scale=1.0 / 128).then_inc(sub_rms, 1)
                    act.wait_ge(ot_mm, b + 2)
                    act.activation(o_fm[:, :, bass.ds(turn * 128 + first, 128)],
                                   PS[2][:, :].rearrange("p (k t) -> p k t", k=KD), ACT.Copy).then_inc(ot_ev, 1)
                chain.leave(trips)

            def upper_weights(L, n, i=0):
                slot = L * LAYER_SLOTS + MERGE0 + n // 2
                if n % 2 == 0:
                    act.wait_ge(slot_loaded[slot % RING], (i + slot // RING + 1) * 16)
                act.wait_ge(prod_mm, units(L, n + 1 - W_BUFS) + i * 18)
                act.activation(w_hi_r[:, n % W_BUFS, :], ring[:, slot % RING, 1024 * (n % 2):1024 * (n % 2) + 1024],
                               ACT.Copy).then_inc(w_hi_done, 1)

            def upper(dst, src, k, lo):
                act.activation(dst[:, k, lo:NT], src[:, k, lo:NT], ACT.Copy).then_inc(hi_done, 1)

            def merge_block(L, j, i=0):
                lo = NC_ if L == DEPTH - 1 else 0
                for u in range(4):
                    upper_weights(L, 4 * j + u + 2, i)
                    if u == 0:
                        act.wait_ge(y_done[L], 3 * i + j + 1)
                    if u < 3:
                        act.wait_ge(prod_mm, products(L, 6 * j + u + 1) + i * 18)
                        act.activation(gate[:, u, lo:NT], PS[u][:, 0:NT - lo], ACT.Sigmoid).then_inc(gate_ev[L], 1)

            act.sem_inc(exp_done, 2)
            act.sem_inc(pt_ev, 1)
            act.sem_inc(ot_ev, 1)
            act.sem_inc(d_ev, 1)
            act.wait_ge(consts_in, 16)
            act.wait_ge(consts_set, 1)
            for L in range(DEPTH):
                last = L == DEPTH - 1
                ctx_too = not last
                nb0 = 2 if last else 0
                act.wait_ge(c_zeroed[L], 1)
                act.activation(c_pad[:, :, 0:2], glob[:, O_C:O_C + 16].rearrange("p (k v) -> p k v", v=2),
                               ACT.Silu).then_inc(c_ready[L], 1)

                def x_ready_1():
                    if L:
                        x_final(act, L - 1)
                    else:
                        act.wait_ge(x_in_s, 16)

                norm(2 * L, False, x_ready_1, lambda k, v: amp[:, 0, k, v:v + 1], lambda k, v: mod[:, k, v:v + 1], h_fm)
                act.wait_ge(lam_in[L], 1)
                act.activation(tiny[:, 66:68], tiny[:, 66:68], ACT.Exp).then_inc(lam_exp[L], 1)
                act.wait_ge(rpb_out[L], 16)
                for j in range(N_Q + N_K):
                    act.wait_ge(slot_done, finished(L, QK0 + j // 2 + 1))
                    lo = NC_ if last and j < N_Q else 0
                    act.activation(qk[:, j, lo:NT], PS[j % 4][:, 0:NT - lo], ACT.Copy).then_inc(qk_ev[L], 1)
                if L:
                    act.wait_ge(x_saved, 16)
                if ctx_too:
                    heads((L, "c"), 0, NC_ // 128, NC_)
                heads((L, "l"), NC_, NL // 128, NT)
                lo = NC_ if last else 0
                full = L * LAYER_SLOTS + MERGE0 + RING - 1
                act.wait_ge(slot_loaded[full % RING], (full // RING + 1) * 16)
                upper_weights(L, 0)
                act.wait_ge(ot_ev, BLOCKS_BEFORE[L, "l"] + NL // 128 + 1)
                for k in range(KD):
                    upper(h_hi_r, h_fm, k, lo)
                upper_weights(L, 1)
                for k in range(KD):
                    upper(o_hi_r, o_fm, k, lo)
                with act.Fori(0, 2) as i:
                    for j in range(3):
                        merge_block(L, j, i)
                for j in (6, 7):
                    merge_block(L, j)
                act.wait_ge(prod_mm, products(L, 6 * KD - 3))
                for k in range(KD):
                    act.wait_ge(y_done[L], k + 2)
                    upper(h_hi_r, y_fm, k, lo)
                for n in range(4 * KD + 2, 5 * KD):
                    upper_weights(L, n)

                def x_ready_2():
                    act.wait_ge(out_ev[L], KD)

                norm(2 * L + 1, last, x_ready_2, lambda k, v: amp[:, 1, k, v:v + 1],
                     lambda k, v: mod[:, 24 + k, v:v + 1], h2_fm)
                lo = NC_ if last else 0
                act.wait_ge(lg_mm[L], 1)
                act.activation(logit_e[0:NE, lo:NT], PS[0][0:NE, 0:NT - lo], ACT.Copy).then_inc(lg_ev[L], 1)
                act.wait_ge(ex_in[L], 1)
                act.activation(ex_t[:, nb0:6, :], ex_t[:, nb0:6, :], ACT.Exp).then_inc(ex_out[L], 1)
                for n, nb in enumerate(range(nb0, 6)):
                    act.wait_ge(ht_mm[L], n + 1)
                    act.activation(h_tok[:, nb, :], PS[n % 2][:, :], ACT.Copy).then_inc(ht_ev[L], 1)
                wide = NT if ctx_too else NL
                def gathered(p):
                    act.wait_ge(gat_mm, L * ROUNDS + p + 1)
                    act.activation(xs.rearrange("p k s -> p (k s)"), PS[2][:, :], ACT.Copy).then_inc(gat_ev, 1)

                def gathered_context(p):
                    act.wait_ge(gatc_mm, p + 1)
                    act.activation(xsc.rearrange("p k s -> p (k s)"), PS[0][:, :], ACT.Copy).then_inc(gatc_ev, 1)

                gathered(0)
                if ctx_too:
                    gathered_context(0)
                with act.Fori(0, NE // 4) as turn:
                    i = turn + L * (NE // 4)
                    for pair in range(2):
                        pr = i * 2 + pair
                        base = finished(L, MOE0 + 24 * pair)
                        for par in range(2):
                            act.wait_ge(slot_done, turn * 48 + base + 8 * par + 4)
                            act.activation(silu[:, par, 0:wide], PS[0][:, 0:wide], ACT.Silu).then_inc(g_ev, 1)
                        gathered(turn * 2 + pair + 1)
                        if ctx_too and pair == 1:
                            gathered_context(turn + 1)
                        for par in range(2):
                            act.wait_ge(hidt_mm, pr * 2 + par + 1)
                            act.activation(hid_t[:, par, 0:wide], PS[3][:, 0:wide], ACT.Copy).then_inc(hidt_ev, 1)
                            act.wait_ge(slot_done, turn * 48 + base + 16 + 4 * par + 4)
                            for half in range(2):
                                ins = act.activation(y_pair[64 * par:64 * par + 64, 512 * half:512 * half + 512],
                                                     PS[0 if par else 2][64 * half:64 * half + 64, 0:512], ACT.Copy)
                            ins.then_inc(d_ev, 1)

            def x_ready_f():
                x_final(act, DEPTH - 1)

            norm(NORMS - 1, True, x_ready_f, lambda k, v: glob[:, O_FG + k:O_FG + k + 1], lambda k, v: zero_col, h_fm)

        @block.vector
        def _(dve):
            chain = Chain(dve, dve_chain)
            done = chain.done

            def norm(n, last, x_ready):
                lo = NC_ if last else 0
                x_ready()
                dve.wait_ge(rms_done, n + 1)
                if n % 2 == 0 and n < NORMS - 1:
                    modulation(n // 2)
                done(dve.reciprocal(rstd[:, lo:NT], rstd[:, lo:NT]))
                for k in range(KD):
                    if k >= 2:
                        dve.wait_ge(h_done, n * KD + k - 1)
                    dve.tensor_tensor(xr[:, k % 2, lo:NT], x_fm[:, k, lo:NT], rstd[:, lo:NT], ALU.mult
                                      ).then_inc(xr_done, 1)

            def modulation(L):
                dve.wait_ge(small_in_s[L], 16)
                for r in range(3):
                    dve.wait_ge(mod_tr[L], r + 1)
                    cols = PS[1][:, 0:512].rearrange("p (c g v) -> p g c v", c=4, g=4)[:, :, :, 0:2]
                    dst = mod[:, 16 * r:16 * r + 16, :].rearrange("p (g c) v -> p g c v", g=4)
                    b_mod = small[:, O_BMOD + 16 * r:O_BMOD + 16 * r + 16].rearrange("p (g c) -> p g c", g=4)
                    dve.tensor_tensor(dst, cols, b_mod.unsqueeze(3).broadcast_to((128, 4, 4, 2)), ALU.add
                                      ).then_inc(mod_done[L], 1)
                dve.wait_ge(mod_done[L], 3)
                for n, off in ((0, O_G1), (1, O_G2)):
                    g = small[:, off:off + KD].unsqueeze(2).broadcast_to((128, KD, 2))
                    ins = dve.scalar_tensor_tensor(out=amp[:, n, :, :], in0=mod[:, 8 + 24 * n:16 + 24 * n, :],
                                                   scalar=1.0, in1=g, op0=ALU.add, op1=ALU.mult)
                    if n == 0:
                        done(ins)
                ins.then_inc(mod_done[L], 1)

            def lambdas(L):
                init = 0.8 - 0.6 * math.exp(-0.3 * L)
                for n, dst in enumerate((lam_a, lam_b)):
                    a = small[:, O_LAM + 128 * n:O_LAM + 128 * n + 64]
                    b = small[:, O_LAM + 128 * n + 64:O_LAM + 128 * n + 128]
                    done(dve.tensor_tensor(lam_t, a, b, ALU.mult))
                    done(dve.tensor_reduce(dst, lam_t, AX, ALU.add))
                dve.tensor_scalar(sink8, small[:, O_SINK:O_SINK + 4], 1.0 / SCALE, None, ALU.mult)
                g = small[:, O_SUBG:O_SUBG + 128]
                dve.tensor_scalar(g, g, 1.0 - init, None, ALU.mult).then_inc(lam_in[L], 1)
                dve.wait_ge(lam_exp[L], 1)
                dve.tensor_scalar(neg_lam, lam_b, lam_a, -init, ALU.subtract, ALU.add).then_inc(bias_done[L], 1)

            def heads(key, trips, n_keys):
                L = key[0]
                latent = key[1] == "l"
                steps = 0
                for kind, *_ in UNITS:
                    steps += {"na": 4 if latent else 2, "diff": 5, "swa": 5 if latent else 4}[kind]
                with dve.Fori(0, trips) as turn:
                    b = turn + BLOCKS_BEFORE[key]
                    chain.enter(turn, steps + 1)

                    def maxima(n):
                        kind, qb, kb, vc, oc, br, sk = UNITS[MAPS[n][0]]
                        t8 = 8 * (n % 8)
                        mx0, mx1, nm = (tiny[:, t8 + c:t8 + c + 1] for c in (0, 1, 3))
                        dve.wait_ge(s_mm, b * N_MAPS + n + 3)
                        if kind == "diff" or not latent:
                            done(dve.tensor_reduce(mx0, PS[n % 2][:, 0:n_keys], AX, ALU.max))
                        else:
                            before = MAPS[(n - 4) % N_MAPS][0] + 1 + (N_UNITS if n >= 4 else 0)
                            dve.wait_ge(pt_mm, b * N_UNITS + before)
                            shifted = bias[:, br, bass.ds(384 - turn * 128, NL)]
                            done(dve.tensor_tensor(probs[:, n % 4, NC_:NT], PS[n % 2][:, NC_:NT], shifted, ALU.add))
                            dve.tensor_reduce(mx1, PS[n % 2][:, 0:NC_], AX, ALU.max)
                            done(dve.tensor_reduce(mx0, probs[:, n % 4, NC_:NT], AX, ALU.max))
                        both = mx1 if (kind != "diff" and latent) else mx0
                        if sk is not None:
                            done(dve.tensor_scalar(mx0, mx0, both, sink8[:, sk:sk + 1], ALU.max, ALU.max))
                            dve.tensor_scalar(nm, mx0, -SCALE, None, ALU.mult).then_inc(max_done, 1)
                        else:
                            dve.tensor_scalar(nm, mx0, both, -SCALE, ALU.max, ALU.mult).then_inc(max_done, 1)

                    def mix(u):
                        n = FIRST_MAP[u]
                        dve.wait_ge(exp_done, b * N_MAPS + n + 4)
                        s0 = tiny[:, 8 * (n % 8) + 4:8 * (n % 8) + 5]
                        s1 = tiny[:, 8 * ((n + 1) % 8) + 4:8 * ((n + 1) % 8) + 5]
                        r1 = tiny[:, 8 * ((n + 1) % 8) + 5:8 * ((n + 1) % 8) + 6]
                        coef = tiny[:, 8 * ((n + 1) % 8) + 6:8 * ((n + 1) % 8) + 7]
                        done(dve.reciprocal(r1, s1))
                        done(dve.tensor_scalar(coef, r1, s0, neg_lam, ALU.mult, ALU.mult))
                        dve.scalar_tensor_tensor(out=probs[:, n % 4, 0:n_keys], in0=probs[:, (n + 1) % 4, 0:n_keys],
                                                 scalar=coef, in1=probs[:, n % 4, 0:n_keys], op0=ALU.mult, op1=ALU.add
                                                 ).then_inc(mix_done, 1)

                    def outputs(u):
                        kind, qb, kb, vc, oc, br, sk = UNITS[u]
                        w = 128 if kind == "diff" else 64
                        t8 = 8 * (FIRST_MAP[u] % 8)
                        s0, s1, s2, rs = (tiny[:, t8 + c:t8 + c + 1] for c in (4, 5, 6, 7))
                        dve.wait_ge(o_mm, b * N_UNITS + u + 3)
                        if u == 0:
                            dve.wait_ge(ot_mm, b + 1)
                        if kind == "diff":
                            done(dve.reciprocal(rs, s0))
                        else:
                            if latent and sk is not None:
                                done(dve.tensor_scalar(s0, s0, s1, s2, ALU.add, ALU.add))
                            elif latent:
                                done(dve.tensor_scalar(s0, s0, s1, None, ALU.add))
                            elif sk is not None:
                                done(dve.tensor_scalar(s0, s0, s2, None, ALU.add))
                            done(dve.reciprocal(rs, s0))
                        dve.tensor_scalar(o_tok[:, oc:oc + w], PS[3][:, 512 * (u % 2):512 * (u % 2) + w], rs, None, ALU.mult
                                          ).then_inc(o_ev, 1)

                    for n in range(N_MAPS + 4):
                        if n < N_MAPS:
                            maxima(n)
                        if n - 1 in LAST_MAP and UNITS[LAST_MAP.index(n - 1)][0] == "diff":
                            mix(LAST_MAP.index(n - 1))
                        if n - 4 in LAST_MAP:
                            outputs(LAST_MAP.index(n - 4))
                    dve.wait_ge(sub_rms, b + 1)
                    done(dve.reciprocal(rr4, rms4))
                    dve.wait_ge(o_ev, b * N_UNITS + N_UNITS + 2)
                    for h in range(4):
                        o = o_tok[:, 256 + 128 * h:384 + 128 * h]
                        ins = dve.scalar_tensor_tensor(out=o, in0=o, scalar=rr4[:, h:h + 1],
                                                       in1=small[:, O_SUBG:O_SUBG + 128], op0=ALU.mult, op1=ALU.mult)
                    ins.then_inc(o_norm, 1)
                    if chain.count - chain.start != chain.step:
                        raise AssertionError((key, chain.count - chain.start, chain.step))
                chain.leave(trips)

            def merge_block(L, j, finish):
                lo = NC_ if L == DEPTH - 1 else 0
                for br in range(3):
                    dve.wait_ge(prod_mm, finish + br)
                    dve.tensor_tensor(gate[:, br, lo:NT], gate[:, br, lo:NT], PS[br][:, 0:NT - lo], ALU.mult
                                      ).then_inc(br_ev[L], 1)
                dve.wait_ge(br_ev[L], 3 * j + 6)
                done(dve.tensor_tensor(gate[:, 0, lo:NT], gate[:, 0, lo:NT], gate[:, 1, lo:NT], ALU.add))
                dst = y_fm[:, bass.ds(j, 1), lo:NT]
                dve.tensor_tensor(dst, gate[:, 0:1, lo:NT], gate[:, 2:3, lo:NT], ALU.add).then_inc(y_done[L], 1)

            def lower(n, dst, src, rounded, k, lo):
                dve.wait_ge(hi_done, n * KD + k + 1)
                dve.tensor_tensor(dst[:, k, lo:NT], src[:, k, lo:NT], rounded[:, k, lo:NT], ALU.subtract
                                  ).then_inc(lo_done, 1)

            dve.sem_inc(o_ev, 2)
            dve.sem_inc(cb_ev, 4)
            dve.sem_inc(cbc_ev, 2)
            dve.sem_inc(dc_ev, 1)
            dve.memset(ones[:, :], 1.0)
            dve.memset(q_pad[:, :, :], 0.0)
            dve.memset(zero_col, 0.0)
            dve.memset(eps_col, EPS).then_inc(consts_set, 1)
            dve.wait_ge(consts_in, 16)
            for L in range(DEPTH):
                last = L == DEPTH - 1
                ctx_too = not last
                nb0 = 2 if last else 0
                lo = NC_ if last else 0
                if L:
                    x_final(dve, L - 1)
                dve.memset(c_pad, 0.0).then_inc(c_zeroed[L], 1)

                def x_ready_1():
                    if L == 0:
                        dve.wait_ge(x_in_s, 16)

                norm(2 * L, False, x_ready_1)
                lambdas(L)
                dve.wait_ge(rope_in_s[L], 16)
                for n, j in enumerate(ROPE_BLOCKS):
                    dve.wait_ge(qk_ev[L], j + 1)
                    if n:
                        dve.wait_ge(rope_done[L], n)
                    v = qk[:, j, NC_:NT]
                    done(dve.stream_shuffle(rot, v, [(c + 16) % 32 for c in range(32)]))
                    dve.tensor_tensor(v, v, rope[:, 0, :], ALU.mult)
                    done(dve.tensor_tensor(rot, rot, rope[:, 1, :], ALU.mult))
                    dve.tensor_tensor(v, v, rot, ALU.add).then_inc(rope_done[L], 1)
                for nb in range(NT // 128):
                    if nb < NT // 128 - 1:
                        dve.wait_ge(v_mm[L], nb + 1)
                    else:
                        dve.wait_ge(slot_done, finished(L, V0 + V_SLOTS))
                    dve.tensor_copy(v_tok[:, nb, :].rearrange("p (c n) -> p c n", c=2),
                                    PS[nb % 4][:, :].rearrange("p (c n) -> p c n", c=2)[:, :, 0:448]).then_inc(v_ev[L], 1)
                dve.wait_ge(bias_in[L], 16 * 10)
                table = bias[:, 0:4, :].rearrange("p h (r c) -> p (h r) c", c=GRID_W)
                done(dve.scalar_tensor_tensor(out=table, in0=table, scalar=1.0 / SCALE,
                                              in1=col_mask.unsqueeze(1).broadcast_to((128, 56, GRID_W)),
                                              op0=ALU.mult, op1=ALU.add))
                if ctx_too:
                    heads((L, "c"), NC_ // 128, NC_)
                heads((L, "l"), NL // 128, NT)
                dve.sem_inc(br_ev[L], 3)
                dve.sem_inc(y_done[L], 1)
                for k in range(KD):
                    lower(3 * L, h_lo_r, h_fm, h_hi, k, lo)
                for k in range(KD):
                    lower(3 * L + 1, o_lo_r, o_fm, o_hi, k, lo)
                with dve.Fori(0, 2) as i:
                    chain.enter(i, 3)
                    for j in range(3):
                        merge_block(L, 3 * i + j, products(L, 6 * j + 4) + i * 18)
                chain.leave(2)
                for j in (6, 7):
                    merge_block(L, j, products(L, 6 * j + 4))
                for k in range(KD):
                    lower(3 * L + 2, h_lo_r, y_fm, h_hi, k, lo)
                dve.wait_ge(x_back[L], 16)
                for j in range(KD):
                    dve.wait_ge(prod_mm, products(L, 6 * KD + j + 1))
                    for v, a, b, c in segments(last):
                        ins = dve.scalar_tensor_tensor(out=x_fm[:, j, a:b], in0=PS[j % 4][:, c:c + b - a],
                                                       scalar=mod[:, 16 + j, v:v + 1], in1=x_fm[:, j, a:b],
                                                       op0=ALU.mult, op1=ALU.add)
                    ins.then_inc(out_ev[L], 1)
                dve.wait_ge(out_ev[L], KD)
                norm(2 * L + 1, last, lambda: None)
                dve.wait_ge(lt_mm[L], 1)
                nb_n = 6 - nb0
                logits = PS[1][:, 0:96].rearrange("p (n e) -> p n e", e=NE)[:, nb0:6, :]
                done(dve.tensor_reduce(red_t[:, 0, nb0:6], logits, AX, ALU.max))
                dve.tensor_tensor(ex_t[:, nb0:6, :], logits, red_t[:, 0, nb0:6].unsqueeze(2).broadcast_to((128, nb_n, NE)),
                                  ALU.subtract).then_inc(ex_in[L], 1)
                dve.wait_ge(ex_out[L], 1)
                done(dve.tensor_reduce(red_t[:, 1, nb0:6], ex_t[:, nb0:6, :], AX, ALU.add))
                done(dve.reciprocal(red_t[:, 0, nb0:6], red_t[:, 1, nb0:6]))
                dve.tensor_tensor(aff_t[:, nb0:6, :], ex_t[:, nb0:6, :],
                                  red_t[:, 0, nb0:6].unsqueeze(2).broadcast_to((128, nb_n, NE)), ALU.mult
                                  ).then_inc(aff_done[L], 1)
                done(dve.memset(zero_e[0:NE, :], 0.0))
                dve.wait_ge(at_mm[L], 1)
                dve.tensor_copy(aff_e[0:NE, lo:NT], PS[2][0:NE, lo:NT])
                done(dve.tensor_copy(work_e[0:NE, lo:NT], PS[2][0:NE, lo:NT]))
                for v, a, b, c in segments(last):
                    work = work_e[0:NE, a:b]
                    for _ in range((CAP_C if v else CAP_L) // 8):
                        done(dve.max(best[0:NE, :], work))
                        done(dve.match_replace(work, best[0:NE, :], work, -1.0))
                done(dve.tensor_tensor(mask_e[0:NE, lo:NT], work_e[0:NE, lo:NT], aff_e[0:NE, lo:NT], ALU.not_equal))
                for v, a, b, c in segments(last):
                    done(dve.tensor_tensor_scan(pos_e[0:NE, a:b], mask_e[0:NE, a:b], zero_e[0:NE, a:b], 0.0,
                                                ALU.add, ALU.add))
                dve.tensor_tensor(pos_e[0:NE, lo:NT], pos_e[0:NE, lo:NT], mask_e[0:NE, lo:NT], ALU.mult
                                  ).then_inc(pos_done[L], 1)
                dve.wait_ge(pos_tr[L], 1)
                done(dve.memset(pos_t, 0.0))
                dve.tensor_copy(pos_t[:, nb0:6, 0:NE], PS[3][:, 0:96].rearrange("p (n e) -> p n e", e=NE)[:, nb0:6, :]
                                ).then_inc(router_done[L], 1)
                dve.wait_ge(router_done[L], 1)
                wide = NT if ctx_too else NL
                def pick(dst, pos, tokens, first, n_experts, cap):
                    shape = (128, tokens[1] - tokens[0], n_experts, cap)
                    at = pos[:, tokens[0]:tokens[1], bass.ds(first, n_experts)].unsqueeze(3).broadcast_to(shape)
                    slot = iota[:, 0:cap].unsqueeze(1).unsqueeze(1).broadcast_to(shape)
                    return dve.tensor_tensor(dst.rearrange("p n (e s) -> p n e s", s=cap), at, slot, ALU.is_equal)

                def weigh(dst, tokens, first, n_experts, cap):
                    shape = (128, tokens[1] - tokens[0], n_experts, cap)
                    aff = aff_t[:, tokens[0]:tokens[1], bass.ds(first, n_experts)].unsqueeze(3).broadcast_to(shape)
                    d4 = dst.rearrange("p n (e s) -> p n e s", s=cap)
                    return dve.tensor_tensor(d4, d4, aff, ALU.mult)

                def combined(p):
                    n = L * ROUNDS + p
                    for k in range(KD):
                        dve.wait_ge(cb_mm, n * KD + k + 1)
                        bank = PS[2 + (k % 4) // 2][:, 512 * (k % 2):512 * (k % 2) + 512]
                        dve.scalar_tensor_tensor(out=x_fm[:, k, NC_:NT], in0=bank, scalar=mod[:, 40 + k, 0:1],
                                                 in1=x_fm[:, k, NC_:NT], op0=ALU.mult, op1=ALU.add
                                                 ).then_inc(cb_ev, 1)

                def combined_context(p):
                    for c in range(4):
                        dve.wait_ge(cbc_mm, p * 4 + c + 1)
                        for k in (2 * c, 2 * c + 1):
                            at = 512 * (c % 2) + 256 * (k % 2)
                            ins = dve.scalar_tensor_tensor(out=x_fm[:, k, 0:NC_], in0=PS[3][:, at:at + 256],
                                                           scalar=mod[:, 40 + k, 1:2], in1=x_fm[:, k, 0:NC_],
                                                           op0=ALU.mult, op1=ALU.add)
                        ins.then_inc(cbc_ev, 1)

                pick(sel, pos_t, (2, 6), 0, 2, CAP_L).then_inc(sel_done, 1)
                if ctx_too:
                    pick(selc, pos_t, (0, 2), 0, 4, CAP_C).then_inc(selc_done, 1)
                dve.memset(y_pair, 0.0)
                dve.memset(y_ctx, 0.0)
                dve.memset(selw_t, 0.0)
                dve.memset(selcw_t, 0.0).then_inc(y_zeroed[L], 1)
                with dve.Fori(0, NE // 4) as turn:
                    i = turn + L * (NE // 4)
                    chain.enter(turn, 3 if ctx_too else 2)
                    for pair in range(2):
                        pr = i * 2 + pair
                        p = turn * 2 + pair
                        dve.wait_ge(st_mm, pr + 1)
                        if ctx_too and pair == 0:
                            done(pick(selcw, pos_t, (0, 2), turn * 4, 4, CAP_C))
                            weigh(selcw, (0, 2), turn * 4, 4, CAP_C)
                        done(pick(selw, pos_t, (2, 6), turn * 4 + 2 * pair, 2, CAP_L))
                        weigh(selw, (2, 6), turn * 4 + 2 * pair, 2, CAP_L).then_inc(selw_done, 1)
                        dve.wait_ge(gat_mm, L * ROUNDS + p + 1)
                        pick(sel, pos_t, (2, 6), turn * 4 + 2 * pair + 2, 2, CAP_L).then_inc(sel_done, 1)
                        if ctx_too and pair == 0:
                            dve.wait_ge(gatc_mm, turn + 1)
                            pick(selc, pos_t, (0, 2), turn * 4 + 4, 4, CAP_C).then_inc(selc_done, 1)
                        base = finished(L, MOE0 + 24 * pair)
                        for par in range(2):
                            dve.wait_ge(g_ev, pr * 2 + par + 1)
                            dve.wait_ge(slot_done, turn * 48 + base + 8 * par + 8)
                            dve.tensor_tensor(hid[:, par, 0:wide], silu[:, par, 0:wide], PS[1][:, 0:wide], ALU.mult
                                              ).then_inc(hid_done, 1)
                            if par == 0:
                                combined(p)
                                if ctx_too and pair == 0:
                                    combined_context(turn)
                        dve.wait_ge(st_mm, pr + 2)
                        if ctx_too and pair == 0:
                            dve.tensor_copy(selcw_t, PS[3][:, 512:768])
                        dve.tensor_copy(selw_t, PS[3][:, 0:512]).then_inc(st_ev, 1)
                        if ctx_too:
                            for par in range(2):
                                q = 2 * pair + par
                                dve.wait_ge(slot_done, turn * 48 + base + 16 + 4 * par + 4)
                                for g in range(4):
                                    ins = dve.tensor_copy(y_ctx[32 * q:32 * q + 32, 256 * g:256 * g + 256],
                                                          PS[0 if par else 2][32 * g:32 * g + 32, 512:768])
                                ins.then_inc(dc_ev, 1)
                chain.leave(NE // 4)
                combined(NE // 2)
                if ctx_too:
                    combined_context(NE // 4)
            x_final(dve, DEPTH - 1)
            norm(NORMS - 1, True, lambda: None)


def shape_tables():
    f = np.float32
    t = np.arange(NL)
    row, col = (t // GRID_W).astype(f), (t % GRID_W).astype(f)
    inv = (f(10000.0) ** (-np.arange(16, dtype=f) / f(16))).astype(f)
    ang = np.concatenate([np.outer(inv, row)] * 2 + [np.outer(inv, col)] * 2).astype(f)
    sign = np.where(np.arange(64) % 32 < 16, f(-1), f(1))[:, None]
    rope = np.stack([np.tile(np.cos(ang), (2, 1)), np.tile(np.sin(ang) * sign, (2, 1))], axis=1).astype(f)
    p = np.arange(128)[:, None]
    swa = np.where(np.abs(np.arange(896)[None, :] - 384 - p) <= 128, f(0), f(NEG))
    start = np.clip(p % GRID_W - 8, 0, GRID_W - 16)
    k = np.arange(GRID_W)[None, :]
    cols = np.where((k >= start) & (k < start + 16), f(0), f(NEG))
    return rope, np.concatenate([swa, cols], axis=1).astype(f)


def feature_blocks(w):
    k = w.shape[0] // 128
    return w.reshape(k, 128, -1, 128).transpose(2, 1, 0, 3).reshape(-1, 128, k * 128)


def layer_stream(l, a):
    w_in = a["w_in"][l]
    slots = []
    mod = a["w_mod"][l].reshape(KD, 128, 3, SLOT)
    slots += [mod[k, :, r, :] for r in range(3) for k in range(KD)]
    swa_order = [768 + 64 * h + c for h in (0, 2, 1, 3) for c in range(64)]
    q = np.concatenate([w_in[:, 0:768], w_in[:, swa_order]], axis=1)
    qk = feature_blocks(np.concatenate([q, w_in[:, 1024:1920]], axis=1))
    qk = np.concatenate([qk, np.zeros((1, 128, 1024), qk.dtype)])
    slots += [np.concatenate([qk[2 * s], qk[2 * s + 1]], axis=1) for s in range(QK_SLOTS)]
    v = w_in[:, 1920:2816].reshape(4, 2, 128, 896).transpose(0, 2, 1, 3).reshape(4, 128, 1792)
    slots += list(np.concatenate([v, np.zeros((4, 128, SLOT - 1792), v.dtype)], axis=2))
    gates = feature_blocks(w_in[:, 2816:])
    branch = feature_blocks(np.concatenate([a["w_branch_na"][l], a["w_branch_diff"][l], a["w_branch_swa"][l]]))
    for j in range(KD):
        slots.append(np.concatenate([gates[j], gates[8 + j]], axis=1))
        slots.append(np.concatenate([gates[16 + j], branch[j]], axis=1))
    wo = feature_blocks(a["w_out"][l])
    slots += [np.concatenate([wo[2 * s], wo[2 * s + 1]], axis=1) for s in range(OUT_SLOTS)]
    gate, up, down = (a[n][l].reshape(NE, 4, 2, 128, D).transpose(0, 1, 3, 2, 4).reshape(NE, 4, 128, SLOT)
                      for n in ("w_expert_gate", "w_expert_up", "w_expert_down"))
    for e in range(0, NE, 2):
        for w, n in ((gate, e), (up, e), (gate, e + 1), (up, e + 1), (down, e), (down, e + 1)):
            slots += list(w[n])
    return slots


def columns(v):
    return v.reshape(-1, 128).T


def kernel(**inputs):
    import concourse.bacc as bacc
    from concourse.bass_utils import run_bass_kernel_spmd as run

    a = {k: np.asarray(v) for k, v in inputs.items()}
    f = a["x"].dtype
    stream = np.stack([s for l in range(DEPTH) for s in layer_stream(l, a)])
    assert stream.shape[0] == TOTAL_SLOTS, stream.shape
    tokens = np.concatenate([a["ctx"][0], a["x"][0]])
    x_fm = tokens.T.reshape(KD, 128, NT).transpose(1, 0, 2)

    def rep(v):
        return np.broadcast_to(v.reshape(1, -1), (128, v.size))

    small = np.stack([np.concatenate([
        columns(a["b_mod"][l]), columns(a["norm1_g"][l]), columns(a["norm2_g"][l]), rep(a["diff_subln_g"][l]),
        rep(a["diff_lambda"][l]), rep(a["swa_sink"][l]),
        a["w_router"][l].reshape(KD, 128, NE).transpose(1, 0, 2).reshape(128, KD * NE)], axis=1) for l in range(DEPTH)])
    c2 = np.stack([columns(a["c"][0]), columns(a["c_ctx"])], axis=2).reshape(128, 16)
    glob = np.concatenate([c2, columns(a["final_g"]), np.eye(128, dtype=f), rep(np.arange(1, 65, dtype=f))], axis=1)
    rope, mask = shape_tables()
    arrays = {"stream": stream, "x_in": x_fm, "small_in": small, "global_in": glob, "rope_in": rope,
              "mask_in": mask, "rpb_in": a["na_rpb"].reshape(DEPTH, 60, 31)}
    arrays = {k: np.ascontiguousarray(v) for k, v in arrays.items()}
    nc = bacc.Bacc("TRN2", target_bir_lowering=False, num_devices=1)
    args = [nc.dram_tensor(k, v.shape, mybir.dt.from_np(v.dtype), kind="ExternalInput").ap()
            for k, v in arrays.items()]
    out = nc.dram_tensor("out_fm", (128, KD, NL), mybir.dt.float32, kind="ExternalOutput").ap()
    build(nc, *args, out)
    r = run(nc, [arrays], core_ids=[0])
    y = r.results[0]["out_fm"]
    return np.ascontiguousarray(y.transpose(2, 1, 0).reshape(1, NL, D))
```

```python
import math
from contextlib import ExitStack

import numpy as np

import concourse.bass as bass
from concourse import mybir

D = 1024
KD = D // 128
NC_, NL = 256, 512
NT = NC_ + NL
DEPTH = 2
GRID_W = 64
NE = 16
CAP_L, CAP_C = 2 * NL // NE, 2 * NC_ // NE
W_BUFS = 3
QKV_BUFS = 2
SLOT = 2048
RING = 6
NEG = -1.0e30
SCALE = 64 ** -0.5
EPS = 1e-6
FF_HALF = 512

V_HALF = 448
V_UNIT0 = 15
MERGE_UNIT0 = V_UNIT0 + 8
ATT_UNITS = MERGE_UNIT0 + 5 * KD
QKV_PRODUCTS = V_UNIT0 + 2 * (3 + NT // 128)
ATT_PRODUCTS = QKV_PRODUCTS + 7 * KD

MOD_SLOTS, QK_SLOTS, V_SLOTS, MERGE_SLOTS, OUT_SLOTS, MOE_SLOTS = 24, 8, 4, 16, 4, 12 * NE
QK0 = MOD_SLOTS
V0 = QK0 + QK_SLOTS
MERGE0 = V0 + V_SLOTS
OUT0 = MERGE0 + MERGE_SLOTS
MOE0 = OUT0 + OUT_SLOTS
LAYER_SLOTS = MOE0 + MOE_SLOTS
TOTAL_SLOTS = DEPTH * LAYER_SLOTS

O_BMOD, O_G1, O_G2, O_SUBG, O_LAM, O_SINK, O_WR = 0, 48, 56, 64, 192, 448, 452
SMALL = O_WR + 128
O_C, O_FG, O_ID, O_IOTA = 0, 16, 24, 152
GLOBAL = O_IOTA + 64

ARENA = 27072
AT_WQ = ARENA - 2 * QKV_BUFS * 1024
REGIONS = (("region_x", KD * NT), ("region_h", KD * NT), ("arena", ARENA))

N_Q, N_K = 8, 7
ROPE_BLOCKS = (2, 3, 4, 5, 6, 7, 10, 11, 12, 13, 14)
AHEAD = 2
N_UNITS, N_MAPS = 12, 16


def unit_list():
    units = []
    for h in range(4):
        units.append(("na", h // 2, 8 + h // 2, 64 * h, 64 * h, h, None))
    for h in range(4):
        units.append(("diff", 2 + h, 10 + h, 256 + 128 * h, 256 + 128 * h, None, None))
    for j in range(2):
        for kv in range(2):
            head = 2 * kv + j
            units.append(("swa", 6 + j, 14, 768 + 64 * kv, 768 + 64 * head, 4, head))
    return units


def build(nc, stream, x_in, small_in, global_in, rope_in, mask_in, rpb_in, out):
    f32, f32r = mybir.dt.float32, mybir.dt.float32r
    ALU = mybir.AluOpType
    ACT = mybir.ActivationFunctionType
    AX = mybir.AxisListType.X
    UNITS = unit_list()
    MAPS = [(u, half) for u in range(N_UNITS) for half in ((0, 1) if UNITS[u][0] == "diff" else (None,))]
    FIRST_MAP = [min(n for n, (v, _) in enumerate(MAPS) if v == u) for u in range(N_UNITS)]
    LAST_MAP = [max(n for n, (v, _) in enumerate(MAPS) if v == u) for u in range(N_UNITS)]
    ctx = ExitStack()
    with ctx:
        def sb(name, shape, dtype=f32, stack=ctx):
            return stack.enter_context(nc.sbuf_tensor(name, shape, dtype))

        def sem(name):
            return ctx.enter_context(nc.semaphore(name))

        def sems(name):
            return [sem(f"{name}{L}") for L in range(DEPTH)]

        ring = sb("ring", [128, RING, SLOT])
        small = sb("small", [128, SMALL])
        glob = sb("glob", [128, GLOBAL])
        ones = sb("ones", [128, 128])
        mod = sb("mod", [128, 48, 2])
        amp = sb("amp", [128, 2, KD, 2])
        tiny = sb("tiny", [128, 96])
        junk = sb("junk", [128, 128])
        q_pad = sb("q_pad", [128, 2, 128])
        with ExitStack() as place:
            region_x, region_h, arena = (sb(n, [128, w], f32, place) for n, w in REGIONS)
        with ExitStack() as place:
            sb("below_wq", [128, 2 * KD * NT + AT_WQ], f32, place)
            wq_hi_r = sb("wq_hi_r", [128, QKV_BUFS, 1024], f32r, place)
            wq_lo_r = sb("wq_lo_r", [128, QKV_BUFS, 1024], f32r, place)
        region_x_r, region_h_r = (sb(n + "_r", [128, w], f32r) for n, w in REGIONS[:2])
        merge_out = sb("merge_out", [128, KD + 3, NT])
        h_hi_r = sb("h_hi_r", [128, KD, NT], f32r)
        o_hi_r = sb("o_hi_r", [128, KD, NT], f32r)
        w_hi_r = sb("w_hi_r", [128, W_BUFS, 1024], f32r)
        w_lo_r = sb("w_lo_r", [128, W_BUFS, 1024], f32r)
        x_fm = region_x[:, :].rearrange("p (k t) -> p k t", k=KD)
        o_fm = x_fm
        h_fm = region_h[:, :].rearrange("p (k t) -> p k t", k=KD)
        h_tok = region_h[:, :].rearrange("p (n d) -> p n d", n=NT // 128)
        ident = glob[:, O_ID:O_ID + 128]
        iota = glob[:, O_IOTA:O_IOTA + 64]
        eps_col, neg_lam, lam_a, lam_b = (tiny[:, c:c + 1] for c in (64, 65, 66, 67))
        sink8, ssq, rms4, rr4, zero_col = tiny[:, 68:72], tiny[:, 72:76], tiny[:, 76:80], tiny[:, 80:84], tiny[:, 84:85]

        def carve(at, *dims):
            n = int(np.prod(dims))
            assert at + n <= ARENA, (at, n)
            flat = arena[:, at:at + n]
            if len(dims) == 2:
                flat = flat.rearrange("p (a b) -> p a b", a=dims[0])
            return flat, at + n

        qk, a_v = carve(0, N_Q + N_K, NT)
        v_tok, a_b = carve(a_v, NT // 128, 896)
        bias, a_p = carve(a_b, 5, 896)
        probs, a_t = carve(a_p, 4, NT)
        probs_t, a_o = carve(a_t, 2, NT)
        o_tok, _ = carve(a_o, D)
        rope, a1 = carve(a_p, 2, NL)
        rot, a1 = carve(a1, NL)
        col_mask, a1 = carve(a1, GRID_W)
        assert a1 <= AT_WQ
        sq, a1 = carve(0, 2, NT)
        rstd, a1 = carve(a1, NT)
        xr, a1 = carve(a1, 2, NT)
        c_pad, a1 = carve(a1, KD, 32)
        mod_row, a1 = carve(a1, 512)
        lam_t, _ = carve(a1, 64)
        rpb_pad = arena[0:60, a_v:a_v + 128]
        y_fm = merge_out[:, 0:KD, :]
        gate = merge_out[:, KD:KD + 3, :]
        h_hi, o_hi, w_hi, wq_hi = (r[:, :, :].bitcast(f32) for r in (h_hi_r, o_hi_r, w_hi_r, wq_hi_r))
        h_lo_r, o_lo_r = (r[:, :].rearrange("p (k t) -> p k t", k=KD) for r in (region_h_r, region_x_r))
        h_up_r = o_lo_r
        h_up, h_low = h_up_r.bitcast(f32), h_lo_r.bitcast(f32)
        h2_fm, a_e = carve(KD * NT, KD, NT)
        logit_e, a1 = carve(a_e, NT)
        aff_e, a1 = carve(a1, NT)
        work_e, a1 = carve(a1, NT)
        pos_e, a1 = carve(a1, NT)
        mask_e, a1 = carve(a1, NT)
        zero_e, a1 = carve(a1, NT)
        best, a1 = carve(a1, 8)
        ex_t, a1 = carve(a1, 6, NE)
        red_t, a1 = carve(a1, 2, 6)
        aff_t, a1 = carve(a1, 6, NE)
        pos_t, a_s = carve(a1, 6, NE + 4)
        sel, a1 = carve(a_s, 4, 128)
        selw, a1 = carve(a1, 4, 128)
        selc, a1 = carve(a1, 2, 128)
        selcw, a1 = carve(a1, 2, 128)
        selw_t, a1 = carve(a1, NL)
        selcw_t, a1 = carve(a1, NC_)
        xs, a1 = carve(a1, KD, 128)
        xsc, a1 = carve(a1, KD, 128)
        silu, a1 = carve(0, 2, NT)
        hid, a1 = carve(a1, 2, NT)
        hid_t, a1 = carve(a1, 2, NT)
        y_pair, a1 = carve(a1, D)
        y_ctx, a1 = carve(a1, D)

        PS = [ctx.enter_context(nc.psum_tensor(f"PS{i}", [128, 1024], f32)) for i in range(4)]
        rpb_scr = [nc.dram_tensor(f"rpb_scr{L}", (60, 64, 128), f32, kind="Internal").ap() for L in range(DEPTH)]
        x_scr = nc.dram_tensor("x_scr", (128, KD, NL), f32, kind="Internal").ap()

        slot_loaded, slot_done = [sem(f"slot_loaded{s}") for s in range(RING)], sem("slot_done")
        consts_in, x_in_s, x_saved, out_done = sem("consts_in"), sem("x_in_s"), sem("x_saved"), sem("out_done")
        pad_zeroed = sem("pad_zeroed")
        small_in_s, rpb_in_s, rpb_out, bias_in, rope_in_s, x_back = (
            sems("small_in"), sems("rpb_in"), sems("rpb_out"), sems("bias_in"), sems("rope_in"), sems("x_back"))
        c_zeroed, c_ready, mod_ev, mod_tr, mod_done = (
            sems("c_zeroed"), sems("c_ready"), sems("mod_ev"), sems("mod_tr"), sems("mod_done"))
        NORMS = 2 * DEPTH + 1
        sq_done, sum_done, total_mm, rms_done, xr_done, h_done = (
            sem("sq_done"), sem("sum_done"), sem("total_mm"), sem("rms_done"), sem("xr_done"), sem("h_done"))
        consts_set = sem("consts_set")
        lam_in, lam_exp = sems("lam_in"), sems("lam_exp")
        qk_ev, rope_done, v_ev, bias_done = sems("qk_ev"), sems("rope_done"), sems("v_ev"), sems("bias_done")
        h_whole = sem("h_whole")
        BLOCKS_BEFORE, n = {}, 0
        for L in range(DEPTH):
            for name, tokens in (("c", 0 if L == DEPTH - 1 else NC_), ("l", NL)):
                BLOCKS_BEFORE[L, name] = n
                n += tokens // 128
        q_staged, s_mm, max_done, exp_done, mix_done, pt_mm, pt_ev = (
            sem("q_staged"), sem("s_mm"), sem("max_done"), sem("exp_done"),
            sem("mix_done"), sem("pt_mm"), sem("pt_ev"))
        o_mm, o_ev, sub_rms, o_norm, ot_mm, ot_ev = (
            sem("o_mm"), sem("o_ev"), sem("sub_rms"), sem("o_norm"),
            sem("ot_mm"), sem("ot_ev"))
        gate_ev, br_ev, y_done, out_ev = sems("gate_ev"), sems("br_ev"), sems("y_done"), sems("out_ev")
        prod_mm, w_hi_done, w_lo_done, hi_done, lo_done = (
            sem("prod_mm"), sem("w_hi_done"), sem("w_lo_done"), sem("hi_done"), sem("lo_done"))
        lg_mm, lg_ev, lt_mm, ex_in, ex_out, aff_done, at_mm, pos_done, pos_tr, router_done = (
            sems("lg_mm"), sems("lg_ev"), sems("lt_mm"), sems("ex_in"), sems("ex_out"), sems("aff_done"),
            sems("at_mm"), sems("pos_done"), sems("pos_tr"), sems("router_done"))
        ht_mm, ht_ev = sems("ht_mm"), sems("ht_ev")
        sel_done, selc_done, gat_mm, gat_ev, gatc_mm, gatc_ev, st_mm, st_ev = (
            sem("sel_done"), sem("selc_done"), sem("gat_mm"), sem("gat_ev"), sem("gatc_mm"),
            sem("gatc_ev"), sem("st_mm"), sem("st_ev"))
        selw_done, y_zeroed = sem("selw_done"), sems("y_zeroed")
        g_ev, hid_done, hidt_mm, hidt_ev, d_ev, dc_ev, cb_mm, cb_ev, cbc_mm, cbc_ev = (
            sem("g_ev"), sem("hid_done"), sem("hidt_mm"), sem("hidt_ev"), sem("d_ev"), sem("dc_ev"),
            sem("cb_mm"), sem("cb_ev"), sem("cbc_mm"), sem("cbc_ev"))
        dve_chain, act_chain = sem("dve_chain"), sem("act_chain")

        ROUNDS, ROUNDS_C = NE // 2 + 1, NE // 4 + 1

        def products(L, n):
            return ATT_PRODUCTS * L + QKV_PRODUCTS + n

        def units(L, n):
            if n <= V_UNIT0:
                return ATT_PRODUCTS * L + n
            if n < MERGE_UNIT0:
                return ATT_PRODUCTS * L + n + (n >= V_UNIT0 + 4) * (NT // 128 - 1)
            m = n - MERGE_UNIT0
            return products(L, 6 * (m // 4) + m % 4 if m <= 4 * KD else 2 * KD + m)

        def unit_slot(L, n):
            t, half = ((QK0 + n // 2, n % 2) if n < V_UNIT0 else
                       (V0 + (n - V_UNIT0) // 2, (n - V_UNIT0) % 2) if n < MERGE_UNIT0 else
                       (MERGE0 + (n - MERGE_UNIT0) // 2, (n - MERGE_UNIT0) % 2))
            return L * LAYER_SLOTS + t, slice(1024 * half, 1024 * half + 1024)

        def split_to(n, early, late):
            return early[:, n % QKV_BUFS, :] if n < MERGE_UNIT0 else late[:, (n - MERGE_UNIT0) % W_BUFS, :]

        class Chain:

            def __init__(self, engine, s):
                self.engine, self.s, self.count, self.extra = engine, s, 0, 0

            def done(self, ins):
                self.count += 1
                ins.then_inc(self.s, 1)
                self.engine.wait_ge(self.s, self.count + self.extra)

            def enter(self, i, step):
                self.start, self.step, self.extra = self.count, step, i * step

            def leave(self, trips):
                assert self.count - self.start == self.step, (self.count - self.start, self.step)
                self.count, self.extra = self.start + self.step * trips, 0

        def finished(L, slots):
            return RING + L * LAYER_SLOTS + slots

        def pieces(last):
            return [(NC_, NT, 0)] if last else [(0, 512, 0), (512, NT, 512)]

        def segments(last):
            return [(0, NC_, NT, 0)] if last else [(1, 0, NC_, 0), (0, NC_, NT, NC_)]

        def x_final(engine, L):
            engine.wait_ge(cb_ev, 4 + (L + 1) * KD * ROUNDS)
            if L < DEPTH - 1:
                engine.wait_ge(cbc_ev, 2 + (L + 1) * 4 * ROUNDS_C)

        block = ctx.enter_context(nc.Block())

        @block.sync
        def _(sp):
            rows = stream.rearrange("s p n -> p s n")

            def load(t, s, rotation):
                sp.wait_ge(slot_done, rotation * RING + s + 1)
                sp.dma_start(ring[:, s:s + 1, :], rows[:, bass.ds(t, 1), :]).then_inc(slot_loaded[s], 16)

            with sp.Fori(0, TOTAL_SLOTS // RING) as i:
                for s in range(RING):
                    load(i * RING + s, s, i)
            for s in range(TOTAL_SLOTS % RING):
                load(TOTAL_SLOTS - TOTAL_SLOTS % RING + s, s, TOTAL_SLOTS // RING)
            sp.wait_ge(h_done, NORMS * KD)
            sp.dma_start(out, h_fm[:, :, NC_:NT]).then_inc(out_done, 16)
            sp.wait_ge(out_done, 16)

        @block.gpsimd
        def _(pool):
            pool.dma_start(glob[:, :], global_in).then_inc(consts_in, 16)
            pool.dma_start(x_fm, x_in).then_inc(x_in_s, 16)
            for L in range(DEPTH):
                last = L == DEPTH - 1
                if L:
                    x_final(pool, L - 1)
                    pool.dma_start(x_scr, x_fm[:, :, NC_:NT]).then_inc(x_saved, 16)
                pool.dma_start(small[:, :], small_in[L]).then_inc(small_in_s[L], 16)
                pool.memset(rpb_pad, 0.0).then_inc(pad_zeroed, 1)
                pool.wait_ge(pad_zeroed, L + 1)
                pool.dma_start(rpb_pad[:, 48:79], rpb_in[L]).then_inc(rpb_in_s[L], 16)
                pool.wait_ge(rpb_in_s[L], 16)

                def load_tables():
                    pool.dma_start(rope, rope_in).then_inc(rope_in_s[L], 16)
                    pool.dma_start(rpb_scr[L], rpb_pad.unsqueeze(1).broadcast_to((60, 64, 128))).then_inc(rpb_out[L], 16)
                    pool.dma_start(bias[:, 4, :], mask_in[:, 0:896]).then_inc(bias_in[L], 16)
                    pool.dma_start(col_mask, mask_in[:, 896:896 + GRID_W]).then_inc(bias_in[L], 16)

                def shifted_bias(h, half):
                    first = (15 * h + 1 - half) * 64 * 128 + GRID_W - 1
                    shifted = bass.AP(rpb_scr[L].tensor, first, [[127, 64], [64 * 128, 14], [1, 64]])
                    dst = bias[64 * half:64 * half + 64, h, :].rearrange("p (r c) -> p r c", c=64)
                    pool.dma_start(dst, shifted).then_inc(bias_in[L], 16)

                def stage_queries(key, first, trips):
                    with pool.Fori(0, trips) as turn:
                        b = turn + BLOCKS_BEFORE[key]
                        for n, (u, _) in enumerate(MAPS):
                            half = 64 * (n % 2)
                            pool.wait_ge(s_mm, b * N_MAPS + n + 1)
                            pool.tensor_copy(q_pad[half:half + 64, n % 2, :],
                                             qk[half:half + 64, UNITS[u][1], bass.ds(turn * 128 + first, 128)]
                                             ).then_inc(q_staged, 1)

                def lower_weights(n, i=0):
                    pool.wait_ge(w_hi_done, ATT_UNITS * L + n + 1 + i * 12)
                    slot, cols = unit_slot(L, n)
                    pool.tensor_tensor(split_to(n, wq_lo_r, w_lo_r), ring[:, slot % RING, cols],
                                       split_to(n, wq_hi, w_hi), ALU.subtract).then_inc(w_lo_done, 1)

                for n in range(MERGE_UNIT0):
                    lower_weights(n)
                    if n == 1:
                        load_tables()
                    if n == 5:
                        pool.wait_ge(rpb_out[L], 16)
                    if 5 <= n < 13:
                        shifted_bias((n - 5) // 2, (n - 5) % 2)
                pool.wait_ge(w_lo_done, ATT_UNITS * L + MERGE_UNIT0)
                pool.wait_ge(qk_ev[L], N_Q + N_K)
                pool.wait_ge(rope_done[L], len(ROPE_BLOCKS))
                if not last:
                    stage_queries((L, "c"), 0, NC_ // 128)
                stage_queries((L, "l"), NC_, NL // 128)

                with pool.Fori(0, 2) as i:
                    for n in range(12):
                        lower_weights(MERGE_UNIT0 + n, i)
                for n in range(24, 34):
                    lower_weights(MERGE_UNIT0 + n)
                pool.wait_ge(y_done[L], KD + 1)
                if L:
                    pool.wait_ge(x_saved, 16)
                if last:
                    pool.dma_start(x_fm[:, :, NC_:NT], x_scr).then_inc(x_back[L], 16)
                else:
                    pool.dma_start(x_fm, x_in).then_inc(x_back[L], 16)
                for n in range(34, 5 * KD):
                    lower_weights(MERGE_UNIT0 + n)

        @block.tensor
        def _(pe):
            def take(L, t, rotations=0):
                n = L * LAYER_SLOTS + t
                pe.wait_ge(slot_loaded[n % RING], (rotations + n // RING + 1) * 16)
                return ring[:, n % RING, :]

            def norm_total(n, last):
                pe.wait_ge(sum_done, (n + 1) * (KD - 1))
                for lo, hi, c in pieces(last):
                    m = pe.matmul(PS[2][:, c:c + hi - lo], ones[:, :], rstd[:, lo:hi], start=True, stop=True)
                m.then_inc(total_mm, 1)

            def heads(key, trips, n_keys):
                def block_of_queries(b, next_follows):
                    def scores(n):
                        unit = UNITS[MAPS[n % N_MAPS][0]]
                        pe.wait_ge(q_staged, b * N_MAPS + n + 1)
                        pe.wait_ge(exp_done, b * N_MAPS + n + 1)
                        for lo in range(0, n_keys, 512):
                            hi = min(lo + 512, n_keys)
                            m = pe.matmul(PS[n % 2][:, lo:hi], q_pad[:, n % 2, :], qk[:, unit[2], lo:hi],
                                          start=True, stop=True)
                        m.then_inc(s_mm, 1)

                    def transposes(u):
                        if UNITS[u][0] == "diff":
                            pe.wait_ge(mix_done, b * 4 + u - 4 + 1)
                        else:
                            pe.wait_ge(exp_done, b * N_MAPS + FIRST_MAP[u] + 3)
                        pe.wait_ge(pt_ev, b * N_UNITS + u + 1)
                        if u == 0:
                            pe.wait_ge(ot_ev, b + 1)
                        for kb in range(n_keys // 128):
                            m = pe.transpose(PS[2][:, 128 * kb:128 * kb + 128],
                                             probs[:, FIRST_MAP[u] % 4, 128 * kb:128 * kb + 128], ident)
                        m.then_inc(pt_mm, 1)

                    def values(u):
                        kind, qb, kb_, vc, oc, br, sk = UNITS[u]
                        w = 128 if kind == "diff" else 64
                        pe.wait_ge(pt_ev, b * N_UNITS + u + 2)
                        pe.wait_ge(o_ev, b * N_UNITS + u + 1)
                        for kb in range(n_keys // 128):
                            m = pe.matmul(PS[3][:, 512 * (u % 2):512 * (u % 2) + w],
                                          probs_t[:, u % 2, 128 * kb:128 * kb + 128], v_tok[:, kb, vc:vc + w],
                                          start=(kb == 0), stop=(kb == n_keys // 128 - 1))
                        m.then_inc(o_mm, 1)

                    for n in range(N_MAPS + 3):
                        if AHEAD - 1 <= n < N_MAPS - 1 or next_follows and N_MAPS - 1 <= n < N_MAPS - 1 + AHEAD:
                            scores(n + 1)
                        if n - 2 in LAST_MAP:
                            transposes(LAST_MAP.index(n - 2))
                        if n - 3 in LAST_MAP:
                            values(LAST_MAP.index(n - 3))
                    pe.wait_ge(o_norm, b + 1)
                    for k in range(KD):
                        m = pe.transpose(PS[2][:, 128 * k:128 * k + 128], o_tok[:, 128 * k:128 * k + 128], ident)
                    m.then_inc(ot_mm, 1)

                def first_scores(b):
                    for n in range(AHEAD):
                        pe.wait_ge(q_staged, b * N_MAPS + n + 1)
                        pe.wait_ge(exp_done, b * N_MAPS + n + 1)
                        for lo in range(0, n_keys, 512):
                            hi = min(lo + 512, n_keys)
                            m = pe.matmul(PS[n % 2][:, lo:hi], q_pad[:, n % 2, :], qk[:, UNITS[MAPS[n][0]][2], lo:hi],
                                          start=True, stop=True)
                        m.then_inc(s_mm, 1)

                first_scores(BLOCKS_BEFORE[key])
                with pe.Fori(0, trips - 1) as turn:
                    block_of_queries(turn + BLOCKS_BEFORE[key], True)
                block_of_queries(trips - 1 + BLOCKS_BEFORE[key], False)
                pe.wait_ge(ot_ev, BLOCKS_BEFORE[key] + trips + 1)

            def split_weights(L, n, i=0):
                pe.wait_ge(w_lo_done, ATT_UNITS * L + n + 1 + i * 12)
                slot, cols = unit_slot(L, n)
                if cols.start or n == V_UNIT0 - 1:
                    pe.sem_inc(slot_done, 1)
                return split_to(n, wq_hi_r, w_hi_r), split_to(n, wq_lo_r, w_lo_r)

            def split_product(tile, weights, hi, lo_, last, k0=0, kn=KD, arriving=None):
                w_h, w_l = weights
                for k in range(k0, k0 + kn):
                    if arriving is not None:
                        pe.wait_ge(lo_done, arriving + k + 1)
                    for lo, hi_t, c in pieces(last):
                        for w, v in ((w_h, hi), (w_h, lo_), (w_l, hi)):
                            m = pe.matmul(PS[tile][:, c:c + hi_t - lo], w[:, 128 * k:128 * k + 128], v[:, k, lo:hi_t],
                                          start=(k == k0 and w is w_h and v is hi),
                                          stop=(k == k0 + kn - 1 and w is w_l))
                m.then_inc(prod_mm, 1)

            def merge_block(L, j, i=0):
                last = L == DEPTH - 1
                block = 3 * i + j
                for br in range(3):
                    weights = split_weights(L, MERGE_UNIT0 + 4 * j + br, i)
                    pe.wait_ge(br_ev[L], 3 * block + br + 1)
                    split_product(br, weights, h_hi_r, h_lo_r, last,
                                  arriving=(4 * L + 1) * KD if j == 0 and br == 0 else None)
                weights = split_weights(L, MERGE_UNIT0 + 4 * j + 3, i)
                for br, (k0, kn) in enumerate(((0, 2), (2, 4), (6, 2))):
                    pe.wait_ge(gate_ev[L], 3 * block + br + 1)
                    split_product(br, weights, o_hi_r, o_lo_r, last, k0, kn,
                                  arriving=(4 * L + 2) * KD if j == 0 else None)

            def expert_up(L, turn, t, tile, lhs, lhs_c, ctx_too):
                passes = (0, 1) if ctx_too else (0,)
                for p in passes:
                    for s in range(4):
                        w = take(L, t + s, 8 * turn) if p == 0 else ring[:, (L * LAYER_SLOTS + t + s) % RING, :]
                        for kk in range(2):
                            k = 2 * s + kk
                            row = w[:, 1024 * kk:1024 * kk + 1024]
                            n_t, width, src, at = ((2, 512, lhs, 0), (4, 256, lhs_c, 512))[p]
                            for g in range(n_t):
                                m = pe.matmul(PS[tile][128 // n_t * g:128 // n_t * (g + 1), at:at + width],
                                              src(k), row[:, width * g:width * (g + 1)],
                                              start=(k == 0), stop=(k == KD - 1))
                        if p == passes[-1]:
                            m.then_inc(slot_done, 1)

            pe.sem_inc(slot_done, RING)
            pe.sem_inc(s_mm, 2)
            pe.sem_inc(pt_mm, N_UNITS)
            pe.sem_inc(o_mm, 2)
            pe.sem_inc(ot_mm, 1)
            pe.sem_inc(st_mm, 1)
            pe.wait_ge(consts_in, 16)
            pe.wait_ge(consts_set, 1)
            for L in range(DEPTH):
                last = L == DEPTH - 1
                ctx_too = not last
                pe.wait_ge(c_ready[L], 1)
                for r in range(3):
                    if r:
                        pe.wait_ge(mod_ev[L], r)
                    for k in range(KD):
                        w = take(L, KD * r + k)
                        for g in range(4):
                            m = pe.matmul(PS[0][32 * g:32 * g + 32, 0:512], c_pad[:, k, :], w[:, 512 * g:512 * g + 512],
                                          start=(k == 0), stop=(k == KD - 1))
                        m.then_inc(slot_done, 1)
                    pe.wait_ge(mod_ev[L], r + 1)
                    if r:
                        pe.wait_ge(mod_done[L], r)
                    for c in range(4):
                        m = pe.transpose(PS[1][:, 128 * c:128 * c + 128], mod_row[:, 128 * c:128 * c + 128], ident)
                    m.then_inc(mod_tr[L], 1)
                    if r == 0:
                        norm_total(2 * L, False)
                pe.wait_ge(mod_done[L], 3)
                for j in range(N_Q + N_K):
                    if j >= 4:
                        pe.wait_ge(qk_ev[L], j - 3)
                    split_product(j % 4, split_weights(L, j), h_up_r, h_lo_r, last and j < N_Q,
                                  arriving=4 * L * KD if j == 0 else None)
                for n in range(8):
                    w_h, w_l = split_weights(L, V_UNIT0 + n)
                    half = n // 4
                    for kk in range(2):
                        k = 2 * (n % 4) + kk
                        for nb in range(NT // 128):
                            if k == 0 and half == 0:
                                pe.wait_ge(qk_ev[L], 13 + nb // 2)
                            if k == 0 and half == 1 and nb >= 2:
                                pe.wait_ge(v_ev[L], nb - 1)
                            bank = (6 * half + nb) % 8
                            cols = slice(V_HALF * kk, V_HALF * kk + V_HALF)
                            tokens = slice(128 * nb, 128 * nb + 128)
                            for v, w in ((h_up_r, w_h), (h_lo_r, w_h), (h_up_r, w_l)):
                                m = pe.matmul(PS[bank // 2][:, 512 * (bank % 2):512 * (bank % 2) + V_HALF],
                                              v[:, k, tokens], w[:, cols],
                                              start=(k == 0 and v is h_up_r and w is w_h), stop=(k == KD - 1 and w is w_l))
                            if k == KD - 1:
                                m.then_inc(prod_mm, 1)
                    if n % 4 < 3:
                        m.then_inc(prod_mm, 1)
                pe.wait_ge(v_ev[L], 2 * (NT // 128))
                pe.wait_ge(rope_done[L], len(ROPE_BLOCKS))
                if ctx_too:
                    heads((L, "c"), NC_ // 128, NC_)
                heads((L, "l"), NL // 128, NT)
                with pe.Fori(0, 2) as i:
                    for j in range(3):
                        merge_block(L, j, i)
                for j in (6, 7):
                    merge_block(L, j)
                for j in range(KD):
                    weights = split_weights(L, MERGE_UNIT0 + 4 * KD + j)
                    if j < 3:
                        pe.wait_ge(br_ev[L], 3 * KD + j + 1)
                    elif j >= 4:
                        pe.wait_ge(out_ev[L], j - 3)
                    split_product(j % 4, weights, h_hi_r, h_lo_r, last,
                                  arriving=(4 * L + 3) * KD if j == 0 else None)
                pe.wait_ge(out_ev[L], KD)
                norm_total(2 * L + 1, last)
                nb0 = 2 if last else 0
                for k in range(KD):
                    pe.wait_ge(h_done, (2 * L + 1) * KD + k + 1)
                    for lo, hi, c in pieces(last):
                        m = pe.matmul(PS[0][0:NE, c:c + hi - lo], small[:, O_WR + NE * k:O_WR + NE * k + NE],
                                      h2_fm[:, k, lo:hi], start=(k == 0), stop=(k == KD - 1))
                m.then_inc(lg_mm[L], 1)
                pe.wait_ge(lg_ev[L], 1)
                for nb in range(nb0, 6):
                    m = pe.transpose(PS[1][:, NE * nb:NE * nb + NE], logit_e[0:NE, 128 * nb:128 * nb + 128],
                                     ident[0:NE, 0:NE])
                m.then_inc(lt_mm[L], 1)
                pe.wait_ge(aff_done[L], 1)
                for nb in range(nb0, 6):
                    m = pe.transpose(PS[2][0:NE, 128 * nb:128 * nb + 128], aff_t[:, nb, :], ident)
                m.then_inc(at_mm[L], 1)
                for n, nb in enumerate(range(nb0, 6)):
                    if n >= 2:
                        pe.wait_ge(ht_ev[L], n - 1)
                    for k in range(KD):
                        m = pe.transpose(PS[n % 2][:, 128 * k:128 * k + 128], h2_fm[:, k, 128 * nb:128 * nb + 128], ident)
                    m.then_inc(ht_mm[L], 1)
                pe.wait_ge(pos_done[L], 1)
                for nb in range(nb0, 6):
                    m = pe.transpose(PS[3][:, NE * nb:NE * nb + NE], pos_e[0:NE, 128 * nb:128 * nb + 128],
                                     ident[0:NE, 0:NE])
                m.then_inc(pos_tr[L], 1)
                pe.wait_ge(router_done[L], 1)
                pe.wait_ge(ht_ev[L], 6 - nb0)
                def gather(p):
                    pe.wait_ge(sel_done, L * ROUNDS + p + 1)
                    for k in range(KD):
                        for nb in range(4):
                            m = pe.matmul(PS[2][:, 128 * k:128 * k + 128], h_tok[:, 2 + nb, 128 * k:128 * k + 128],
                                          sel[:, nb, :], start=(nb == 0), stop=(nb == 3))
                    m.then_inc(gat_mm, 1)

                def gather_context(p):
                    pe.wait_ge(selc_done, p + 1)
                    for k in range(KD):
                        for nb in range(2):
                            m = pe.matmul(PS[0][:, 128 * k:128 * k + 128], h_tok[:, nb, 128 * k:128 * k + 128],
                                          selc[:, nb, :], start=(nb == 0), stop=(nb == 1))
                    m.then_inc(gatc_mm, 1)

                def combine(p):
                    n = L * ROUNDS + p
                    for k in range(KD):
                        pe.wait_ge(cb_ev, n * KD + k + 1)
                        bank = PS[2 + (k % 4) // 2][:, 512 * (k % 2):512 * (k % 2) + 512]
                        pe.matmul(bank, y_pair[:, 128 * k:128 * k + 128], selw_t, start=True, stop=True
                                  ).then_inc(cb_mm, 1)
                    pe.wait_ge(cb_ev, n * KD + KD + 4)

                def combine_context(p):
                    for c in range(4):
                        pe.wait_ge(cbc_ev, p * 4 + c + 1)
                        for k in (2 * c, 2 * c + 1):
                            at = 512 * (c % 2) + 256 * (k % 2)
                            m = pe.matmul(PS[3][:, at:at + 256], y_ctx[:, 128 * k:128 * k + 128], selcw_t,
                                          start=True, stop=True)
                        m.then_inc(cbc_mm, 1)
                    pe.wait_ge(cbc_ev, p * 4 + 4 + 2)

                gather(0)
                if ctx_too:
                    gather_context(0)
                    pe.wait_ge(gatc_ev, 1)
                pe.wait_ge(gat_ev, L * ROUNDS + 1)
                pe.wait_ge(y_zeroed[L], 1)
                with pe.Fori(0, NE // 4) as turn:
                    i = turn + L * (NE // 4)
                    for pair in range(2):
                        pr = i * 2 + pair
                        p = turn * 2 + pair
                        t = MOE0 + 24 * pair

                        def gate_up(par):
                            q = 2 * pair + par
                            e = i * 4 + q

                            def lhs(k):
                                return xs[:, k, 64 * par:64 * par + 64]

                            def lhs_c(k):
                                return xsc[:, k, 32 * q:32 * q + 32]

                            if par:
                                pe.wait_ge(g_ev, e)
                            expert_up(L, turn, t + 8 * par, 0, lhs, lhs_c, ctx_too)
                            if par:
                                pe.wait_ge(hid_done, e)
                            expert_up(L, turn, t + 8 * par + 4, 1, lhs, lhs_c, ctx_too)

                        def down(par):
                            q = 2 * pair + par
                            e = i * 4 + q
                            pe.wait_ge(hid_done, e + 1)
                            if par:
                                pe.wait_ge(hidt_ev, e)
                            else:
                                pe.wait_ge(st_ev, pr + 1)
                            for c in range(6 if ctx_too else 4):
                                m = pe.transpose(PS[3][:, 128 * c:128 * c + 128], hid[:, q % 2, 128 * c:128 * c + 128], ident)
                            m.then_inc(hidt_mm, 1)
                            if par:
                                pe.wait_ge(g_ev, e + 1)
                                if ctx_too and pair == 1:
                                    pe.wait_ge(gatc_ev, turn + 2)
                            else:
                                pe.wait_ge(gat_ev, L * ROUNDS + p + 2)
                            pe.wait_ge(hidt_ev, e + 1)

                            def lhs(k):
                                at = 128 * (k % 4) + 64 * (k // 4)
                                return hid_t[:, q % 2, at:at + 64]

                            def lhs_c(k):
                                at = 512 + 128 * (k % 2) + 32 * (k // 2)
                                return hid_t[:, q % 2, at:at + 32]

                            expert_up(L, turn, t + 16 + 4 * par, 0 if par else 2, lhs, lhs_c, ctx_too)

                        pe.wait_ge(d_ev, pr * 2 + 1)
                        if ctx_too:
                            pe.wait_ge(dc_ev, pr * 2 + 1)
                        gate_up(0)
                        combine(p)
                        if ctx_too and pair == 0:
                            combine_context(turn)
                        gate_up(1)
                        pe.wait_ge(selw_done, pr + 1)
                        for nb in range(4):
                            m = pe.transpose(PS[3][:, 128 * nb:128 * nb + 128], selw[:, nb, :], ident)
                        if ctx_too and pair == 0:
                            for nb in range(2):
                                m = pe.transpose(PS[3][:, 512 + 128 * nb:512 + 128 * nb + 128], selcw[:, nb, :], ident)
                        m.then_inc(st_mm, 1)
                        gather(p + 1)
                        if ctx_too and pair == 1:
                            pe.wait_ge(g_ev, i * 4 + 4)
                            gather_context(turn + 1)
                        down(0)
                        down(1)
                pe.wait_ge(d_ev, (L + 1) * NE + 1)
                if ctx_too:
                    pe.wait_ge(dc_ev, (L + 1) * NE + 1)
                combine(NE // 2)
                if ctx_too:
                    combine_context(NE // 4)
                x_final(pe, L)
            norm_total(NORMS - 1, True)

        @block.scalar
        def _(act):
            chain = Chain(act, act_chain)

            def upper_weights(L, n, i=0):
                slot, cols = unit_slot(L, n)
                if not cols.start:
                    act.wait_ge(slot_loaded[slot % RING], (i + slot // RING + 1) * 16)
                if n >= QKV_BUFS:
                    bufs = QKV_BUFS if n < MERGE_UNIT0 else W_BUFS
                    act.wait_ge(prod_mm, units(L, n + 1 - bufs) + i * 18)
                act.activation(split_to(n, wq_hi_r, w_hi_r), ring[:, slot % RING, cols], ACT.Copy).then_inc(w_hi_done, 1)

            def upper(dst, src, k, lo):
                act.activation(dst[:, k, lo:NT], src[:, k, lo:NT], ACT.Copy).then_inc(hi_done, 1)

            def square(n, k, lo):
                if k >= 2:
                    act.wait_ge(sum_done, n * (KD - 1) + max(1, k - 2))
                act.activation(sq[:, k % 2, lo:NT], x_fm[:, k, lo:NT], ACT.Square).then_inc(sq_done, 1)

            def norm(n, last, gains, shifts, dst):
                first = n % 2 == 0 and n < NORMS - 1
                lo = NC_ if last else 0
                if first:
                    modulation(n // 2, 0)
                act.wait_ge(total_mm, n + 1)
                act.activation(rstd[:, lo:NT], PS[2][:, 0:NT - lo], ACT.Sqrt, bias=eps_col, scale=1.0 / D
                               ).then_inc(rms_done, 1)
                if first:
                    modulation(n // 2, 1)
                    modulation(n // 2, 2)
                if n < NORMS - 1:
                    act.wait_ge(mod_done[n // 2], 4)
                if first:
                    if n:
                        act.wait_ge(x_saved, 16)
                    for unit in range(QKV_BUFS):
                        upper_weights(n // 2, unit)
                for k in range(KD):
                    act.wait_ge(xr_done, n * KD + k + 1)
                    for m_i, (v, a, b, c) in enumerate(segments(last)):
                        ins = act.activation(dst[:, k, a:b], xr[:, k % 2, a:b], ACT.Identity,
                                             bias=shifts(k, v), scale=gains(k, v))
                    ins.then_inc(h_done, 1)
                    if first:
                        act.wait_ge(h_done, n * KD + k + 1)
                        upper(h_up_r, h_fm, k, 0)

            def modulation(L, r):
                act.wait_ge(slot_done, finished(L, KD * (r + 1)))
                if r:
                    act.wait_ge(mod_tr[L], r)
                act.activation(mod_row, PS[0][:, 0:512], ACT.Copy).then_inc(mod_ev[L], 1)

            def heads(key, first, trips, n_keys):
                L = key[0]
                latent = key[1] == "l"

                def block_of_queries(turn, part):
                    b = turn + BLOCKS_BEFORE[key]

                    def exps(n):
                        kind, qb, kb, vc, oc, br, sk = UNITS[MAPS[n % N_MAPS][0]]
                        t8 = 8 * (n % 8)
                        nm = tiny[:, t8 + 3:t8 + 4]
                        act.wait_ge(max_done, b * N_MAPS + n + 1)
                        if kind == "diff" or not latent:
                            before = MAPS[(n - 4) % N_MAPS][0] + 1 + N_UNITS * ((n - 4) // N_MAPS + 1)
                            act.wait_ge(pt_mm, b * N_UNITS + before)
                            if sk is not None:
                                act.activation(tiny[:, t8 + 6:t8 + 7], sink8[:, sk:sk + 1], ACT.Exp, bias=nm, scale=SCALE)
                            act.activation(probs[:, n % 4, 0:n_keys], PS[n % 2][:, 0:n_keys], ACT.Exp, bias=nm,
                                           scale=SCALE, accum_out=tiny[:, t8 + 4:t8 + 5]).then_inc(exp_done, 1)
                        else:
                            if sk is not None:
                                act.activation(tiny[:, t8 + 6:t8 + 7], sink8[:, sk:sk + 1], ACT.Exp, bias=nm, scale=SCALE)
                            act.activation(probs[:, n % 4, NC_:NT], probs[:, n % 4, NC_:NT], ACT.Exp, bias=nm,
                                           scale=SCALE, accum_out=tiny[:, t8 + 4:t8 + 5])
                            act.activation(probs[:, n % 4, 0:NC_], PS[n % 2][:, 0:NC_], ACT.Exp, bias=nm,
                                           scale=SCALE, accum_out=tiny[:, t8 + 5:t8 + 6]).then_inc(exp_done, 1)

                    def evacuate(u):
                        act.wait_ge(pt_mm, b * N_UNITS + u + 1 + N_UNITS)
                        act.wait_ge(o_mm, b * N_UNITS + u + 1)
                        act.activation(probs_t[:, u % 2, 0:n_keys], PS[2][:, 0:n_keys], ACT.Copy).then_inc(pt_ev, 1)

                    if part == "first":
                        for n in range(AHEAD):
                            exps(n)
                        return
                    for n in range(N_MAPS + AHEAD):
                        if AHEAD <= n < N_MAPS or part == "middle" and n >= N_MAPS:
                            exps(n)
                        if n - 2 in LAST_MAP:
                            evacuate(LAST_MAP.index(n - 2))
                    act.wait_ge(o_ev, b * N_UNITS + 8 + 2)
                    for h in range(4):
                        chain.done(act.activation(junk[:, :], o_tok[:, 256 + 128 * h:384 + 128 * h], ACT.Square,
                                                  accum_out=ssq[:, h:h + 1]))
                    act.activation(rms4, ssq, ACT.Sqrt, bias=eps_col, scale=1.0 / 128).then_inc(sub_rms, 1)
                    act.wait_ge(ot_mm, b + 2)
                    act.activation(o_fm[:, :, bass.ds(turn * 128 + first, 128)],
                                   PS[2][:, :].rearrange("p (k t) -> p k t", k=KD), ACT.Copy).then_inc(ot_ev, 1)

                block_of_queries(0, "first")
                with act.Fori(0, trips - 1) as turn:
                    chain.enter(turn, 4)
                    block_of_queries(turn, "middle")
                chain.leave(trips - 1)
                block_of_queries(trips - 1, "last")

            def merge_block(L, j, i=0):
                lo = NC_ if L == DEPTH - 1 else 0
                for u in range(4):
                    upper_weights(L, MERGE_UNIT0 + 4 * j + u + 2, i)
                    if u == 0:
                        act.wait_ge(y_done[L], 3 * i + j + 1)
                    if u < 3:
                        act.wait_ge(prod_mm, products(L, 6 * j + u + 1) + i * 18)
                        act.activation(gate[:, u, lo:NT], PS[u][:, 0:NT - lo], ACT.Sigmoid).then_inc(gate_ev[L], 1)

            act.sem_inc(exp_done, 2)
            act.sem_inc(pt_ev, 1)
            act.sem_inc(ot_ev, 1)
            act.sem_inc(d_ev, 1)
            act.wait_ge(consts_in, 16)
            act.wait_ge(consts_set, 1)
            for L in range(DEPTH):
                last = L == DEPTH - 1
                ctx_too = not last
                nb0 = 2 if last else 0
                act.wait_ge(c_zeroed[L], 1)
                act.activation(c_pad[:, :, 0:2], glob[:, O_C:O_C + 16].rearrange("p (k v) -> p k v", v=2),
                               ACT.Silu).then_inc(c_ready[L], 1)

                if L:
                    x_final(act, L - 1)
                else:
                    act.wait_ge(x_in_s, 16)
                for k in range(KD):
                    square(2 * L, k, 0)
                norm(2 * L, False, lambda k, v: amp[:, 0, k, v:v + 1], lambda k, v: mod[:, k, v:v + 1], h_fm)
                act.wait_ge(lam_in[L], 1)
                act.activation(tiny[:, 66:68], tiny[:, 66:68], ACT.Exp).then_inc(lam_exp[L], 1)
                for j in range(N_Q + N_K):
                    upper_weights(L, j + QKV_BUFS)
                    lo = NC_ if last and j < N_Q else 0
                    act.activation(qk[:, j, lo:NT], PS[j % 4][:, 0:NT - lo], ACT.Copy).then_inc(qk_ev[L], 1)
                for n in range(N_Q + N_K + QKV_BUFS, MERGE_UNIT0):
                    upper_weights(L, n)
                act.wait_ge(h_whole, KD * (L + 1))
                if ctx_too:
                    heads((L, "c"), 0, NC_ // 128, NC_)
                heads((L, "l"), NC_, NL // 128, NT)
                lo = NC_ if last else 0
                upper_weights(L, MERGE_UNIT0)
                act.wait_ge(ot_ev, BLOCKS_BEFORE[L, "l"] + NL // 128 + 1)
                for k in range(KD):
                    upper(h_hi_r, h_fm, k, lo)
                upper_weights(L, MERGE_UNIT0 + 1)
                for k in range(KD):
                    upper(o_hi_r, o_fm, k, lo)
                with act.Fori(0, 2) as i:
                    for j in range(3):
                        merge_block(L, j, i)
                for j in (6, 7):
                    merge_block(L, j)
                act.wait_ge(prod_mm, products(L, 6 * KD - 3))
                for k in range(KD):
                    act.wait_ge(y_done[L], k + 2)
                    upper(h_hi_r, y_fm, k, lo)
                upper_weights(L, MERGE_UNIT0 + 4 * KD + 2)
                for k in range(KD):
                    if k < KD - 3:
                        upper_weights(L, MERGE_UNIT0 + 4 * KD + 3 + k)
                    act.wait_ge(out_ev[L], k + 1)
                    square(2 * L + 1, k, lo)
                norm(2 * L + 1, last, lambda k, v: amp[:, 1, k, v:v + 1],
                     lambda k, v: mod[:, 24 + k, v:v + 1], h2_fm)
                lo = NC_ if last else 0
                act.wait_ge(lg_mm[L], 1)
                act.activation(logit_e[0:NE, lo:NT], PS[0][0:NE, 0:NT - lo], ACT.Copy).then_inc(lg_ev[L], 1)
                act.wait_ge(ex_in[L], 1)
                act.activation(ex_t[:, nb0:6, :], ex_t[:, nb0:6, :], ACT.Exp).then_inc(ex_out[L], 1)
                for n, nb in enumerate(range(nb0, 6)):
                    act.wait_ge(ht_mm[L], n + 1)
                    act.activation(h_tok[:, nb, :], PS[n % 2][:, :], ACT.Copy).then_inc(ht_ev[L], 1)
                wide = NT if ctx_too else NL
                def gathered(p):
                    act.wait_ge(gat_mm, L * ROUNDS + p + 1)
                    act.activation(xs.rearrange("p k s -> p (k s)"), PS[2][:, :], ACT.Copy).then_inc(gat_ev, 1)

                def gathered_context(p):
                    act.wait_ge(gatc_mm, p + 1)
                    act.activation(xsc.rearrange("p k s -> p (k s)"), PS[0][:, :], ACT.Copy).then_inc(gatc_ev, 1)

                gathered(0)
                if ctx_too:
                    gathered_context(0)
                with act.Fori(0, NE // 4) as turn:
                    i = turn + L * (NE // 4)
                    for pair in range(2):
                        pr = i * 2 + pair
                        base = finished(L, MOE0 + 24 * pair)
                        for par in range(2):
                            act.wait_ge(slot_done, turn * 48 + base + 8 * par + 4)
                            act.activation(silu[:, par, 0:wide], PS[0][:, 0:wide], ACT.Silu).then_inc(g_ev, 1)
                        gathered(turn * 2 + pair + 1)
                        if ctx_too and pair == 1:
                            gathered_context(turn + 1)
                        for par in range(2):
                            act.wait_ge(hidt_mm, pr * 2 + par + 1)
                            act.activation(hid_t[:, par, 0:wide], PS[3][:, 0:wide], ACT.Copy).then_inc(hidt_ev, 1)
                            act.wait_ge(slot_done, turn * 48 + base + 16 + 4 * par + 4)
                            for half in range(2):
                                ins = act.activation(y_pair[64 * par:64 * par + 64, 512 * half:512 * half + 512],
                                                     PS[0 if par else 2][64 * half:64 * half + 64, 0:512], ACT.Copy)
                            ins.then_inc(d_ev, 1)

            x_final(act, DEPTH - 1)
            for k in range(KD):
                square(NORMS - 1, k, NC_)
            norm(NORMS - 1, True, lambda k, v: glob[:, O_FG + k:O_FG + k + 1], lambda k, v: zero_col, h_fm)

        @block.vector
        def _(dve):
            chain = Chain(dve, dve_chain)
            done = chain.done

            def lower(n, dst, src, rounded, k, lo):
                dve.wait_ge(hi_done, n * KD + k + 1)
                dve.tensor_tensor(dst[:, k, lo:NT], src[:, k, lo:NT], rounded[:, k, lo:NT], ALU.subtract
                                  ).then_inc(lo_done, 1)

            def add_square(n, k, lo):
                dve.wait_ge(sq_done, n * KD + k + 1)
                if k >= 2:
                    dve.wait_ge(sum_done, n * (KD - 1) + k - 1)
                before = sq[:, 0, lo:NT] if k == 1 else rstd[:, lo:NT]
                dve.tensor_tensor(rstd[:, lo:NT], before, sq[:, k % 2, lo:NT], ALU.add).then_inc(sum_done, 1)

            def norm(n, last):
                first = n % 2 == 0 and n < NORMS - 1
                lo = NC_ if last else 0
                if first:
                    modulation(n // 2, 0)
                dve.wait_ge(rms_done, n + 1)
                done(dve.reciprocal(rstd[:, lo:NT], rstd[:, lo:NT]))
                if first:
                    modulation(n // 2, 1)
                    modulation(n // 2, 2)
                for k in range(KD):
                    if k >= 2:
                        dve.wait_ge(h_done, n * KD + k - 1)
                    dve.tensor_tensor(xr[:, k % 2, lo:NT], x_fm[:, k, lo:NT], rstd[:, lo:NT], ALU.mult
                                      ).then_inc(xr_done, 1)
                    if first and k:
                        lower(2 * n, h_lo_r, h_fm, h_up, k - 1, 0)
                if first:
                    lower(2 * n, h_lo_r, h_fm, h_up, KD - 1, 0)

            def modulation(L, r):
                dve.wait_ge(small_in_s[L], 16)
                dve.wait_ge(mod_tr[L], r + 1)
                cols = PS[1][:, 0:512].rearrange("p (c g v) -> p g c v", c=4, g=4)[:, :, :, 0:2]
                dst = mod[:, 16 * r:16 * r + 16, :].rearrange("p (g c) v -> p g c v", g=4)
                b_mod = small[:, O_BMOD + 16 * r:O_BMOD + 16 * r + 16].rearrange("p (g c) -> p g c", g=4)
                dve.tensor_tensor(dst, cols, b_mod.unsqueeze(3).broadcast_to((128, 4, 4, 2)), ALU.add
                                  ).then_inc(mod_done[L], 1)
                if r < 2:
                    return
                dve.wait_ge(mod_done[L], 3)
                for n, off in ((0, O_G1), (1, O_G2)):
                    g = small[:, off:off + KD].unsqueeze(2).broadcast_to((128, KD, 2))
                    ins = dve.scalar_tensor_tensor(out=amp[:, n, :, :], in0=mod[:, 8 + 24 * n:16 + 24 * n, :],
                                                   scalar=1.0, in1=g, op0=ALU.add, op1=ALU.mult)
                    if n == 0:
                        done(ins)
                ins.then_inc(mod_done[L], 1)

            def lambdas(L):
                init = 0.8 - 0.6 * math.exp(-0.3 * L)
                for n, dst in enumerate((lam_a, lam_b)):
                    a = small[:, O_LAM + 128 * n:O_LAM + 128 * n + 64]
                    b = small[:, O_LAM + 128 * n + 64:O_LAM + 128 * n + 128]
                    done(dve.tensor_tensor(lam_t, a, b, ALU.mult))
                    done(dve.tensor_reduce(dst, lam_t, AX, ALU.add))
                dve.tensor_scalar(sink8, small[:, O_SINK:O_SINK + 4], 1.0 / SCALE, None, ALU.mult)
                g = small[:, O_SUBG:O_SUBG + 128]
                dve.tensor_scalar(g, g, 1.0 - init, None, ALU.mult).then_inc(lam_in[L], 1)
                dve.wait_ge(lam_exp[L], 1)
                dve.tensor_scalar(neg_lam, lam_b, lam_a, -init, ALU.subtract, ALU.add).then_inc(bias_done[L], 1)

            def heads(key, trips, n_keys):
                L = key[0]
                latent = key[1] == "l"
                steps = 0
                for kind, *_ in UNITS:
                    steps += {"na": 4 if latent else 2, "diff": 5, "swa": 5 if latent else 4}[kind]

                def block_of_queries(turn, part):
                    b = turn + BLOCKS_BEFORE[key]

                    def maxima(n):
                        kind, qb, kb, vc, oc, br, sk = UNITS[MAPS[n % N_MAPS][0]]
                        t8 = 8 * (n % 8)
                        mx0, mx1, nm = (tiny[:, t8 + c:t8 + c + 1] for c in (0, 1, 3))
                        dve.wait_ge(s_mm, b * N_MAPS + n + 3)
                        if kind == "diff" or not latent:
                            done(dve.tensor_reduce(mx0, PS[n % 2][:, 0:n_keys], AX, ALU.max))
                        else:
                            before = MAPS[(n - 4) % N_MAPS][0] + 1 + N_UNITS * ((n - 4) // N_MAPS + 1)
                            dve.wait_ge(pt_mm, b * N_UNITS + before)
                            shifted = bias[:, br, bass.ds(384 - (turn + n // N_MAPS) * 128, NL)]
                            done(dve.tensor_tensor(probs[:, n % 4, NC_:NT], PS[n % 2][:, NC_:NT], shifted, ALU.add))
                            dve.tensor_reduce(mx1, PS[n % 2][:, 0:NC_], AX, ALU.max)
                            done(dve.tensor_reduce(mx0, probs[:, n % 4, NC_:NT], AX, ALU.max))
                        both = mx1 if (kind != "diff" and latent) else mx0
                        if sk is not None:
                            done(dve.tensor_scalar(mx0, mx0, both, sink8[:, sk:sk + 1], ALU.max, ALU.max))
                            dve.tensor_scalar(nm, mx0, -SCALE, None, ALU.mult).then_inc(max_done, 1)
                        else:
                            dve.tensor_scalar(nm, mx0, both, -SCALE, ALU.max, ALU.mult).then_inc(max_done, 1)

                    def mix(u):
                        n = FIRST_MAP[u]
                        dve.wait_ge(exp_done, b * N_MAPS + n + 4)
                        s0 = tiny[:, 8 * (n % 8) + 4:8 * (n % 8) + 5]
                        s1 = tiny[:, 8 * ((n + 1) % 8) + 4:8 * ((n + 1) % 8) + 5]
                        r1 = tiny[:, 8 * ((n + 1) % 8) + 5:8 * ((n + 1) % 8) + 6]
                        coef = tiny[:, 8 * ((n + 1) % 8) + 6:8 * ((n + 1) % 8) + 7]
                        done(dve.reciprocal(r1, s1))
                        done(dve.tensor_scalar(coef, r1, s0, neg_lam, ALU.mult, ALU.mult))
                        dve.scalar_tensor_tensor(out=probs[:, n % 4, 0:n_keys], in0=probs[:, (n + 1) % 4, 0:n_keys],
                                                 scalar=coef, in1=probs[:, n % 4, 0:n_keys], op0=ALU.mult, op1=ALU.add
                                                 ).then_inc(mix_done, 1)

                    def outputs(u):
                        kind, qb, kb, vc, oc, br, sk = UNITS[u]
                        w = 128 if kind == "diff" else 64
                        t8 = 8 * (FIRST_MAP[u] % 8)
                        s0, s1, s2, rs = (tiny[:, t8 + c:t8 + c + 1] for c in (4, 5, 6, 7))
                        dve.wait_ge(o_mm, b * N_UNITS + u + 3)
                        if u == 0:
                            dve.wait_ge(ot_mm, b + 1)
                        if kind == "diff":
                            done(dve.reciprocal(rs, s0))
                        else:
                            if latent and sk is not None:
                                done(dve.tensor_scalar(s0, s0, s1, s2, ALU.add, ALU.add))
                            elif latent:
                                done(dve.tensor_scalar(s0, s0, s1, None, ALU.add))
                            elif sk is not None:
                                done(dve.tensor_scalar(s0, s0, s2, None, ALU.add))
                            done(dve.reciprocal(rs, s0))
                        dve.tensor_scalar(o_tok[:, oc:oc + w], PS[3][:, 512 * (u % 2):512 * (u % 2) + w], rs, None, ALU.mult
                                          ).then_inc(o_ev, 1)

                    if part == "first":
                        for n in range(AHEAD):
                            maxima(n)
                        return
                    for n in range(N_MAPS + 4):
                        if AHEAD <= n < N_MAPS or part == "middle" and N_MAPS <= n < N_MAPS + AHEAD:
                            maxima(n)
                        if n - 1 in LAST_MAP and UNITS[LAST_MAP.index(n - 1)][0] == "diff":
                            mix(LAST_MAP.index(n - 1))
                        if n - 4 in LAST_MAP:
                            outputs(LAST_MAP.index(n - 4))
                    dve.wait_ge(sub_rms, b + 1)
                    done(dve.reciprocal(rr4, rms4))
                    dve.wait_ge(o_ev, b * N_UNITS + N_UNITS + 2)
                    for h in range(4):
                        o = o_tok[:, 256 + 128 * h:384 + 128 * h]
                        ins = dve.scalar_tensor_tensor(out=o, in0=o, scalar=rr4[:, h:h + 1],
                                                       in1=small[:, O_SUBG:O_SUBG + 128], op0=ALU.mult, op1=ALU.mult)
                    ins.then_inc(o_norm, 1)

                block_of_queries(0, "first")
                with dve.Fori(0, trips - 1) as turn:
                    chain.enter(turn, steps + 1)
                    block_of_queries(turn, "middle")
                chain.leave(trips - 1)
                block_of_queries(trips - 1, "last")

            def merge_block(L, j, finish):
                lo = NC_ if L == DEPTH - 1 else 0
                for br in range(3):
                    dve.wait_ge(prod_mm, finish + br)
                    dve.tensor_tensor(gate[:, br, lo:NT], gate[:, br, lo:NT], PS[br][:, 0:NT - lo], ALU.mult
                                      ).then_inc(br_ev[L], 1)
                dve.wait_ge(br_ev[L], 3 * j + 6)
                done(dve.tensor_tensor(gate[:, 0, lo:NT], gate[:, 0, lo:NT], gate[:, 1, lo:NT], ALU.add))
                dst = y_fm[:, bass.ds(j, 1), lo:NT]
                dve.tensor_tensor(dst, gate[:, 0:1, lo:NT], gate[:, 2:3, lo:NT], ALU.add).then_inc(y_done[L], 1)

            dve.sem_inc(o_ev, 2)
            dve.sem_inc(cb_ev, 4)
            dve.sem_inc(cbc_ev, 2)
            dve.sem_inc(dc_ev, 1)
            dve.memset(ones[:, :], 1.0)
            dve.memset(q_pad[:, :, :], 0.0)
            dve.memset(zero_col, 0.0)
            dve.memset(eps_col, EPS).then_inc(consts_set, 1)
            dve.wait_ge(consts_in, 16)
            for L in range(DEPTH):
                last = L == DEPTH - 1
                ctx_too = not last
                nb0 = 2 if last else 0
                lo = NC_ if last else 0
                if L:
                    x_final(dve, L - 1)
                dve.memset(c_pad, 0.0).then_inc(c_zeroed[L], 1)

                for k in range(1, KD):
                    add_square(2 * L, k, 0)
                norm(2 * L, False)
                lambdas(L)
                dve.wait_ge(rope_in_s[L], 16)
                for n, j in enumerate(ROPE_BLOCKS):
                    dve.wait_ge(qk_ev[L], j + 1)
                    if n:
                        dve.wait_ge(rope_done[L], n)
                    v = qk[:, j, NC_:NT]
                    done(dve.stream_shuffle(rot, v, [(c + 16) % 32 for c in range(32)]))
                    dve.tensor_tensor(v, v, rope[:, 0, :], ALU.mult)
                    done(dve.tensor_tensor(rot, rot, rope[:, 1, :], ALU.mult))
                    dve.tensor_tensor(v, v, rot, ALU.add).then_inc(rope_done[L], 1)
                def values_out(half):
                    for nb in range(NT // 128):
                        dve.wait_ge(prod_mm, units(L, V_UNIT0 + 4 * half + 3) + nb + 1)
                        bank = (6 * half + nb) % 8
                        dve.tensor_copy(v_tok[:, nb, V_HALF * half:V_HALF * half + V_HALF],
                                        PS[bank // 2][:, 512 * (bank % 2):512 * (bank % 2) + V_HALF]).then_inc(v_ev[L], 1)

                def whole(k):
                    dve.tensor_tensor(h_fm[:, k, :], h_low[:, k, :], h_up[:, k, :], ALU.add).then_inc(h_whole, 1)

                dve.wait_ge(rpb_out[L], 16)
                values_out(0)
                for n in range(3):
                    dve.wait_ge(prod_mm, units(L, V_UNIT0 + 4 + n + 1))
                    whole(2 * n)
                    whole(2 * n + 1)
                values_out(1)
                whole(KD - 2)
                whole(KD - 1)
                dve.wait_ge(bias_in[L], 16 * 10)
                table = bias[:, 0:4, :].rearrange("p h (r c) -> p (h r) c", c=GRID_W)
                done(dve.scalar_tensor_tensor(out=table, in0=table, scalar=1.0 / SCALE,
                                              in1=col_mask.unsqueeze(1).broadcast_to((128, 56, GRID_W)),
                                              op0=ALU.mult, op1=ALU.add))
                if ctx_too:
                    heads((L, "c"), NC_ // 128, NC_)
                heads((L, "l"), NL // 128, NT)
                dve.sem_inc(br_ev[L], 3)
                dve.sem_inc(y_done[L], 1)
                for k in range(KD):
                    lower(4 * L + 1, h_lo_r, h_fm, h_hi, k, lo)
                for k in range(KD):
                    lower(4 * L + 2, o_lo_r, o_fm, o_hi, k, lo)
                with dve.Fori(0, 2) as i:
                    chain.enter(i, 3)
                    for j in range(3):
                        merge_block(L, 3 * i + j, products(L, 6 * j + 4) + i * 18)
                chain.leave(2)
                merge_block(L, 6, products(L, 6 * 6 + 4))
                for k in range(KD - 1):
                    lower(4 * L + 3, h_lo_r, y_fm, h_hi, k, lo)
                merge_block(L, 7, products(L, 6 * 7 + 4))
                lower(4 * L + 3, h_lo_r, y_fm, h_hi, KD - 1, lo)
                dve.wait_ge(x_back[L], 16)
                for j in range(KD):
                    dve.wait_ge(prod_mm, products(L, 6 * KD + j + 1))
                    for v, a, b, c in segments(last):
                        ins = dve.scalar_tensor_tensor(out=x_fm[:, j, a:b], in0=PS[j % 4][:, c:c + b - a],
                                                       scalar=mod[:, 16 + j, v:v + 1], in1=x_fm[:, j, a:b],
                                                       op0=ALU.mult, op1=ALU.add)
                    ins.then_inc(out_ev[L], 1)
                    if j >= 2:
                        add_square(2 * L + 1, j - 1, lo)
                add_square(2 * L + 1, KD - 1, lo)
                norm(2 * L + 1, last)
                dve.wait_ge(lt_mm[L], 1)
                nb_n = 6 - nb0
                logits = PS[1][:, 0:96].rearrange("p (n e) -> p n e", e=NE)[:, nb0:6, :]
                done(dve.tensor_reduce(red_t[:, 0, nb0:6], logits, AX, ALU.max))
                dve.tensor_tensor(ex_t[:, nb0:6, :], logits, red_t[:, 0, nb0:6].unsqueeze(2).broadcast_to((128, nb_n, NE)),
                                  ALU.subtract).then_inc(ex_in[L], 1)
                dve.wait_ge(ex_out[L], 1)
                done(dve.tensor_reduce(red_t[:, 1, nb0:6], ex_t[:, nb0:6, :], AX, ALU.add))
                done(dve.reciprocal(red_t[:, 0, nb0:6], red_t[:, 1, nb0:6]))
                dve.tensor_tensor(aff_t[:, nb0:6, :], ex_t[:, nb0:6, :],
                                  red_t[:, 0, nb0:6].unsqueeze(2).broadcast_to((128, nb_n, NE)), ALU.mult
                                  ).then_inc(aff_done[L], 1)
                done(dve.memset(zero_e[0:NE, :], 0.0))
                dve.wait_ge(at_mm[L], 1)
                dve.tensor_copy(aff_e[0:NE, lo:NT], PS[2][0:NE, lo:NT])
                done(dve.tensor_copy(work_e[0:NE, lo:NT], PS[2][0:NE, lo:NT]))
                for v, a, b, c in segments(last):
                    work = work_e[0:NE, a:b]
                    for _ in range((CAP_C if v else CAP_L) // 8):
                        done(dve.max(best[0:NE, :], work))
                        done(dve.match_replace(work, best[0:NE, :], work, -1.0))
                done(dve.tensor_tensor(mask_e[0:NE, lo:NT], work_e[0:NE, lo:NT], aff_e[0:NE, lo:NT], ALU.not_equal))
                for v, a, b, c in segments(last):
                    done(dve.tensor_tensor_scan(pos_e[0:NE, a:b], mask_e[0:NE, a:b], zero_e[0:NE, a:b], 0.0,
                                                ALU.add, ALU.add))
                dve.tensor_tensor(pos_e[0:NE, lo:NT], pos_e[0:NE, lo:NT], mask_e[0:NE, lo:NT], ALU.mult
                                  ).then_inc(pos_done[L], 1)
                dve.wait_ge(pos_tr[L], 1)
                done(dve.memset(pos_t, 0.0))
                dve.tensor_copy(pos_t[:, nb0:6, 0:NE], PS[3][:, 0:96].rearrange("p (n e) -> p n e", e=NE)[:, nb0:6, :]
                                ).then_inc(router_done[L], 1)
                dve.wait_ge(router_done[L], 1)
                wide = NT if ctx_too else NL
                def pick(dst, pos, tokens, first, n_experts, cap):
                    shape = (128, tokens[1] - tokens[0], n_experts, cap)
                    at = pos[:, tokens[0]:tokens[1], bass.ds(first, n_experts)].unsqueeze(3).broadcast_to(shape)
                    slot = iota[:, 0:cap].unsqueeze(1).unsqueeze(1).broadcast_to(shape)
                    return dve.tensor_tensor(dst.rearrange("p n (e s) -> p n e s", s=cap), at, slot, ALU.is_equal)

                def weigh(dst, tokens, first, n_experts, cap):
                    shape = (128, tokens[1] - tokens[0], n_experts, cap)
                    aff = aff_t[:, tokens[0]:tokens[1], bass.ds(first, n_experts)].unsqueeze(3).broadcast_to(shape)
                    d4 = dst.rearrange("p n (e s) -> p n e s", s=cap)
                    return dve.tensor_tensor(d4, d4, aff, ALU.mult)

                def combined(p):
                    n = L * ROUNDS + p
                    for k in range(KD):
                        dve.wait_ge(cb_mm, n * KD + k + 1)
                        bank = PS[2 + (k % 4) // 2][:, 512 * (k % 2):512 * (k % 2) + 512]
                        dve.scalar_tensor_tensor(out=x_fm[:, k, NC_:NT], in0=bank, scalar=mod[:, 40 + k, 0:1],
                                                 in1=x_fm[:, k, NC_:NT], op0=ALU.mult, op1=ALU.add
                                                 ).then_inc(cb_ev, 1)

                def combined_context(p):
                    for c in range(4):
                        dve.wait_ge(cbc_mm, p * 4 + c + 1)
                        for k in (2 * c, 2 * c + 1):
                            at = 512 * (c % 2) + 256 * (k % 2)
                            ins = dve.scalar_tensor_tensor(out=x_fm[:, k, 0:NC_], in0=PS[3][:, at:at + 256],
                                                           scalar=mod[:, 40 + k, 1:2], in1=x_fm[:, k, 0:NC_],
                                                           op0=ALU.mult, op1=ALU.add)
                        ins.then_inc(cbc_ev, 1)

                pick(sel, pos_t, (2, 6), 0, 2, CAP_L).then_inc(sel_done, 1)
                if ctx_too:
                    pick(selc, pos_t, (0, 2), 0, 4, CAP_C).then_inc(selc_done, 1)
                dve.memset(y_pair, 0.0)
                dve.memset(y_ctx, 0.0)
                dve.memset(selw_t, 0.0)
                dve.memset(selcw_t, 0.0).then_inc(y_zeroed[L], 1)
                with dve.Fori(0, NE // 4) as turn:
                    i = turn + L * (NE // 4)
                    chain.enter(turn, 3 if ctx_too else 2)
                    for pair in range(2):
                        pr = i * 2 + pair
                        p = turn * 2 + pair
                        dve.wait_ge(st_mm, pr + 1)
                        if ctx_too and pair == 0:
                            done(pick(selcw, pos_t, (0, 2), turn * 4, 4, CAP_C))
                            weigh(selcw, (0, 2), turn * 4, 4, CAP_C)
                        done(pick(selw, pos_t, (2, 6), turn * 4 + 2 * pair, 2, CAP_L))
                        weigh(selw, (2, 6), turn * 4 + 2 * pair, 2, CAP_L).then_inc(selw_done, 1)
                        dve.wait_ge(gat_mm, L * ROUNDS + p + 1)
                        pick(sel, pos_t, (2, 6), turn * 4 + 2 * pair + 2, 2, CAP_L).then_inc(sel_done, 1)
                        if ctx_too and pair == 0:
                            dve.wait_ge(gatc_mm, turn + 1)
                            pick(selc, pos_t, (0, 2), turn * 4 + 4, 4, CAP_C).then_inc(selc_done, 1)
                        base = finished(L, MOE0 + 24 * pair)
                        for par in range(2):
                            dve.wait_ge(g_ev, pr * 2 + par + 1)
                            dve.wait_ge(slot_done, turn * 48 + base + 8 * par + 8)
                            dve.tensor_tensor(hid[:, par, 0:wide], silu[:, par, 0:wide], PS[1][:, 0:wide], ALU.mult
                                              ).then_inc(hid_done, 1)
                            if par == 0:
                                combined(p)
                                if ctx_too and pair == 0:
                                    combined_context(turn)
                        dve.wait_ge(st_mm, pr + 2)
                        if ctx_too and pair == 0:
                            dve.tensor_copy(selcw_t, PS[3][:, 512:768])
                        dve.tensor_copy(selw_t, PS[3][:, 0:512]).then_inc(st_ev, 1)
                        if ctx_too:
                            for par in range(2):
                                q = 2 * pair + par
                                dve.wait_ge(slot_done, turn * 48 + base + 16 + 4 * par + 4)
                                for g in range(4):
                                    ins = dve.tensor_copy(y_ctx[32 * q:32 * q + 32, 256 * g:256 * g + 256],
                                                          PS[0 if par else 2][32 * g:32 * g + 32, 512:768])
                                ins.then_inc(dc_ev, 1)
                chain.leave(NE // 4)
                combined(NE // 2)
                if ctx_too:
                    combined_context(NE // 4)
            x_final(dve, DEPTH - 1)
            for k in range(1, KD):
                add_square(NORMS - 1, k, NC_)
            norm(NORMS - 1, True)


def shape_tables():
    f = np.float32
    t = np.arange(NL)
    row, col = (t // GRID_W).astype(f), (t % GRID_W).astype(f)
    inv = (f(10000.0) ** (-np.arange(16, dtype=f) / f(16))).astype(f)
    ang = np.concatenate([np.outer(inv, row)] * 2 + [np.outer(inv, col)] * 2).astype(f)
    sign = np.where(np.arange(64) % 32 < 16, f(-1), f(1))[:, None]
    rope = np.stack([np.tile(np.cos(ang), (2, 1)), np.tile(np.sin(ang) * sign, (2, 1))], axis=1).astype(f)
    p = np.arange(128)[:, None]
    swa = np.where(np.abs(np.arange(896)[None, :] - 384 - p) <= 128, f(0), f(NEG))
    start = np.clip(p % GRID_W - 8, 0, GRID_W - 16)
    k = np.arange(GRID_W)[None, :]
    cols = np.where((k >= start) & (k < start + 16), f(0), f(NEG))
    return rope, np.concatenate([swa, cols], axis=1).astype(f)


def feature_blocks(w):
    k = w.shape[0] // 128
    return w.reshape(k, 128, -1, 128).transpose(2, 1, 0, 3).reshape(-1, 128, k * 128)


def layer_stream(l, a):
    w_in = a["w_in"][l]
    slots = []
    mod = a["w_mod"][l].reshape(KD, 128, 3, SLOT)
    slots += [mod[k, :, r, :] for r in range(3) for k in range(KD)]
    swa_order = [768 + 64 * h + c for h in (0, 2, 1, 3) for c in range(64)]
    q = np.concatenate([w_in[:, 0:768], w_in[:, swa_order]], axis=1)
    qk = feature_blocks(np.concatenate([q, w_in[:, 1024:1920]], axis=1))
    qk = np.concatenate([qk, np.zeros((1, 128, 1024), qk.dtype)])
    slots += [np.concatenate([qk[2 * s], qk[2 * s + 1]], axis=1) for s in range(QK_SLOTS)]
    v = w_in[:, 1920:2816].reshape(4, 2, 128, 2, V_HALF).transpose(3, 0, 2, 1, 4).reshape(8, 128, 2 * V_HALF)
    v = np.concatenate([v, np.zeros((8, 128, 1024 - 2 * V_HALF), v.dtype)], axis=2)
    slots += [np.concatenate([v[2 * s], v[2 * s + 1]], axis=1) for s in range(V_SLOTS)]
    gates = feature_blocks(w_in[:, 2816:])
    branch = feature_blocks(np.concatenate([a["w_branch_na"][l], a["w_branch_diff"][l], a["w_branch_swa"][l]]))
    for j in range(KD):
        slots.append(np.concatenate([gates[j], gates[8 + j]], axis=1))
        slots.append(np.concatenate([gates[16 + j], branch[j]], axis=1))
    wo = feature_blocks(a["w_out"][l])
    slots += [np.concatenate([wo[2 * s], wo[2 * s + 1]], axis=1) for s in range(OUT_SLOTS)]
    gate, up, down = (a[n][l].reshape(NE, 4, 2, 128, D).transpose(0, 1, 3, 2, 4).reshape(NE, 4, 128, SLOT)
                      for n in ("w_expert_gate", "w_expert_up", "w_expert_down"))
    for e in range(0, NE, 2):
        for w, n in ((gate, e), (up, e), (gate, e + 1), (up, e + 1), (down, e), (down, e + 1)):
            slots += list(w[n])
    return slots


def columns(v):
    return v.reshape(-1, 128).T


def kernel(**inputs):
    import concourse.bacc as bacc
    from concourse.bass_utils import run_bass_kernel_spmd as run

    a = {k: np.asarray(v) for k, v in inputs.items()}
    f = a["x"].dtype
    stream = np.stack([s for l in range(DEPTH) for s in layer_stream(l, a)])
    assert stream.shape[0] == TOTAL_SLOTS, stream.shape
    tokens = np.concatenate([a["ctx"][0], a["x"][0]])
    x_fm = tokens.T.reshape(KD, 128, NT).transpose(1, 0, 2)

    def rep(v):
        return np.broadcast_to(v.reshape(1, -1), (128, v.size))

    small = np.stack([np.concatenate([
        columns(a["b_mod"][l]), columns(a["norm1_g"][l]), columns(a["norm2_g"][l]), rep(a["diff_subln_g"][l]),
        rep(a["diff_lambda"][l]), rep(a["swa_sink"][l]),
        a["w_router"][l].reshape(KD, 128, NE).transpose(1, 0, 2).reshape(128, KD * NE)], axis=1) for l in range(DEPTH)])
    c2 = np.stack([columns(a["c"][0]), columns(a["c_ctx"])], axis=2).reshape(128, 16)
    glob = np.concatenate([c2, columns(a["final_g"]), np.eye(128, dtype=f), rep(np.arange(1, 65, dtype=f))], axis=1)
    rope, mask = shape_tables()
    arrays = {"stream": stream, "x_in": x_fm, "small_in": small, "global_in": glob, "rope_in": rope,
              "mask_in": mask, "rpb_in": a["na_rpb"].reshape(DEPTH, 60, 31)}
    arrays = {k: np.ascontiguousarray(v) for k, v in arrays.items()}
    nc = bacc.Bacc("TRN2", target_bir_lowering=False, num_devices=1)
    args = [nc.dram_tensor(k, v.shape, mybir.dt.from_np(v.dtype), kind="ExternalInput").ap()
            for k, v in arrays.items()]
    out = nc.dram_tensor("out_fm", (128, KD, NL), mybir.dt.float32, kind="ExternalOutput").ap()
    build(nc, *args, out)
    r = run(nc, [arrays], core_ids=[0])
    y = r.results[0]["out_fm"]
    return np.ascontiguousarray(y.transpose(2, 1, 0).reshape(1, NL, D))
```
